# Optimizing a Trainium2 kernel written in Bass

```python
import math
import jax, jax.numpy as jnp
from jax import lax
import numpy as np

D_MODEL = 1024
BATCH = 1
SEQ = 256
DEPTH = 2

N_MIXERS = 2
RMS_EPS = 1e-6
FFN_HIDDEN = 2816
Q_BLOCK = 128
NEG = -1e30
MLA_HEADS = 16
MLA_Q_LORA = 384
MLA_KV_LORA = 256
MLA_NOPE = 64
MLA_ROPE = 32
MLA_V = 64
ROPE_THETA = 10000.0
NSA_HEADS = 16
NSA_GROUPS = 4
NSA_QK = 64
NSA_V = 64
CMP_BLOCK = 32
CMP_STRIDE = 16
CMP_HIDDEN = 128
SEL_BLOCK = 64
SEL_TOP_N = 16
WINDOW = 512
SEL_Q_CHUNK = 16
REL_BUCKETS = 32
REL_MAX_DIST = 128


def rmsnorm(x, g):
    x32 = x.astype(jnp.float32)
    y = x32 * lax.rsqrt(jnp.mean(x32 * x32, axis=-1, keepdims=True) + RMS_EPS)
    return y.astype(x.dtype) * g

def swiglu(x, w_gate, w_up, w_down):
    return (jax.nn.silu(x @ w_gate) * (x @ w_up)) @ w_down

def rope_angles(S):
    half = MLA_ROPE // 2
    inv = ROPE_THETA ** (-jnp.arange(half, dtype=jnp.float32) * 2.0 / MLA_ROPE)
    ang = jnp.arange(S, dtype=jnp.float32)[:, None] * inv[None, :]
    return jnp.cos(ang), jnp.sin(ang)

def apply_rotary(x, cos, sin):
    half = x.shape[-1] // 2
    cos = cos.astype(x.dtype)
    sin = sin.astype(x.dtype)
    x1, x2 = x[..., :half], x[..., half:]
    return jnp.concatenate([x1 * cos - x2 * sin, x1 * sin + x2 * cos], axis=-1)

def t5_bucket(dist):
    n = jnp.maximum(dist, 0)
    max_exact = REL_BUCKETS // 2
    nf = jnp.maximum(n, 1).astype(jnp.float32)
    large = max_exact + (jnp.log(nf / max_exact) / math.log(REL_MAX_DIST / max_exact)
                         * (REL_BUCKETS - max_exact)).astype(jnp.int32)
    large = jnp.minimum(large, REL_BUCKETS - 1)
    return jnp.where(n < max_exact, n, large)

def mla_mixer(h, w_in, q_norm, kv_norm, w_uq, w_ukv, w_o):
    B, S, _ = h.shape
    H = MLA_HEADS
    proj = h @ w_in
    c_q = proj[..., :MLA_Q_LORA]
    c_kv = proj[..., MLA_Q_LORA:MLA_Q_LORA + MLA_KV_LORA]
    k_rope = proj[..., MLA_Q_LORA + MLA_KV_LORA:]
    q = (rmsnorm(c_q, q_norm) @ w_uq).reshape(B, S, H, MLA_NOPE + MLA_ROPE)
    kv = (rmsnorm(c_kv, kv_norm) @ w_ukv).reshape(B, S, H, MLA_NOPE + MLA_V)
    cos, sin = rope_angles(S)
    q_nope = q[..., :MLA_NOPE]
    q_rope = apply_rotary(q[..., MLA_NOPE:], cos[:, None, :], sin[:, None, :])
    k_rope = apply_rotary(k_rope, cos, sin)
    k_nope = kv[..., :MLA_NOPE]
    v = kv[..., MLA_NOPE:]
    scale = (MLA_NOPE + MLA_ROPE) ** -0.5
    n_blk = S // Q_BLOCK
    qn_b = q_nope.reshape(B, n_blk, Q_BLOCK, H, MLA_NOPE).swapaxes(0, 1)
    qr_b = q_rope.reshape(B, n_blk, Q_BLOCK, H, MLA_ROPE).swapaxes(0, 1)
    starts = jnp.arange(n_blk) * Q_BLOCK
    kpos = jnp.arange(S)

    def block(args):
        qn, qr, s0 = args
        s = (jnp.einsum('bqhd,bkhd->bhqk', qn, k_nope)
             + jnp.einsum('bqhd,bkd->bhqk', qr, k_rope)).astype(jnp.float32) * scale
        qpos = s0 + jnp.arange(Q_BLOCK)
        p = jax.nn.softmax(jnp.where(kpos[None, :] <= qpos[:, None], s, NEG), axis=-1)
        return jnp.einsum('bhqk,bkhd->bqhd', p.astype(v.dtype), v)

    o = lax.map(block, (qn_b, qr_b, starts)).swapaxes(0, 1).reshape(B, S, H * MLA_V)
    return o @ w_o

def compress_blocks(x, blk_idx, pos_emb, w1, w2):
    B = x.shape[0]
    n_cmp, L = blk_idx.shape
    blocks = x[:, blk_idx] + pos_emb[None, None, :, None, :]
    flat = jnp.moveaxis(blocks, 3, 2).reshape(B, n_cmp, x.shape[2], L * x.shape[3])
    return jax.nn.gelu(flat @ w1) @ w2

def selection_overlap(n_cmp, n_sel):
    cs = np.arange(n_cmp) * CMP_STRIDE
    ce = cs + CMP_BLOCK
    ss = np.arange(n_sel) * SEL_BLOCK
    se = ss + SEL_BLOCK
    ov = np.minimum(ce[:, None], se[None, :]) - np.maximum(cs[:, None], ss[None, :])
    return (np.clip(ov, 0, None) / CMP_BLOCK).astype(np.float32)

def selected_attention(q, k, v, sel_idx, tbl, scale):
    B, S, G, R, dk = q.shape
    dv = v.shape[-1]
    n_sel = S // SEL_BLOCK
    n_top = sel_idx.shape[-1]
    kb = k.reshape(B, n_sel, SEL_BLOCK, G, dk).transpose(0, 3, 1, 2, 4)
    vb = v.reshape(B, n_sel, SEL_BLOCK, G, dv).transpose(0, 3, 1, 2, 4)
    C = SEL_Q_CHUNK
    n_ch = S // C
    q_ch = q.reshape(B, n_ch, C, G, R, dk).swapaxes(0, 1)
    idx_ch = sel_idx.reshape(B, G, n_ch, C, n_top).transpose(2, 0, 1, 3, 4)
    starts = jnp.arange(n_ch) * C
    gather = jax.vmap(jax.vmap(lambda blocks, ix: blocks[ix]))
    g_ar = jnp.arange(G)[None, :, None, None]
    K = n_top * SEL_BLOCK

    def chunk(args):
        q_i, ix, s0 = args
        kg = gather(kb, ix).reshape(B, G, C, K, dk)
        vg = gather(vb, ix).reshape(B, G, C, K, dv)
        kpos = (ix[..., None] * SEL_BLOCK + jnp.arange(SEL_BLOCK)).reshape(B, G, C, K)
        qpos = s0 + jnp.arange(C)
        dist = qpos[None, None, :, None] - kpos
        bias = tbl[t5_bucket(dist), g_ar]
        s = jnp.einsum('bcgrd,bgckd->bgcrk', q_i, kg).astype(jnp.float32) * scale \
            + jnp.moveaxis(bias, -1, 3).astype(jnp.float32)
        p = jax.nn.softmax(jnp.where((dist >= 0)[:, :, :, None, :], s, NEG), axis=-1)
        return jnp.einsum('bgcrk,bgckd->bcgrd', p.astype(vg.dtype), vg)

    out = lax.map(chunk, (q_ch, idx_ch, starts))
    return out.swapaxes(0, 1).reshape(B, S, G, R, dv)

def window_attention(q, k, v, tbl, scale):
    B, S, G, R, dk = q.shape
    n_blk = S // Q_BLOCK
    span = WINDOW + Q_BLOCK
    k_pad = jnp.pad(k, ((0, 0), (WINDOW, 0), (0, 0), (0, 0)))
    v_pad = jnp.pad(v, ((0, 0), (WINDOW, 0), (0, 0), (0, 0)))
    q_b = q.reshape(B, n_blk, Q_BLOCK, G, R, dk).swapaxes(0, 1)
    starts = jnp.arange(n_blk) * Q_BLOCK

    def block(args):
        q_i, s0 = args
        k_i = lax.dynamic_slice_in_dim(k_pad, s0, span, axis=1)
        v_i = lax.dynamic_slice_in_dim(v_pad, s0, span, axis=1)
        qpos = s0 + jnp.arange(Q_BLOCK)
        kpos = s0 - WINDOW + jnp.arange(span)
        dist = qpos[:, None] - kpos[None, :]
        mask = (dist >= 0) & (dist < WINDOW) & (kpos >= 0)[None, :]
        bias = tbl[t5_bucket(dist)].transpose(2, 3, 0, 1)
        s = jnp.einsum('bqgrd,bkgd->bgrqk', q_i, k_i).astype(jnp.float32) * scale + bias.astype(jnp.float32)
        p = jax.nn.softmax(jnp.where(mask, s, NEG), axis=-1)
        return jnp.einsum('bgrqk,bkgd->bqgrd', p.astype(v_i.dtype), v_i)

    out = lax.map(block, (q_b, starts))
    return out.swapaxes(0, 1).reshape(B, S, G, R, v.shape[-1])

def nsa_mixer(h, rel_bias, w_in, pos_k, w1_k, w2_k, pos_v, w1_v, w2_v, w_o):
    B, S, _ = h.shape
    H, G = NSA_HEADS, NSA_GROUPS
    R = H // G
    sizes = [H * NSA_QK, G * NSA_QK, G * NSA_V, G * NSA_QK, G * NSA_V, G * NSA_QK, G * NSA_V, H * 3]
    cuts = [int(c) for c in np.cumsum(sizes[:-1])]
    q, k_c, v_c, k_s, v_s, k_w, v_w, g = jnp.split(h @ w_in, cuts, axis=-1)
    q = q.reshape(B, S, G, R, NSA_QK)
    k_c, k_s, k_w = (t.reshape(B, S, G, NSA_QK) for t in (k_c, k_s, k_w))
    v_c, v_s, v_w = (t.reshape(B, S, G, NSA_V) for t in (v_c, v_s, v_w))
    gates = jax.nn.sigmoid(g.astype(jnp.float32)).astype(h.dtype).reshape(B, S, G, R, 3)
    tbl = rel_bias.reshape(REL_BUCKETS, G, R)
    scale = NSA_QK ** -0.5
    pos = jnp.arange(S)

    n_cmp = (S - CMP_BLOCK) // CMP_STRIDE + 1
    blk_idx = jnp.arange(n_cmp)[:, None] * CMP_STRIDE + jnp.arange(CMP_BLOCK)[None, :]
    kc = compress_blocks(k_c, blk_idx, pos_k, w1_k, w2_k)
    vc = compress_blocks(v_c, blk_idx, pos_v, w1_v, w2_v)
    cmp_end = jnp.arange(n_cmp) * CMP_STRIDE + CMP_BLOCK - 1
    dist = pos[:, None] - cmp_end[None, :]
    valid = dist >= 0
    bias = tbl[t5_bucket(dist)].transpose(2, 3, 0, 1)
    s = jnp.einsum('bsgrd,bngd->bgrsn', q, kc).astype(jnp.float32) * scale + bias.astype(jnp.float32)
    p_cmp = jax.nn.softmax(jnp.where(valid, s, NEG), axis=-1) * valid
    o_cmp = jnp.einsum('bgrsn,bngd->bsgrd', p_cmp.astype(vc.dtype), vc)

    n_sel = S // SEL_BLOCK
    overlap = jnp.asarray(selection_overlap(n_cmp, n_sel))
    imp = jnp.einsum('bgrsn,nj->bgsj', p_cmp, overlap)
    blk_t = (pos // SEL_BLOCK)[:, None]
    j = jnp.arange(n_sel)[None, :]
    forced = (j == 0) | (j == blk_t) | (j == blk_t - 1)
    score = jnp.where(forced, 1e6, jnp.where(j <= blk_t, imp, -1e6))
    n_top = min(SEL_TOP_N, n_sel)
    _, sel_idx = lax.top_k(score, n_top)
    o_sel = selected_attention(q, k_s, v_s, sel_idx, tbl, scale)

    o_win = window_attention(q, k_w, v_w, tbl, scale)

    o = gates[..., 0:1] * o_cmp + gates[..., 1:2] * o_sel + gates[..., 2:3] * o_win
    return o.reshape(B, S, H * NSA_V) @ w_o

def first_inputs(seed: int = 0) -> dict:
    key = jax.random.key(seed)
    ks = iter(jax.random.split(key, 32))
    n_mla = len(range(0, DEPTH, N_MIXERS))
    n_nsa = DEPTH - n_mla

    def dense(shape, fan_in):
        return jax.random.normal(next(ks), shape, jnp.float32) * fan_in ** -0.5

    def gain(shape):
        return 1.0 + 0.01 * jax.random.normal(next(ks), shape, jnp.float32)

    def small(shape, s):
        return s * jax.random.normal(next(ks), shape, jnp.float32)

    mla_in = MLA_Q_LORA + MLA_KV_LORA + MLA_ROPE
    nsa_in = NSA_HEADS * NSA_QK + 3 * NSA_GROUPS * (NSA_QK + NSA_V) + 3 * NSA_HEADS
    return {
        "x": jax.random.normal(next(ks), (BATCH, SEQ, D_MODEL), jnp.float32),
        "ffn_norm_a": gain((DEPTH, D_MODEL)),
        "ffn_a_w_gate": dense((DEPTH, D_MODEL, FFN_HIDDEN), D_MODEL),
        "ffn_a_w_up": dense((DEPTH, D_MODEL, FFN_HIDDEN), D_MODEL),
        "ffn_a_w_down": dense((DEPTH, FFN_HIDDEN, D_MODEL), FFN_HIDDEN),
        "mix_norm": gain((DEPTH, D_MODEL)),
        "ffn_norm_b": gain((DEPTH, D_MODEL)),
        "ffn_b_w_gate": dense((DEPTH, D_MODEL, FFN_HIDDEN), D_MODEL),
        "ffn_b_w_up": dense((DEPTH, D_MODEL, FFN_HIDDEN), D_MODEL),
        "ffn_b_w_down": dense((DEPTH, FFN_HIDDEN, D_MODEL), FFN_HIDDEN),
        "final_norm": gain((D_MODEL,)),
        "rel_bias": small((REL_BUCKETS, NSA_HEADS), 0.5),
        "mla_w_in": dense((n_mla, D_MODEL, mla_in), D_MODEL),
        "mla_q_norm": gain((n_mla, MLA_Q_LORA)),
        "mla_kv_norm": gain((n_mla, MLA_KV_LORA)),
        "mla_w_uq": dense((n_mla, MLA_Q_LORA, MLA_HEADS * (MLA_NOPE + MLA_ROPE)), MLA_Q_LORA),
        "mla_w_ukv": dense((n_mla, MLA_KV_LORA, MLA_HEADS * (MLA_NOPE + MLA_V)), MLA_KV_LORA),
        "mla_w_o": dense((n_mla, MLA_HEADS * MLA_V, D_MODEL), MLA_HEADS * MLA_V),
        "nsa_w_in": dense((n_nsa, D_MODEL, nsa_in), D_MODEL),
        "nsa_cmp_pos_k": small((n_nsa, CMP_BLOCK, NSA_QK), 0.1),
        "nsa_cmp_w1_k": dense((n_nsa, CMP_BLOCK * NSA_QK, CMP_HIDDEN), CMP_BLOCK * NSA_QK),
        "nsa_cmp_w2_k": dense((n_nsa, CMP_HIDDEN, NSA_QK), CMP_HIDDEN),
        "nsa_cmp_pos_v": small((n_nsa, CMP_BLOCK, NSA_V), 0.1),
        "nsa_cmp_w1_v": dense((n_nsa, CMP_BLOCK * NSA_V, CMP_HIDDEN), CMP_BLOCK * NSA_V),
        "nsa_cmp_w2_v": dense((n_nsa, CMP_HIDDEN, NSA_V), CMP_HIDDEN),
        "nsa_w_o": dense((n_nsa, NSA_HEADS * NSA_V, D_MODEL), NSA_HEADS * NSA_V),
    }

def first_block(x, ffn_norm_a, ffn_a_w_gate, ffn_a_w_up, ffn_a_w_down, mix_norm, ffn_norm_b,
              ffn_b_w_gate, ffn_b_w_up, ffn_b_w_down, final_norm, rel_bias,
              mla_w_in, mla_q_norm, mla_kv_norm, mla_w_uq, mla_w_ukv, mla_w_o,
              nsa_w_in, nsa_cmp_pos_k, nsa_cmp_w1_k, nsa_cmp_w2_k,
              nsa_cmp_pos_v, nsa_cmp_w1_v, nsa_cmp_w2_v, nsa_w_o):
    h = x
    for i in range(DEPTH):
        h = h + 0.5 * swiglu(rmsnorm(h, ffn_norm_a[i]), ffn_a_w_gate[i], ffn_a_w_up[i], ffn_a_w_down[i])
        m = rmsnorm(h, mix_norm[i])
        j = i // N_MIXERS
        if i % N_MIXERS == 0:
            h = h + mla_mixer(m, mla_w_in[j], mla_q_norm[j], mla_kv_norm[j],
                              mla_w_uq[j], mla_w_ukv[j], mla_w_o[j])
        else:
            h = h + nsa_mixer(m, rel_bias, nsa_w_in[j], nsa_cmp_pos_k[j], nsa_cmp_w1_k[j], nsa_cmp_w2_k[j],
                              nsa_cmp_pos_v[j], nsa_cmp_w1_v[j], nsa_cmp_w2_v[j], nsa_w_o[j])
        h = h + 0.5 * swiglu(rmsnorm(h, ffn_norm_b[i]), ffn_b_w_gate[i], ffn_b_w_up[i], ffn_b_w_down[i])
    return rmsnorm(h, final_norm)


DEPTH_2 = 1

MEM_LEN = 256
DA_HEADS = 8
DA_HEAD_DIM = 64
DA_QK = DA_HEADS * 2 * DA_HEAD_DIM
DA_V = DA_HEADS * 2 * DA_HEAD_DIM
SSD_EXPAND = 2
SSD_INNER = SSD_EXPAND * D_MODEL
SSD_HEAD_DIM = 64
SSD_HEADS = SSD_INNER // SSD_HEAD_DIM
SSD_GROUPS = 4
SSD_HEADS_PER_GROUP = SSD_HEADS // SSD_GROUPS
SSD_STATE = 128
SSD_CONV = 4
SSD_CHUNK = 128
SSD_CONV_DIM = SSD_INNER + 2 * SSD_GROUPS * SSD_STATE
XA_HEADS = 4
XA_HEAD_DIM = D_MODEL // XA_HEADS
D_FF = 2816
N_BRANCH = 2
IN_SIZES = (DA_QK, DA_QK, DA_V, SSD_INNER, SSD_CONV_DIM, SSD_HEADS, N_BRANCH * D_MODEL)
IN_WIDTH = DA_QK + DA_QK + DA_V + SSD_INNER + SSD_CONV_DIM + SSD_HEADS + N_BRANCH * D_MODEL
NORM_EPS = 1e-6
SUBLN_EPS = 1e-5


def _rmsnorm(x, g, eps=NORM_EPS):
    xf = x.astype(jnp.float32)
    y = xf * lax.rsqrt(jnp.mean(xf * xf, axis=-1, keepdims=True) + eps)
    return (y * g.astype(jnp.float32)).astype(x.dtype)

def _swiglu(h, w_gu, w_down):
    g, u = jnp.split(h @ w_gu, 2, axis=-1)
    return (jax.nn.silu(g) * u) @ w_down

def _diff_attention(q, k, v, lam):
    b, s = q.shape[0], q.shape[1]
    q1, q2 = q[:, :, :, 0].transpose(0, 2, 1, 3), q[:, :, :, 1].transpose(0, 2, 1, 3)
    k1, k2 = k[:, :, :, 0].transpose(0, 2, 1, 3), k[:, :, :, 1].transpose(0, 2, 1, 3)
    vh = v.transpose(0, 2, 1, 3)
    nblk = s // Q_BLOCK
    scale = DA_HEAD_DIM ** -0.5
    key_pos = jnp.arange(s)

    def blocks(t):
        return t.reshape(b, DA_HEADS, nblk, Q_BLOCK, DA_HEAD_DIM).transpose(2, 0, 1, 3, 4)

    def one_block(args):
        q1b, q2b, start = args
        mask = (start + jnp.arange(Q_BLOCK))[:, None] >= key_pos[None, :]

        def probs(qb, kk):
            sc = jnp.einsum('bhqd,bhkd->bhqk', qb, kk).astype(jnp.float32) * scale
            return jax.nn.softmax(jnp.where(mask, sc, -jnp.inf), axis=-1)

        p = probs(q1b, k1) - lam * probs(q2b, k2)
        return jnp.einsum('bhqk,bhke->bhqe', p.astype(vh.dtype), vh)

    out = lax.map(one_block, (blocks(q1), blocks(q2), jnp.arange(nblk, dtype=jnp.int32) * Q_BLOCK))
    return out.transpose(1, 2, 0, 3, 4).reshape(b, DA_HEADS, s, 2 * DA_HEAD_DIM)

def _segsum(a):
    t = a.shape[-1]
    cs = jnp.cumsum(a, axis=-1)
    seg = cs[..., :, None] - cs[..., None, :]
    return jnp.where(jnp.tril(jnp.ones((t, t), dtype=bool)), seg, -jnp.inf)

def _ssd_chunked(xdt, adt, bm, cm):
    b, s = xdt.shape[0], xdt.shape[1]
    c = s // SSD_CHUNK
    G, R, P, N, Lc = SSD_GROUPS, SSD_HEADS_PER_GROUP, SSD_HEAD_DIM, SSD_STATE, SSD_CHUNK
    X = xdt.astype(jnp.float32).reshape(b, c, Lc, G, R, P)
    A = adt.astype(jnp.float32).reshape(b, c, Lc, G, R).transpose(0, 3, 4, 1, 2)
    Bc = bm.astype(jnp.float32).reshape(b, c, Lc, G, N)
    Cc = cm.astype(jnp.float32).reshape(b, c, Lc, G, N)
    a_cs = jnp.cumsum(A, axis=-1)
    Lmat = jnp.exp(_segsum(A))
    cb = jnp.einsum('bclgn,bcsgn->bgcls', Cc, Bc)
    y_diag = jnp.einsum('bgrcls,bcsgrp->bclgrp', cb[:, :, None] * Lmat, X)
    decay_states = jnp.exp(a_cs[..., -1:] - a_cs)
    states = jnp.einsum('bclgn,bgrcl,bclgrp->bcgrpn', Bc, decay_states, X)
    chunk_end = jnp.pad(a_cs[..., -1], ((0, 0), (0, 0), (0, 0), (1, 0)))
    decay_chunk = jnp.exp(_segsum(chunk_end))
    states = jnp.concatenate([jnp.zeros_like(states[:, :1]), states], axis=1)
    prev_states = jnp.einsum('bgrzc,bcgrpn->bzgrpn', decay_chunk, states)[:, :-1]
    y_off = jnp.einsum('bclgn,bcgrpn,bgrcl->bclgrp', Cc, prev_states, jnp.exp(a_cs))
    return (y_diag + y_off).reshape(b, s, SSD_HEADS, P)

def _depthwise_causal_conv(u, w, bias):
    y = lax.conv_general_dilated(u, w.astype(u.dtype)[:, None, :], window_strides=(1,),
                                 padding=[(SSD_CONV - 1, 0)],
                                 dimension_numbers=('NWC', 'WIO', 'NWC'),
                                 feature_group_count=u.shape[-1])
    return y + bias.astype(u.dtype)

def _layer(x, mem, layer_idx,
           ffn1_pre_g, ffn1_post_g, ffn1_w_gu, ffn1_w_down,
           mix_pre_g, mix_post_g, w_in, b_gate,
           da_lambda_q1, da_lambda_k1, da_lambda_q2, da_lambda_k2, da_subln_g,
           ssd_conv_w, ssd_conv_b, ssd_dt_bias, ssd_A_log, ssd_D, ssd_norm_g,
           w_branch_attn, w_branch_ssd, w_mix_out,
           xa_pre_g, xa_post_g, mem_norm_g, xa_w_q, xa_w_kv, xa_w_o,
           ffn2_pre_g, ffn2_post_g, ffn2_w_gu, ffn2_w_down):
    b, s, _ = x.shape
    x = x + 0.5 * _rmsnorm(_swiglu(_rmsnorm(x, ffn1_pre_g), ffn1_w_gu, ffn1_w_down), ffn1_post_g)

    h = _rmsnorm(x, mix_pre_g)
    cuts = [sum(IN_SIZES[:i + 1]) for i in range(len(IN_SIZES) - 1)]
    q, k, v, z, xbc, dt_raw, gate_logits = jnp.split(h @ w_in, cuts, axis=-1)

    lam_init = 0.8 - 0.6 * math.exp(-0.3 * layer_idx)
    lam = (jnp.exp(jnp.sum(da_lambda_q1 * da_lambda_k1).astype(jnp.float32))
           - jnp.exp(jnp.sum(da_lambda_q2 * da_lambda_k2).astype(jnp.float32)) + lam_init)
    o = _diff_attention(q.reshape(b, s, DA_HEADS, 2, DA_HEAD_DIM),
                        k.reshape(b, s, DA_HEADS, 2, DA_HEAD_DIM),
                        v.reshape(b, s, DA_HEADS, 2 * DA_HEAD_DIM), lam)
    o = _rmsnorm(o, da_subln_g, SUBLN_EPS) * (1.0 - lam_init)
    attn_out = o.transpose(0, 2, 1, 3).reshape(b, s, DA_V) @ w_branch_attn

    xbc = jax.nn.silu(_depthwise_causal_conv(xbc, ssd_conv_w, ssd_conv_b))
    xs, bm, cm = jnp.split(xbc, [SSD_INNER, SSD_INNER + SSD_GROUPS * SSD_STATE], axis=-1)
    dt = jax.nn.softplus(dt_raw.astype(jnp.float32) + ssd_dt_bias.astype(jnp.float32))
    a = -jnp.exp(ssd_A_log.astype(jnp.float32))
    xh = xs.reshape(b, s, SSD_HEADS, SSD_HEAD_DIM)
    y = _ssd_chunked(xh * dt[..., None], a * dt,
                     bm.reshape(b, s, SSD_GROUPS, SSD_STATE), cm.reshape(b, s, SSD_GROUPS, SSD_STATE))
    y = (y + ssd_D.astype(jnp.float32)[:, None] * xh).astype(x.dtype).reshape(b, s, SSD_INNER)
    yg = (y * jax.nn.silu(z)).reshape(b, s, SSD_GROUPS, SSD_INNER // SSD_GROUPS)
    y = _rmsnorm(yg, ssd_norm_g.reshape(SSD_GROUPS, SSD_INNER // SSD_GROUPS), SUBLN_EPS)
    ssd_out = y.reshape(b, s, SSD_INNER) @ w_branch_ssd

    g_attn, g_ssd = jnp.split(jax.nn.sigmoid(gate_logits + b_gate), N_BRANCH, axis=-1)
    mixed = (g_attn * attn_out + g_ssd * ssd_out) @ w_mix_out
    x = x + _rmsnorm(mixed, mix_post_g)

    hq = _rmsnorm(x, xa_pre_g)
    qx = (hq @ xa_w_q).reshape(b, s, XA_HEADS, XA_HEAD_DIM)
    kx, vx = jnp.split(_rmsnorm(mem, mem_norm_g) @ xa_w_kv, 2, axis=-1)
    m = mem.shape[1]
    kx = kx.reshape(b, m, XA_HEADS, XA_HEAD_DIM)
    vx = vx.reshape(b, m, XA_HEADS, XA_HEAD_DIM)
    sc = jnp.einsum('bqhd,bkhd->bhqk', qx, kx).astype(jnp.float32) * (XA_HEAD_DIM ** -0.5)
    p = jax.nn.softmax(sc, axis=-1).astype(vx.dtype)
    xo = jnp.einsum('bhqk,bkhd->bqhd', p, vx).reshape(b, s, D_MODEL) @ xa_w_o
    x = x + _rmsnorm(xo, xa_post_g)

    x = x + 0.5 * _rmsnorm(_swiglu(_rmsnorm(x, ffn2_pre_g), ffn2_w_gu, ffn2_w_down), ffn2_post_g)
    return x

def second_inputs(seed: int = 0) -> dict:
    key = jax.random.key(seed)
    ks = iter(jax.random.split(key, 48))
    L = DEPTH_2

    def nrm(shape, scale):
        return scale * jax.random.normal(next(ks), shape, jnp.float32)

    def gain(n):
        return 1.0 + 0.02 * jax.random.normal(next(ks), (L, n), jnp.float32)

    inp = {}
    inp["x"] = nrm((BATCH, SEQ, D_MODEL), 1.0)
    inp["mem"] = nrm((BATCH, MEM_LEN, D_MODEL), 1.0)
    inp["ffn1_pre_g"] = gain(D_MODEL)
    inp["ffn1_post_g"] = gain(D_MODEL)
    inp["ffn1_w_gu"] = nrm((L, D_MODEL, 2 * D_FF), D_MODEL ** -0.5)
    inp["ffn1_w_down"] = nrm((L, D_FF, D_MODEL), D_FF ** -0.5)
    inp["mix_pre_g"] = gain(D_MODEL)
    inp["mix_post_g"] = gain(D_MODEL)
    inp["w_in"] = nrm((L, D_MODEL, IN_WIDTH), D_MODEL ** -0.5)
    inp["b_gate"] = nrm((L, N_BRANCH * D_MODEL), 0.02)
    inp["da_lambda_q1"] = nrm((L, DA_HEAD_DIM), 0.1)
    inp["da_lambda_k1"] = nrm((L, DA_HEAD_DIM), 0.1)
    inp["da_lambda_q2"] = nrm((L, DA_HEAD_DIM), 0.1)
    inp["da_lambda_k2"] = nrm((L, DA_HEAD_DIM), 0.1)
    inp["da_subln_g"] = gain(2 * DA_HEAD_DIM)
    inp["ssd_conv_w"] = nrm((L, SSD_CONV, SSD_CONV_DIM), SSD_CONV ** -0.5)
    inp["ssd_conv_b"] = nrm((L, SSD_CONV_DIM), 0.02)
    u = jax.random.uniform(next(ks), (L, SSD_HEADS), jnp.float32)
    dt0 = jnp.exp(u * (math.log(0.1) - math.log(0.001)) + math.log(0.001))
    inp["ssd_dt_bias"] = dt0 + jnp.log(-jnp.expm1(-dt0))
    inp["ssd_A_log"] = jnp.log(jax.random.uniform(next(ks), (L, SSD_HEADS), jnp.float32, 1.0, 16.0))
    inp["ssd_D"] = 1.0 + nrm((L, SSD_HEADS), 0.1)
    inp["ssd_norm_g"] = gain(SSD_INNER)
    inp["w_branch_attn"] = nrm((L, DA_V, D_MODEL), DA_V ** -0.5)
    inp["w_branch_ssd"] = nrm((L, SSD_INNER, D_MODEL), SSD_INNER ** -0.5)
    inp["w_mix_out"] = nrm((L, D_MODEL, D_MODEL), D_MODEL ** -0.5)
    inp["xa_pre_g"] = gain(D_MODEL)
    inp["xa_post_g"] = gain(D_MODEL)
    inp["mem_norm_g"] = gain(D_MODEL)
    inp["xa_w_q"] = nrm((L, D_MODEL, D_MODEL), D_MODEL ** -0.5)
    inp["xa_w_kv"] = nrm((L, D_MODEL, 2 * D_MODEL), D_MODEL ** -0.5)
    inp["xa_w_o"] = nrm((L, D_MODEL, D_MODEL), D_MODEL ** -0.5)
    inp["ffn2_pre_g"] = gain(D_MODEL)
    inp["ffn2_post_g"] = gain(D_MODEL)
    inp["ffn2_w_gu"] = nrm((L, D_MODEL, 2 * D_FF), D_MODEL ** -0.5)
    inp["ffn2_w_down"] = nrm((L, D_FF, D_MODEL), D_FF ** -0.5)
    return inp

def second_block(x, mem, ffn1_pre_g, ffn1_post_g, ffn1_w_gu, ffn1_w_down,
              mix_pre_g, mix_post_g, w_in, b_gate,
              da_lambda_q1, da_lambda_k1, da_lambda_q2, da_lambda_k2, da_subln_g,
              ssd_conv_w, ssd_conv_b, ssd_dt_bias, ssd_A_log, ssd_D, ssd_norm_g,
              w_branch_attn, w_branch_ssd, w_mix_out,
              xa_pre_g, xa_post_g, mem_norm_g, xa_w_q, xa_w_kv, xa_w_o,
              ffn2_pre_g, ffn2_post_g, ffn2_w_gu, ffn2_w_down):
    for l in range(DEPTH_2):
        x = _layer(x, mem, l,
                   ffn1_pre_g[l], ffn1_post_g[l], ffn1_w_gu[l], ffn1_w_down[l],
                   mix_pre_g[l], mix_post_g[l], w_in[l], b_gate[l],
                   da_lambda_q1[l], da_lambda_k1[l], da_lambda_q2[l], da_lambda_k2[l], da_subln_g[l],
                   ssd_conv_w[l], ssd_conv_b[l], ssd_dt_bias[l], ssd_A_log[l], ssd_D[l], ssd_norm_g[l],
                   w_branch_attn[l], w_branch_ssd[l], w_mix_out[l],
                   xa_pre_g[l], xa_post_g[l], mem_norm_g[l], xa_w_q[l], xa_w_kv[l], xa_w_o[l],
                   ffn2_pre_g[l], ffn2_post_g[l], ffn2_w_gu[l], ffn2_w_down[l])
    return x


def setup_inputs(seed=0):
    out = dict(first_inputs(seed))
    for name, value in second_inputs(seed + 1).items():
        if name != "x":
            out[name + "_2"] = value
    return out


def reference(
    x, ffn_norm_a, ffn_a_w_gate, ffn_a_w_up, ffn_a_w_down, mix_norm, ffn_norm_b, ffn_b_w_gate,
    ffn_b_w_up, ffn_b_w_down, final_norm, rel_bias, mla_w_in, mla_q_norm, mla_kv_norm, mla_w_uq,
    mla_w_ukv, mla_w_o, nsa_w_in, nsa_cmp_pos_k, nsa_cmp_w1_k, nsa_cmp_w2_k, nsa_cmp_pos_v,
    nsa_cmp_w1_v, nsa_cmp_w2_v, nsa_w_o, mem_2, ffn1_pre_g_2, ffn1_post_g_2, ffn1_w_gu_2,
    ffn1_w_down_2, mix_pre_g_2, mix_post_g_2, w_in_2, b_gate_2, da_lambda_q1_2, da_lambda_k1_2,
    da_lambda_q2_2, da_lambda_k2_2, da_subln_g_2, ssd_conv_w_2, ssd_conv_b_2, ssd_dt_bias_2,
    ssd_A_log_2, ssd_D_2, ssd_norm_g_2, w_branch_attn_2, w_branch_ssd_2, w_mix_out_2,
    xa_pre_g_2, xa_post_g_2, mem_norm_g_2, xa_w_q_2, xa_w_kv_2, xa_w_o_2, ffn2_pre_g_2,
    ffn2_post_g_2, ffn2_w_gu_2, ffn2_w_down_2,
):
    x = first_block(
        x, ffn_norm_a, ffn_a_w_gate, ffn_a_w_up, ffn_a_w_down, mix_norm, ffn_norm_b,
        ffn_b_w_gate, ffn_b_w_up, ffn_b_w_down, final_norm, rel_bias, mla_w_in, mla_q_norm,
        mla_kv_norm, mla_w_uq, mla_w_ukv, mla_w_o, nsa_w_in, nsa_cmp_pos_k, nsa_cmp_w1_k,
        nsa_cmp_w2_k, nsa_cmp_pos_v, nsa_cmp_w1_v, nsa_cmp_w2_v, nsa_w_o,
    )
    return second_block(
        x, mem_2, ffn1_pre_g_2, ffn1_post_g_2, ffn1_w_gu_2, ffn1_w_down_2, mix_pre_g_2,
        mix_post_g_2, w_in_2, b_gate_2, da_lambda_q1_2, da_lambda_k1_2, da_lambda_q2_2,
        da_lambda_k2_2, da_subln_g_2, ssd_conv_w_2, ssd_conv_b_2, ssd_dt_bias_2, ssd_A_log_2,
        ssd_D_2, ssd_norm_g_2, w_branch_attn_2, w_branch_ssd_2, w_mix_out_2, xa_pre_g_2,
        xa_post_g_2, mem_norm_g_2, xa_w_q_2, xa_w_kv_2, xa_w_o_2, ffn2_pre_g_2, ffn2_post_g_2,
        ffn2_w_gu_2, ffn2_w_down_2,
    )


_drawn_inputs = setup_inputs


def setup_inputs(seed=0):
    import zlib

    import numpy as np

    out = dict(_drawn_inputs(seed))
    spreads = {}
    factors = {'ffn_norm_a': 6.445,
     'mix_norm': 7.461,
     'ffn_norm_b': 7.504,
     'final_norm': 4.202,
     'mla_q_norm': 8.0,
     'mla_kv_norm': 8.0,
     'nsa_cmp_pos_k': 8.0,
     'ffn1_pre_g_2': 3.624,
     'ffn1_post_g_2': 5.114,
     'mix_pre_g_2': 2.88,
     'mix_post_g_2': 3.973,
     'b_gate_2': 8.0,
     'da_lambda_q1_2': 5.272,
     'da_lambda_k1_2': 8.0,
     'da_subln_g_2': 6.957,
     'ssd_conv_b_2': 3.891,
     'ssd_norm_g_2': 5.429,
     'xa_pre_g_2': 5.122,
     'xa_post_g_2': 20.623,
     'mem_norm_g_2': 3.28,
     'ffn2_pre_g_2': 31.783,
     'ffn2_post_g_2': 50.424,
     'nsa_cmp_pos_v': 4.361,
     'ssd_D_2': 8.0}
    for name, (base, spread) in spreads.items():
        noise = np.random.default_rng([zlib.crc32(name.encode()), seed]).standard_normal(out[name].shape)
        drawn = base * np.exp(spread * noise) if base else spread * noise
        out[name] = __import__('jax').numpy.asarray(drawn.astype(out[name].dtype))
    for name, factor in factors.items():
        out[name] = (out[name] * factor).astype(out[name].dtype)
    return out
```

```python
from contextlib import ExitStack, contextmanager

import numpy as np
import concourse.bass as bass
from concourse import mybir

F32 = mybir.dt.float32
ACT = mybir.ActivationFunctionType
ALU = mybir.AluOpType
AX = mybir.AxisListType

P = 128
T = 256
D = 1024
DC = D // P
FF = 2816
FC = FF // P
HEADS = 16
NEG = -1e30
SLOTS = 4
SLOT_TILES = FC
MLA_Q, MLA_KV, MLA_NOPE, MLA_ROPE, MLA_V = 384, 256, 64, 32, 64
NSA_GROUPS, CMP_BLOCK, CMP_STRIDE = 4, 32, 16
N_CMP = (T - CMP_BLOCK) // CMP_STRIDE + 1
N_CMP0 = (P - CMP_BLOCK) // CMP_STRIDE + 1
REL_BUCKETS, REL_MAX_DIST = 32, 128
TOEP = 2 * T - P - 1
DA_HEADS = 8
SSD_HEADS, SSD_GROUPS, SSD_INNER = 32, 4, 2048
SSD_P = SSD_INNER // SSD_HEADS
SC = SSD_INNER // P
XBC = (SSD_INNER + 2 * SSD_GROUPS * P) // P
CONV = 4
XA_HEADS = 4
LAM_INIT = 0.8 - 0.6



def plan():
    ffn = lambda n: [(n + "_gu", FC, 2 * DC, 1), (n + "_dn", DC, FC, 1)]
    return (
        ffn("ffn_a0") + [("mla_in", 4, 14, 2), ("mla_uq", 4, 12, 4), ("mla_uk", 1, 16, 8), ("mla_uv", 1, 16, 4),
                         ("mla_o", 4, 16, 2)]
        + ffn("ffn_b0") + ffn("ffn_a1")
        + [("nsa_in", 8, 16, 2), ("nsa_v", 2, 16, 1), ("nsa_g", 1, 3, 1), ("nsa_w1", 2, 16, 1), ("nsa_w2", 1, 2, 2),
           ("nsa_o", 4, 16, 2)]
        + ffn("ffn_b1") + ffn("ffn1")
        + [("da_qk", 8, 16, 2), ("da_v", 4, 16, 1), ("gate", 8, 16, 2), ("br_attn", 4, 16, 2),
           ("z", 8, 16, 2), ("xbc", 12, 16, 2), ("dt", 1, 2, 1), ("br_ssd", 8, 16, 1), ("mix_out", 4, 16, 2),
           ("xa_q", 4, 16, 2), ("xa_k", 4, 16, 2), ("xa_v", 4, 16, 1), ("xa_o", 4, 16, 2)]
        + ffn("ffn2"))


VECS = {}


def vec_layout():
    at = 0
    for name, n in (("ffn_a0", 8), ("mix0", 8), ("ffn_b0", 8), ("ffn_a1", 8), ("mix1", 8), ("ffn_b1", 8), ("final", 8),
                    ("cq", 3), ("ckv", 2), ("pos_k", 16), ("pos_v", 16),
                    ("ffn1_pre", 8), ("ffn1_post", 8), ("mix_pre", 8), ("mix_post", 8), ("b_gate", 16), ("subln", 1),
                    ("conv_w", XBC * CONV), ("conv_b", XBC), ("ssd_D", SC), ("ssd_g", SC),
                    ("xa_pre", 8), ("xa_post", 8), ("mem", 8), ("ffn2_pre", 8), ("ffn2_post", 8),
                    ("dt_bias", 32), ("A_log", 32), ("lam", 4)):
        VECS[name] = (at, n)
        at += n
    return at


N_VEC = vec_layout()
CONSTS = {}


def const_layout():
    at = 0
    for name, n in (("ident", P), ("ones", P), ("tri", P), ("mask", T), ("cos", T), ("sin", T), ("valid", 2 * N_CMP),
                    ("bucket", TOEP)):
        CONSTS[name] = (at, n)
        at += n
    return at


N_CONST = const_layout()


def shape_constants():
    c = np.zeros((P, N_CONST), np.float32)

    def put(name, a):
        at, n = CONSTS[name]
        c[:a.shape[0], at:at + n] = a

    p = np.arange(P)
    put("ident", np.eye(P))
    put("ones", np.ones((P, P)))
    put("tri", p[:, None] <= p[None, :])
    put("mask", np.where(np.arange(T)[None, :] > P + p[:, None], NEG, 0.0))
    half = MLA_ROPE // 2
    inv = np.float32(10000.0) ** (-np.arange(half, dtype=np.float32) * np.float32(2.0 / MLA_ROPE))
    ang = np.arange(T, dtype=np.float32)[:, None] * inv[None, :]
    row = p % half
    sign = np.where(p % MLA_ROPE < half, -1.0, 1.0)[:, None]
    put("cos", np.cos(ang).T[row])
    put("sin", np.sin(ang).T[row] * sign)
    ends = np.arange(N_CMP) * CMP_STRIDE + CMP_BLOCK - 1
    valid = [(q0 + p[:, None] >= ends[None, :]) for q0 in (0, P)]
    put("valid", np.concatenate(valid, axis=1))
    dist = T - 1 - np.arange(TOEP)
    n = np.maximum(dist, 0)
    exact = REL_BUCKETS // 2
    large = exact + (np.log(np.maximum(n, 1).astype(np.float32) / np.float32(exact)) / np.float32(np.log(REL_MAX_DIST / exact))
                     * np.float32(REL_BUCKETS - exact)).astype(np.int32)
    bucket = np.where(n < exact, n, np.minimum(large, REL_BUCKETS - 1))
    hot = np.zeros((REL_BUCKETS + 1, TOEP))
    hot[:REL_BUCKETS] = (bucket[None, :] == np.arange(REL_BUCKETS)[:, None]) & (dist >= 0)
    hot[REL_BUCKETS] = np.where(dist < 0, NEG, 0.0)
    put("bucket", hot)
    return c


def m_major(w, per_block):
    k, m = w.shape[0] // P, w.shape[1] // P
    t = w.reshape(k, P, m // per_block, per_block, P).transpose(2, 1, 3, 0, 4)
    return np.ascontiguousarray(t).reshape(m // per_block, P, per_block * k * P)


def k_major(w, cols):
    k, n = w.shape[0] // P, w.shape[1] // cols
    t = w.reshape(k, P, n, cols).transpose(2, 1, 0, 3)
    return np.ascontiguousarray(t).reshape(n, P, k * cols)


def lay_out(x):
    a = {}

    def ffn(name, g, u, d):
        gu = np.concatenate([g.reshape(D, FC, 1, P), u.reshape(D, FC, 1, P)], axis=2).reshape(D, 2 * FF)
        a[name + "_gu"] = m_major(gu, 2)
        a[name + "_dn"] = m_major(d, 1)

    for l in range(2):
        for s in "ab":
            ffn(f"ffn_{s}{l}", x[f"ffn_{s}_w_gate"][l], x[f"ffn_{s}_w_up"][l], x[f"ffn_{s}_w_down"][l])
    for n in ("1", "2"):
        gu = x[f"ffn{n}_w_gu_2"][0]
        ffn(f"ffn{n}", gu[:, :FF], gu[:, FF:], x[f"ffn{n}_w_down_2"][0])
    half = MLA_ROPE // 2
    turned = lambda w: np.concatenate([w[..., half:], w[..., :half]], axis=-1)
    w = x["mla_w_in"][0]
    kr = w[:, MLA_Q + MLA_KV:]
    w = np.concatenate([w[:, :MLA_Q + MLA_KV]] + [kr] * 4 + [turned(kr)] * 4, axis=1)
    t = w.reshape(DC, P, 7, P).transpose(2, 1, 0, 3).reshape(7, P, DC * P)
    a["mla_in"] = np.ascontiguousarray(t)
    w = x["mla_w_uq"][0].reshape(MLA_Q, HEADS, MLA_NOPE + MLA_ROPE)
    rope = w[:, :, MLA_NOPE:]
    both = np.concatenate([rope.reshape(MLA_Q, 4, 1, P), turned(rope).reshape(MLA_Q, 4, 1, P)], axis=2)
    w = np.concatenate([w[:, :, :MLA_NOPE].reshape(MLA_Q, -1), both.reshape(MLA_Q, -1)], axis=1)
    a["mla_uq"] = m_major(w, 4)
    w = x["mla_w_ukv"][0].reshape(MLA_KV, HEADS, MLA_NOPE + MLA_V)
    a["mla_uk"] = m_major(w[:, :, :MLA_NOPE].reshape(MLA_KV, -1), 8)
    a["mla_uv"] = k_major(w[:, :, MLA_NOPE:].reshape(MLA_KV, -1), D)
    a["mla_o"] = m_major(x["mla_w_o"][0], 2)
    w = x["nsa_w_in"][0]
    q, kc, vc, ks, vs, kw, vw, g = np.split(w, np.cumsum([D] + [256] * 6), axis=1)
    a["nsa_in"] = m_major(np.concatenate([q, kc, vc, ks, kw], axis=1), 2)
    a["nsa_v"] = k_major(np.concatenate([vs, vw], axis=1), 256)
    a["nsa_g"] = k_major(g, 48)
    a["nsa_w1"] = np.concatenate([k_major(x["nsa_cmp_w1_k"][0], P), k_major(x["nsa_cmp_w1_v"][0], P)])
    w2k, w2v = x["nsa_cmp_w2_k"][0], x["nsa_cmp_w2_v"][0]
    a["nsa_w2"] = np.concatenate([w2k, w2k, w2v, w2v], axis=1)[None]
    a["nsa_o"] = m_major(x["nsa_w_o"][0], 2)
    w = x["w_in_2"][0]
    q, k, v, z, xbc, dt, gate = np.split(w, np.cumsum([D, D, D, SSD_INNER, XBC * P, SSD_HEADS]), axis=1)
    a["da_qk"] = m_major(np.concatenate([q, k], axis=1), 2)
    a["da_v"] = k_major(v, 256)
    a["gate"] = m_major(gate, 2)
    a["z"] = m_major(z, 2)
    a["xbc"] = m_major(xbc, 2)
    a["dt"] = k_major(dt, SSD_HEADS)
    a["br_attn"] = m_major(x["w_branch_attn_2"][0], 2)
    a["br_ssd"] = m_major(x["w_branch_ssd_2"][0], 1)
    a["mix_out"] = m_major(x["w_mix_out_2"][0], 2)
    a["xa_q"] = m_major(x["xa_w_q_2"][0], 2)
    kv = x["xa_w_kv_2"][0]
    a["xa_k"] = m_major(kv[:, :D], 2)
    a["xa_v"] = k_major(kv[:, D:], 256)
    a["xa_o"] = m_major(x["xa_w_o_2"][0], 2)

    cols = lambda v: v.reshape(-1, P).T
    wide = lambda v: np.broadcast_to(v, (P, v.shape[-1]))
    vec = {
        "ffn_a0": cols(x["ffn_norm_a"][0]), "ffn_a1": cols(x["ffn_norm_a"][1]),
        "mix0": cols(x["mix_norm"][0]), "mix1": cols(x["mix_norm"][1]),
        "ffn_b0": cols(x["ffn_norm_b"][0]), "ffn_b1": cols(x["ffn_norm_b"][1]),
        "final": cols(x["final_norm"]), "cq": cols(x["mla_q_norm"]), "ckv": cols(x["mla_kv_norm"]),
        "pos_k": cols(x["nsa_cmp_pos_k"]), "pos_v": cols(x["nsa_cmp_pos_v"]),
        "ffn1_pre": cols(x["ffn1_pre_g_2"]), "ffn1_post": cols(x["ffn1_post_g_2"]),
        "mix_pre": cols(x["mix_pre_g_2"]), "mix_post": cols(x["mix_post_g_2"]),
        "b_gate": cols(x["b_gate_2"]), "subln": cols(x["da_subln_g_2"]),
        "conv_w": x["ssd_conv_w_2"][0].reshape(CONV, XBC, P).transpose(2, 1, 0).reshape(P, -1),
        "conv_b": cols(x["ssd_conv_b_2"]),
        "ssd_D": cols(np.repeat(x["ssd_D_2"][0], SSD_P)), "ssd_g": cols(x["ssd_norm_g_2"]),
        "xa_pre": cols(x["xa_pre_g_2"]), "xa_post": cols(x["xa_post_g_2"]), "mem": cols(x["mem_norm_g_2"]),
        "ffn2_pre": cols(x["ffn2_pre_g_2"]), "ffn2_post": cols(x["ffn2_post_g_2"]),
        "dt_bias": wide(x["ssd_dt_bias_2"]), "A_log": wide(x["ssd_A_log_2"]),
    }
    vecs = np.zeros((P, N_VEC), np.float32)
    for name, v in vec.items():
        at, n = VECS[name]
        vecs[:, at:at + n] = v
    at = VECS["lam"][0]
    for i, name in enumerate(("q1", "k1", "q2", "k2")):
        vecs[:64, at + i] = x[f"da_lambda_{name}_2"][0]
    a["vecs"] = vecs
    a["consts"] = shape_constants()
    a["rel_bias"] = x["rel_bias"]
    feature_major = lambda v: np.ascontiguousarray(v[0].reshape(T, DC, P).transpose(2, 1, 0))
    a["xT"] = feature_major(x["x"])
    a["memT"] = feature_major(x["mem_2"])
    return a




class Steps:

    def __init__(self, sem):
        self.sem, self.n = sem, 0

    def step(self, engine, instruction):
        self.n += 1
        instruction.then_inc(self.sem, 1)
        engine.wait_ge(self.sem, self.n)


class Ring:

    def __init__(self, nc, ctx, w):
        self.buf = [ctx.enter_context(nc.sbuf_tensor(f"weights{s}", [P, SLOT_TILES * P], F32)) for s in range(SLOTS)]
        self.loaded = [ctx.enter_context(nc.semaphore(f"loaded{s}")) for s in range(SLOTS)]
        self.mm_done = ctx.enter_context(nc.semaphore("mm_done"))
        self.blocks, self.first, self.chunk0 = [], {}, {}
        self.end, chunks = [], 0
        for name, n, tiles, per in plan():
            self.first[name] = len(self.blocks)
            self.chunk0[name] = chunks
            for i in range(n):
                if name == "mla_in" and i == n - 1:
                    tiles, per = 7, 1
                self.blocks.append((w[name], name, i, n))
                chunks += per
                self.end.append(chunks)
        self.chunks = chunks

    def source(self, n):
        ap, name, i, _ = self.blocks[n]
        if name == "mla_in":
            m = 2 if i < 3 else 1
            return ap[2 * i:2 * i + m].rearrange("m p c -> p m c"), m * DC * P
        return ap[i], ap.shape[2]

    def load(self, sp, n):
        if n >= len(self.blocks):
            return
        if n >= SLOTS:
            sp.wait_ge(self.mm_done, self.end[n - SLOTS])
        src, size = self.source(n)
        dst = self.buf[n % SLOTS][:, 0:size]
        if len(src.shape) == 3:
            dst = dst.rearrange("p (m c) -> p m c", m=src.shape[1])
        sp.dma_start(dst, src).then_inc(self.loaded[n % SLOTS], 16)

    def loads(self, sp, name):
        a = self.first[name]
        for n in range(a, a + self.blocks[a][3]):
            self.load(sp, n + SLOTS)

    def arrived(self, pe, n):
        pe.wait_ge(self.loaded[n % SLOTS], 16 * (n // SLOTS + 1))

    def tile(self, n, t, cols=P):
        return self.buf[n % SLOTS][:, t * P:t * P + cols]


def emit(nc, w, out, stop=None, dump=None):
    root = ExitStack()
    uid = [0]
    in_use = []
    with root:
        def make(ctx):
            def sb(name, shape):
                uid[0] += 1
                return ctx.enter_context(nc.sbuf_tensor(f"{name}_{uid[0]}", shape, F32))
            return sb

        @contextmanager
        def scope():
            with ExitStack() as c:
                yield make(c)

        def semaphores(*names):
            uid[0] += 1
            new = [nc.alloc_semaphore(name=f"{n}_{uid[0]}") for n in names]
            in_use.extend(new)
            return new

        def recycle():
            nc.clear_and_free_semaphores(list(in_use))
            nc.all_engine_barrier()
            in_use.clear()

        def block():
            return nc.Block(no_gpsimd_drain=True)

        ring = Ring(nc, root, w)
        mm_done = ring.mm_done
        sb = make(root)
        h = sb("residual", [P, DC, T])
        vecs = sb("vecs", [P, N_VEC])
        consts = sb("consts", [P, N_CONST])
        bank = [root.enter_context(nc.psum_tensor(f"bank{i}", [P, 512], F32)) for i in range(8)]

        def const(name):
            at, n = CONSTS[name]
            return consts[:, at:at + n]

        def vec(name, i=0, n=1):
            at, _ = VECS[name]
            return vecs[:, at + i:at + i + n]

        ident, ones, tri = const("ident"), const("ones"), const("tri")
        finished = [False]

        at_start, = semaphores("at_start")
        with block() as b:
            @b.sync
            def _(sp):
                sp.dma_start(h[:, :, :], w["xT"]).then_inc(at_start, 16)
                sp.dma_start(vecs[:, :], w["vecs"]).then_inc(at_start, 16)
                sp.dma_start(consts[:, :], w["consts"]).then_inc(at_start, 16)
                for n in range(SLOTS):
                    ring.load(sp, n)
                sp.wait_ge(at_start, 48)


        def norm(src, dst, gain, chunks, eps, groups=1, residual=None):
            n = chunks * groups
            assert groups <= 8
            squared, summed, rooted, d_step = semaphores("squared", "summed", "rooted", "norm_step")
            with scope() as s:
                sq = s("squares", [P, n, T])
                rt = s("root", [P, groups, T])
                inv = s("inverse", [P, groups, T])
                y = s("normed", [P, T])
                sums = [bank[g][:, 0:T] for g in range(groups)]
                with block() as b:
                    @b.scalar
                    def _(act):
                        for c in range(n):
                            act.activation(sq[:, c, :], src[:, c, :], ACT.Square).then_inc(squared, 1)
                        for g in range(groups):
                            act.wait_ge(summed, g + 1)
                            act.activation(rt[:, g, :], sums[g], ACT.Sqrt, bias=eps_of(eps),
                                           scale=1.0 / (chunks * P)).then_inc(rooted, 1)

                    @b.tensor
                    def _(pe):
                        for g in range(groups):
                            for c in range(chunks):
                                pe.wait_ge(squared, g * chunks + c + 1)
                                last = pe.matmul(sums[g], ones, sq[:, g * chunks + c, :], start=c == 0, stop=c == chunks - 1)
                            last.then_inc(summed, 1)

                    @b.vector
                    def _(dve):
                        steps = Steps(d_step)
                        for g in range(groups):
                            dve.wait_ge(rooted, g + 1)
                            steps.step(dve, dve.reciprocal(inv[:, g, :], rt[:, g, :]))
                            for c in range(g * chunks, (g + 1) * chunks):
                                if residual is None:
                                    dve.scalar_tensor_tensor(out=dst[:, c, :], in0=src[:, c, :], scalar=gain(c),
                                                             in1=inv[:, g, :], op0=ALU.mult, op1=ALU.mult)
                                    continue
                                steps.step(dve, dve.scalar_tensor_tensor(
                                    out=y[:, :], in0=src[:, c, :], scalar=gain(c), in1=inv[:, g, :],
                                    op0=ALU.mult, op1=ALU.mult))
                                steps.step(dve, dve.scalar_tensor_tensor(
                                    out=dst[:, c, :], in0=y[:, :], scalar=residual, in1=dst[:, c, :],
                                    op0=ALU.mult, op1=ALU.add))

        eps_const = {}

        def eps_of(eps):
            return eps_const[eps]

        eps_tile = sb("eps", [P, 2])
        with block() as b:
            @b.vector
            def _(dve):
                for i, e in enumerate((1e-6, 1e-5)):
                    dve.memset(eps_tile[:, i:i + 1], e)
                    eps_const[e] = eps_tile[:, i:i + 1]

        def pe_linear(pe, name, x_of, k, m, free, base=0, banks=(0, 1, 2, 3), rhs_free=None, skip=0, group=None):
            n0, c0 = ring.first[name], ring.chunk0[name]
            for j in range(m):
                chunk = c0 + j + 1
                n = n0 + next(i for i in range(10 ** 6) if ring.end[n0 + i] >= chunk)
                start = ring.end[n - 1] if n else 0
                if chunk - 1 == start:
                    ring.arrived(pe, n)
                tile0 = (chunk - 1 - start) * k
                i = base + j
                if i >= len(banks):
                    pe.wait_ge(free, i - len(banks) + 1)
                for c in range(k):
                    last = pe.matmul(bank[banks[i % len(banks)]][:, 0:T], ring.tile(n, tile0 + c), x_of(c),
                                     start=c == 0, stop=c == k - 1)
                last.then_inc(mm_done, 1)

        def pe_token_major(pe, name, x_of, k, blocks, cols, free, base=0, banks=(0, 1, 2, 3)):
            n0 = ring.first[name]
            for j in range(blocks):
                ring.arrived(pe, n0 + j)
                i = base + j
                if i >= len(banks):
                    pe.wait_ge(free, i - len(banks) + 1)
                for t in range(2):
                    for c in range(k):
                        last = pe.matmul(bank[banks[i % len(banks)]][:, t * cols:(t + 1) * cols],
                                         x_of(c)[:, t * P:(t + 1) * P], ring.buf[(n0 + j) % SLOTS][:, c * cols:(c + 1) * cols],
                                         start=c == 0, stop=c == k - 1)
                last.then_inc(mm_done, 1)

        def ffn(name, src, gate_scale, y=None):
            gu0, dn0 = ring.first[name + "_gu"], ring.first[name + "_dn"]
            gu_c, dn_c = ring.chunk0[name + "_gu"], ring.chunk0[name + "_dn"]
            silu_ready, act_done, out_done = semaphores("silu_ready", "act_done", "out_done")
            trips, rest = divmod(FC, SLOTS)
            slot = lambda j: (gu0 + j) % SLOTS
            with scope() as s:
                sg = s("silu", [P, 2, T])
                act_t = s("hidden", [P, FC * T])
                with block() as b:
                    @b.sync
                    def _(sp):
                        def gate_up(i, j):
                            sp.wait_ge(mm_done, i + (gu_c + 1))
                            src_block = w[name + "_gu"][bass.ds(i + SLOTS, 1)].rearrange("a p c -> (a p) c")
                            sp.dma_start(ring.buf[slot(j)][:, 0:2 * DC * P], src_block).then_inc(ring.loaded[slot(j)], 16)

                        loads = FC - SLOTS
                        with sp.Fori(0, loads // SLOTS) as t:
                            for j in range(SLOTS):
                                gate_up(t * SLOTS + j, j)
                        for i in range(loads // SLOTS * SLOTS, loads):
                            ring.load(sp, gu0 + SLOTS + i)
                        for n in range(gu0 + FC, dn0 + DC):
                            ring.load(sp, n)
                        for n in range(dn0 + DC, dn0 + DC + SLOTS):
                            ring.load(sp, n)

                    @b.tensor
                    def _(pe):
                        def gate_up(i, j):
                            pe.wait_ge(ring.loaded[slot(j)], i * (16 // SLOTS) + (16 * ((gu0 + j) // SLOTS + 1) - j * (16 // SLOTS)))
                            pe.wait_ge(act_done, i + 1)
                            for half in range(2):
                                for c in range(DC):
                                    last = pe.matmul(bank[j % 2][:, half * T:half * T + T],
                                                     ring.buf[slot(j)][:, (half * DC + c) * P:(half * DC + c + 1) * P],
                                                     src[:, c, :], start=c == 0, stop=c == DC - 1)
                            last.then_inc(mm_done, 1)

                        with pe.Fori(0, trips) as t:
                            for j in range(SLOTS):
                                gate_up(t * SLOTS + j, j)
                        for j in range(rest):
                            gate_up(trips * SLOTS + j, j)
                        pe.wait_ge(act_done, FC + 2)
                        for m in range(DC):
                            ring.arrived(pe, dn0 + m)
                            pe.wait_ge(out_done, m + 1)
                            for c in range(FC):
                                last = pe.matmul(bank[2 + m % 2][:, 0:T], ring.tile(dn0 + m, c),
                                                 act_t[:, c * T:(c + 1) * T], start=c == 0, stop=c == FC - 1)
                            last.then_inc(mm_done, 1)

                    @b.scalar
                    def _(act):
                        def silu(i, j):
                            act.wait_ge(mm_done, i + (gu_c + 1))
                            act.wait_ge(act_done, i + 1)
                            act.activation(sg[:, j % 2, :], bank[j % 2][:, 0:T], ACT.Silu).then_inc(silu_ready, 1)

                        with act.Fori(0, FC // 2) as t:
                            for j in range(2):
                                silu(t * 2 + j, j)

                    @b.vector
                    def _(dve):
                        dve.sem_inc(act_done, 2)
                        dve.sem_inc(out_done, 2)

                        def product(i, j):
                            dve.wait_ge(silu_ready, i + 1)
                            dve.tensor_tensor(act_t[:, bass.ds(i * T, T)], sg[:, j % 2, :], bank[j % 2][:, T:2 * T],
                                              ALU.mult).then_inc(act_done, 1)

                        with dve.Fori(0, FC // 2) as t:
                            for j in range(2):
                                product(t * 2 + j, j)

                        for m in range(DC):
                            dve.wait_ge(mm_done, dn_c + m + 1)
                            o = bank[2 + m % 2][:, 0:T]
                            if y is None:
                                dve.scalar_tensor_tensor(out=h[:, m, :], in0=o, scalar=0.5, in1=h[:, m, :],
                                                         op0=ALU.mult, op1=ALU.add).then_inc(out_done, 1)
                            else:
                                dve.tensor_copy(y[:, m, :], o).then_inc(out_done, 1)

        def full_ffn(name, pre, eps=1e-6, post=None):
            with scope() as s:
                x = s("normed", [P, DC, T])
                norm(h, x, lambda c: vec(pre, c), DC, eps)
                if post is None:
                    ffn(name, x, 1.0)
                    return
                y = s("ffn_out", [P, DC, T])
                ffn(name, x, 1.0, y)
                norm(y, h, lambda c: vec(post, c), DC, eps, residual=0.5)

        def linear_stage(name, x, k, m, leave):
            free, = semaphores("left")
            with block() as b:
                @b.sync
                def _(sp):
                    ring.loads(sp, name)

                @b.tensor
                def _(pe):
                    pe_linear(pe, name, lambda c: x[:, c, :], k, m, free)

                @b.vector
                def _(dve):
                    for j in range(m):
                        dve.wait_ge(mm_done, ring.chunk0[name] + j + 1)
                        leave(dve, j, bank[j % 4][:, 0:T]).then_inc(free, 1)

        def add_to_h(dve, j, o):
            return dve.tensor_tensor(h[:, j, :], o, h[:, j, :], ALU.add)

        def attention(jobs, oT, n_out, scale=1.0, causal=True):
            (s_ready, s_max, exp_done, p_ready, t_ready, pt_ready, v_done, o_ready, o_done, d_step) = semaphores(
                "s_ready", "s_max", "exp_done", "p_ready", "t_ready", "pt_ready", "v_done", "o_ready", "o_done",
                "attn_step")
            n = len(jobs)
            w0 = P if causal else T
            width = T + w0
            rows = ((1, 0, T), (0, T, w0))
            cuts = [(T, 0), (0, P)] + ([(P, 2 * P)] if causal else [(T + P, 2 * P), (P, 3 * P)])
            with scope() as s:
                sc = s("scores", [P, 2, width])
                pr = s("probs", [P, 2, width])
                pt = s("probsT", [P, 2, width])
                nm = s("neg_max", [P, 2, 2])
                sm = s("sums", [P, 2, 2])
                cf = s("coef", [P, 2, 2])
                zero = s("no_mask", [P, T])
                with block() as b:
                    @b.gpsimd
                    def _(pool):
                        pool.memset(zero[:, :], 0.0).then_inc(d_step, 1)

                    @b.tensor
                    def _(pe):
                        def score(j):
                            if j >= 2:
                                pe.wait_ge(s_max, 2 * (j - 1))
                            for q, at, keys in rows:
                                parts = jobs[j]["scores"]
                                for i, (qf, kf) in enumerate(parts):
                                    last = pe.matmul(bank[j % 2][:, at:at + keys], qf[:, q * P:(q + 1) * P],
                                                     kf[:, 0:keys], start=i == 0, stop=i == len(parts) - 1)
                            last.then_inc(s_ready, 1)

                        def turn(j):
                            pe.wait_ge(p_ready, j + 1)
                            if j >= 2:
                                pe.wait_ge(pt_ready, j - 1)
                            for a, c in cuts:
                                last = pe.transpose(bank[2 + j % 2][:, c:c + P], pr[:, j % 2, a:a + P], ident)
                            last.then_inc(t_ready, 1)

                        def values(j):
                            job = jobs[j]
                            pe.wait_ge(pt_ready, j + 1)
                            for i, (chunk, r0, rn, v) in enumerate(job["outs"]):
                                o = bank[4 + chunk % 4]
                                if job["first"] and chunk >= 4:
                                    pe.wait_ge(o_done, chunk - 3)
                                x = job.get("extra") if job["first"] else None
                                if x:
                                    pe.matmul(o[r0:r0 + rn, 0:T], x[0], x[1], start=True, stop=False)
                                pe.matmul(o[r0:r0 + rn, 0:T], v(0), pt[:, j % 2, 0:T],
                                          start=job["first"] and not x, stop=False)
                                a, c = (P, T) if causal else (0, T)
                                last = pe.matmul(o[r0:r0 + rn, a:T], v(1), pt[:, j % 2, c:width], start=False,
                                                 stop=job["last"])
                                if job["evict"] and i < len(job["outs"]) - 1:
                                    last.then_inc(o_ready, 1)
                            last.then_inc(v_done, 1)
                            if job["evict"]:
                                pe.wait_ge(v_done, j + 1)
                                pe.sem_inc(o_ready, 1)

                        for j in range(n + 2):
                            if j < n:
                                score(j)
                            if 0 <= j - 1 < n:
                                turn(j - 1)
                            if 0 <= j - 2 < n:
                                values(j - 2)

                    @b.vector
                    def _(dve):
                        steps = Steps(d_step)
                        steps.n = 1
                        dve.wait_ge(d_step, 1)

                        def peak(j):
                            dve.wait_ge(s_ready, j + 1)
                            if j >= 2:
                                dve.wait_ge(exp_done, 2 * (j - 1))
                            for i, (q, at, keys) in enumerate(rows):
                                add = jobs[j]["add"]
                                m = zero[:, 0:keys] if add is None else add[:, T - keys:T]
                                dve.tensor_tensor_reduce(
                                    out=sc[:, j % 2, at:at + keys], in0=bank[j % 2][:, at:at + keys], in1=m,
                                    scale=-scale, scalar=3e38, op0=ALU.add, op1=ALU.min,
                                    accum_out=nm[:, j % 2, i:i + 1]).then_inc(s_max, 1)

                        def weigh(j):
                            dve.wait_ge(exp_done, 2 * (j + 1))
                            steps.step(dve, dve.reciprocal(cf[:, j % 2, :], sm[:, j % 2, :]))
                            if jobs[j].get("coef") is not None:
                                steps.step(dve, dve.tensor_tensor(cf[:, j % 2, :], cf[:, j % 2, :], jobs[j]["coef"], ALU.mult))
                            for i, (q, at, keys) in enumerate(rows):
                                last = dve.tensor_scalar(pr[:, j % 2, at:at + keys], pr[:, j % 2, at:at + keys],
                                                         cf[:, j % 2, i:i + 1], None, ALU.mult)
                                if i == 0:
                                    steps.step(dve, last)
                            last.then_inc(p_ready, 1)

                        for j in range(n + 1):
                            if j < n:
                                peak(j)
                            if j >= 1:
                                weigh(j - 1)

                    @b.scalar
                    def _(act):
                        def exps(j):
                            if j >= 2:
                                act.wait_ge(t_ready, j - 1)
                            for i, (q, at, keys) in enumerate(rows):
                                act.wait_ge(s_max, 2 * j + i + 1)
                                act.activation(pr[:, j % 2, at:at + keys], sc[:, j % 2, at:at + keys], ACT.Exp,
                                               bias=nm[:, j % 2, i:i + 1], scale=-1.0,
                                               accum_out=sm[:, j % 2, i:i + 1]).then_inc(exp_done, 1)

                        def copies(j):
                            act.wait_ge(t_ready, j + 1)
                            if j >= 2:
                                act.wait_ge(v_done, j - 1)
                            act.activation(pt[:, j % 2, :], bank[2 + j % 2][:, 0:width], ACT.Copy).then_inc(pt_ready, 1)

                        def leave(j):
                            for chunk in sorted({o[0] for o in jobs[j]["outs"]}) if jobs[j]["evict"] else ():
                                act.wait_ge(o_ready, chunk + 1)
                                act.activation(oT[:, chunk, :], bank[4 + chunk % 4][:, 0:T], ACT.Copy).then_inc(o_done, 1)

                        for j in range(n + 2):
                            if j < n:
                                exps(j)
                            if 0 <= j - 1 < n:
                                copies(j - 1)
                            if 0 <= j - 2 < n:
                                leave(j - 2)

        def token_major_stage(name, x, k, blocks, leave, cols=256):
            free, = semaphores("left")
            with block() as b:
                @b.sync
                def _(sp):
                    ring.loads(sp, name)

                @b.tensor
                def _(pe):
                    pe_token_major(pe, name, lambda c: x[:, c, :], k, blocks, cols, free)

                @b.vector
                def _(dve):
                    for j in range(blocks):
                        dve.wait_ge(mm_done, ring.chunk0[name] + j + 1)
                        leave(dve, j, bank[j % 4][:, 0:2 * cols].rearrange("p (t c) -> p t c", t=2)).then_inc(free, 1)

        def done(name):
            if stop == name:
                finished[0] = True
            return finished[0]


        def mla():
            with scope() as s:
                x = s("normed", [P, DC, T])
                norm(h, x, lambda c: vec("mix0", c), DC, 1e-6)
                c_in = s("latents", [P, 5, T])
                k_rope = s("k_rope", [P, T])
                tmp = s("tmp", [P, 2, T])
                free, d_step = semaphores("left", "mla_step")
                with block() as b:
                    @b.sync
                    def _(sp):
                        ring.loads(sp, "mla_in")

                    @b.tensor
                    def _(pe):
                        pe_linear(pe, "mla_in", lambda c: x[:, c, :], DC, 7, free)

                    @b.vector
                    def _(dve):
                        steps = Steps(d_step)
                        for j in range(7):
                            dve.wait_ge(mm_done, ring.chunk0["mla_in"] + j + 1)
                            o = bank[j % 4][:, 0:T]
                            if j < 5:
                                dve.tensor_copy(c_in[:, j, :], o).then_inc(free, 1)
                            else:
                                steps.step(dve, dve.tensor_tensor(tmp[:, j - 5, :], o, const(("cos", "sin")[j - 5]), ALU.mult))
                        dve.tensor_tensor(k_rope[:, :], tmp[:, 0, :], tmp[:, 1, :], ALU.add)
                cn = s("latents_normed", [P, 5, T])
                norm(c_in[:, 0:3, :], cn[:, 0:3, :], lambda c: vec("cq", c), 3, 1e-6)
                norm(c_in[:, 3:5, :], cn[:, 3:5, :], lambda c: vec("ckv", c), 2, 1e-6)
                q_n = s("q_nope", [P, 8, T])
                q_r = s("q_rope", [P, 4, T])
                k_n = s("k_nope", [P, 8, T])
                v = s("v", [P, 2, D])
                free, d_step = semaphores("left", "mla_step")
                with block() as b:
                    @b.sync
                    def _(sp):
                        for name in ("mla_uq", "mla_uk", "mla_uv"):
                            ring.loads(sp, name)

                    @b.tensor
                    def _(pe):
                        pe_linear(pe, "mla_uq", lambda c: cn[:, c, :], 3, 16, free)
                        pe_linear(pe, "mla_uk", lambda c: cn[:, 3 + c, :], 2, 8, free, base=16)
                        nv = ring.first["mla_uv"]
                        ring.arrived(pe, nv)
                        for j in range(4):
                            t, half = divmod(j, 2)
                            pe.wait_ge(free, 24 + j - 3)
                            for c in range(2):
                                last = pe.matmul(bank[j % 4][:, 0:512], cn[:, 3 + c, t * P:(t + 1) * P],
                                                 ring.buf[nv % SLOTS][:, c * D + half * 512:c * D + half * 512 + 512],
                                                 start=c == 0, stop=c == 1)
                            last.then_inc(mm_done, 1)

                    @b.vector
                    def _(dve):
                        steps = Steps(d_step)
                        c0 = ring.chunk0["mla_uq"]
                        for j in range(28):
                            dve.wait_ge(mm_done, c0 + j + 1)
                            o = bank[j % 4][:, 0:T]
                            if j < 8:
                                dve.tensor_copy(q_n[:, j, :], o).then_inc(free, 1)
                            elif j < 16:
                                turned = (j - 8) % 2
                                dve.tensor_tensor(tmp[:, turned, :], o, const(("cos", "sin")[turned]), ALU.mult).then_inc(free, 1)
                                if turned:
                                    dve.wait_ge(free, j + 1)
                                    steps.step(dve, dve.tensor_tensor(q_r[:, (j - 8) // 2, :], tmp[:, 0, :], tmp[:, 1, :], ALU.add))
                            elif j < 24:
                                dve.tensor_copy(k_n[:, j - 16, :], o).then_inc(free, 1)
                            else:
                                t, half = divmod(j - 24, 2)
                                dve.tensor_copy(v[:, t, half * 512:half * 512 + 512], bank[j % 4][:, :]).then_inc(free, 1)
                oT = s("heads_out", [P, DC, T])
                jobs = []
                for hd in range(HEADS):
                    c, r = hd // 2, 64 * (hd % 2)
                    rr = 32 * (hd % 4)
                    jobs.append(dict(
                        scores=[(q_n[r:r + 64, c, :], k_n[r:r + 64, c, :]),
                                (q_r[rr:rr + 32, hd // 4, :], k_rope[rr:rr + 32, :])],
                        add=const("mask"), first=True, last=True, evict=hd % 2 == 1,
                        outs=[(c, r, 64, lambda kb, hd=hd: v[:, kb, hd * 64:hd * 64 + 64])]))
                attention(jobs, oT, 8, scale=(MLA_NOPE + MLA_ROPE) ** -0.5)
                linear_stage("mla_o", oT, DC, DC, add_to_h)

        def nsa():
            with scope() as s:
                qT = s("q", [P, DC, T])
                k_s = s("k_sel", [P, NSA_GROUPS, T])
                k_w = s("k_win", [P, NSA_GROUPS, T])
                v_s = s("v_sel", [P, 2, 256])
                v_w = s("v_win", [P, 2, 256])
                gates = s("gates", [P, 2, 48])
                bias = s("bias", [P, HEADS, T])
                vcm = s("v_cmp", [N_CMP, NSA_GROUPS, 64])
                pTc = s("probsT_cmp", [N_CMP, HEADS, T])
                oT = s("heads_out", [P, DC, T])
                with scope() as s2:
                    x = s2("normed", [P, DC, T])
                    norm(h, x, lambda c: vec("mix1", c), DC, 1e-6)
                    kc2 = s2("k_c", [P, NSA_GROUPS, T])
                    vc2 = s2("v_c", [P, NSA_GROUPS, T])
                    rel = s2("rel_bias", [REL_BUCKETS + 1, HEADS])
                    ext = s2("bias_by_distance", [HEADS, TOEP])
                    free, free_a, rel_in, rel_mm, rel_out, rel_stored, bias_in = semaphores("left", "left_a", "rel_in", "rel_mm", "rel_out", "rel_stored", "bias_in")
                    names = ("nsa_in", "nsa_v", "nsa_g")
                    c0 = ring.chunk0["nsa_in"]
                    with block() as b:
                        @b.sync
                        def _(sp):
                            sp.dma_start(rel[0:REL_BUCKETS, :], w["rel_bias"]).then_inc(rel_in, 16)
                            sp.dma_start(rel[REL_BUCKETS:REL_BUCKETS + 1, :], w["consts"][0:1, CONSTS["ones"][0]:CONSTS["ones"][0] + HEADS]).then_inc(rel_in, 16)
                            for name in names:
                                ring.loads(sp, name)

                        @b.gpsimd
                        def _(pool):
                            pool.wait_ge(rel_out, 1)
                            line = ext[:, :]
                            rows = bass.AP(line.tensor, T - 1 - P, [line.ap[0], [-1, P], [1, T]])
                            pool.dma_start(w["scratch"].rearrange("q h k -> h q k"), rows).then_inc(rel_stored, 16)
                            pool.wait_ge(rel_stored, 16)
                            pool.dma_start(bias[:, :, :], w["scratch"]).then_inc(bias_in, 16)
                            pool.wait_ge(bias_in, 16)

                        @b.tensor
                        def _(pe):
                            pe.wait_ge(rel_in, 32)
                            pe.matmul(bank[4][0:HEADS, 0:TOEP], rel[:, :], const("bucket")[0:REL_BUCKETS + 1, :],
                                      start=True, stop=True).then_inc(rel_mm, 1)
                            xk = lambda c: x[:, c, :]
                            pe_linear(pe, "nsa_in", xk, DC, 16, free)
                            pe_token_major(pe, "nsa_v", xk, DC, 2, 256, free, base=16)
                            pe_token_major(pe, "nsa_g", xk, DC, 1, 48, free, base=18)

                        @b.scalar
                        def _(act):
                            act.wait_ge(rel_mm, 1)
                            act.activation(ext[:, :], bank[4][0:HEADS, 0:TOEP], ACT.Copy).then_inc(rel_out, 1)
                            for j in range(8, 16):
                                act.wait_ge(mm_done, c0 + j + 1)
                                o = bank[j % 4]
                                kind, half = divmod(j - 8, 2)
                                dst = (kc2, vc2, k_s, k_w)[kind]
                                act.activation(dst[0:64, 2 * half, :], o[0:64, 0:T], ACT.Copy)
                                act.activation(dst[0:64, 2 * half + 1, :], o[64:128, 0:T], ACT.Copy).then_inc(free_a, 1)
                            act.wait_ge(mm_done, c0 + 19)
                            act.activation(gates[:, :, :], bank[18 % 4][:, 0:96].rearrange("p (t c) -> p t c", t=2),
                                           ACT.Sigmoid)

                        @b.vector
                        def _(dve):
                            for j in range(18):
                                dve.wait_ge(mm_done, c0 + j + 1)
                                o = bank[j % 4]
                                if j < 8:
                                    dve.tensor_scalar(qT[:, j, :], o[:, 0:T], 0.125, None, ALU.mult).then_inc(free, 1)
                                elif j < 16:
                                    kind, half = divmod(j - 8, 2)
                                    dst, shift = ((kc2, 1), (vc2, 1), (k_s, 0), (k_w, 0))[kind]
                                    dve.wait_ge(free_a, j - 7)
                                    dve.tensor_copy(dst[64:128, 2 * half, 0:T - shift], o[0:64, shift:T])
                                    dve.tensor_copy(dst[64:128, 2 * half + 1, 0:T - shift], o[64:128, shift:T]).then_inc(free, 1)
                                else:
                                    dve.tensor_copy((v_s, v_w)[j - 16][:, :, :], o[:, :].rearrange("p (t c) -> p t c", t=2)).then_inc(free, 1)
                    flat = s2("flat", [P, 2, 16, NSA_GROUPS * N_CMP])
                    hid = s2("cmp_hidden", [P, 2, NSA_GROUPS * N_CMP])
                    kcm = s2("k_cmp", [P, NSA_GROUPS * N_CMP])
                    pc = s2("probs_cmp", [P, HEADS * 2, N_CMP])
                    bc = s2("bias_cmp", [P, HEADS, 2, N_CMP])
                    mx = s2("max_cmp", [P, HEADS * 2])
                    sm = s2("sum_cmp", [P, HEADS * 2])
                    fl, hd_, cm, sc_, ex, tr, cp, d_step = semaphores("flat", "hidden", "cmp", "cmp_scores", "cmp_exp",
                                                                      "cmp_turned", "cmp_copied", "cmp_step")
                    c1 = ring.chunk0["nsa_w1"]
                    with block() as b:
                        @b.sync
                        def _(sp):
                            ring.loads(sp, "nsa_w1")
                            ring.loads(sp, "nsa_w2")

                        @b.tensor
                        def _(pe):
                            for i in range(2):
                                n = ring.first["nsa_w1"] + i
                                ring.arrived(pe, n)
                                pe.wait_ge(fl, i + 1)
                                for c in range(16):
                                    last = pe.matmul(bank[i][:, 0:60], ring.tile(n, c), flat[:, i, c, :], start=c == 0, stop=c == 15)
                                last.then_inc(mm_done, 1)
                            n = ring.first["nsa_w2"]
                            ring.arrived(pe, n)
                            pe.wait_ge(hd_, 2)
                            pe.matmul(bank[2][:, 0:60], ring.tile(n, 0), hid[:, 0, :], start=True, stop=True).then_inc(mm_done, 1)
                            for g in range(NSA_GROUPS):
                                last = pe.matmul(bank[3][0:N_CMP, g * 64:g * 64 + 64], hid[:, 1, g * N_CMP:(g + 1) * N_CMP],
                                                 ring.tile(n, 1, 64), start=True, stop=True)
                            last.then_inc(mm_done, 1)
                            pe.wait_ge(cm, 1)
                            for hd in range(HEADS):
                                r, g = 64 * (hd % 2), hd // 4
                                for q in range(2):
                                    at = (hd // 2 * 2 + q) * N_CMP
                                    last = pe.matmul(bank[4 + hd % 2][:, at:at + N_CMP],
                                                     qT[r:r + 64, hd // 2, q * P:(q + 1) * P],
                                                     kcm[r:r + 64, g * N_CMP:(g + 1) * N_CMP], start=True, stop=True)
                            last.then_inc(sc_, 1)
                            pe.wait_ge(ex, 2)
                            for pair in range(8):
                                if pair >= 4:
                                    pe.wait_ge(cp, pair - 3)
                                for i in range(4):
                                    last = pe.transpose(bank[pair % 4][0:N_CMP, i * P:(i + 1) * P], pc[:, 4 * pair + i, :], ident)
                                last.then_inc(tr, 1)

                        @b.scalar
                        def _(act):
                            for i in range(2):
                                act.wait_ge(mm_done, c1 + i + 1)
                                act.activation(hid[:, i, :], bank[i][:, 0:60], ACT.Gelu_apprx_tanh).then_inc(hd_, 1)
                            act.wait_ge(mm_done, c1 + 3)
                            act.activation(kcm[:, :], bank[2][:, 0:60], ACT.Copy).then_inc(cm, 1)
                            act.wait_ge(mm_done, c1 + 4)
                            act.activation(vcm[:, :, :], bank[3][0:N_CMP, 0:256].rearrange("p (g c) -> p g c", g=4), ACT.Copy)
                            act.wait_ge(sc_, 2)
                            act.activation(pc[:, :, :], pc[:, :, :], ACT.Exp).then_inc(ex, 1)
                            for pair in range(8):
                                act.wait_ge(tr, pair + 1)
                                act.activation(pTc[:, 2 * pair:2 * pair + 2, :],
                                               bank[pair % 4][0:N_CMP, :].rearrange("p (h t) -> p h t", h=2), ACT.Copy).then_inc(cp, 1)

                        @b.vector
                        def _(dve):
                            steps = Steps(d_step)
                            for i, (src, pos) in enumerate(((kc2, "pos_k"), (vc2, "pos_v"))):
                                a = src[:, :, :]
                                at, _ = VECS[pos]
                                v0 = vecs[:, at:at + 1]
                                view = bass.AP(a.tensor, a.offset, [a.ap[0], [2, 16], [T, NSA_GROUPS], [CMP_STRIDE, N_CMP]])
                                pos_view = bass.AP(v0.tensor, v0.offset, [v0.ap[0], [1, 16], [0, NSA_GROUPS], [0, N_CMP]])
                                dve.tensor_tensor(flat[:, i, :, :].rearrange("p c (g n) -> p c g n", g=NSA_GROUPS), view, pos_view,
                                                  ALU.add).then_inc(fl, 1)
                            late, early = P * 0 + CMP_BLOCK - 1, P + CMP_BLOCK - 1
                            steps.step(dve, dve.memset(bc[:, :, 0, :], NEG))
                            steps.step(dve, dve.tensor_copy(bc[:, :, 0, 0:N_CMP0], bias[:, :, early:early + CMP_STRIDE * (N_CMP0 - 1) + 1:CMP_STRIDE]))
                            steps.step(dve, dve.tensor_copy(bc[:, :, 1, :], bias[:, :, late:late + CMP_STRIDE * (N_CMP - 1) + 1:CMP_STRIDE]))
                            dve.wait_ge(sc_, 1)
                            rows = lambda t: t[:, :].rearrange("p (a b) -> p a b", b=1).to_broadcast([P, HEADS * 2, N_CMP])
                            for par in range(2):
                                odd = lambda t: t.rearrange("p (a o b) n -> p a o (b n)", o=2, b=2)[:, :, par, :]
                                steps.step(dve, dve.tensor_tensor(
                                    odd(pc[:, :, :]), bank[4 + par][:, 0:HEADS * N_CMP].rearrange("p (a n) -> p a n", a=8),
                                    odd(bc[:, :, :, :].rearrange("p h q n -> p (h q) n")), ALU.add))
                            steps.step(dve, dve.tensor_reduce(mx[:, :], pc[:, :, :], AX.X, ALU.max))
                            dve.tensor_tensor(pc[:, :, :], pc[:, :, :], rows(mx), ALU.subtract).then_inc(sc_, 1)
                            dve.wait_ge(ex, 1)
                            steps.step(dve, dve.tensor_reduce(sm[:, :], pc[:, :, :], AX.X, ALU.add))
                            steps.step(dve, dve.reciprocal(sm[:, :], sm[:, :]))
                            steps.step(dve, dve.tensor_tensor(sm[:, :].rearrange("p (h q) -> p h q", q=2), sm[:, :].rearrange("p (h q) -> p h q", q=2),
                                                              gates[:, :, 0:48:3].rearrange("p q h -> p h q"), ALU.mult))
                            vv = const("valid")
                            ok = bass.AP(vv.tensor, vv.offset, [vv.ap[0], [0, HEADS], [N_CMP, 2], [1, N_CMP]])
                            steps.step(dve, dve.tensor_tensor(pc[:, :, :].rearrange("p (h q) n -> p h q n", q=2), pc[:, :, :].rearrange("p (h q) n -> p h q n", q=2), ok, ALU.mult))
                            dve.tensor_tensor(pc[:, :, :], pc[:, :, :], rows(sm), ALU.mult).then_inc(ex, 1)
                jobs = []
                for hd in range(HEADS):
                    c, r, g = hd // 2, 64 * (hd % 2), hd // 4
                    for i, (kk, vv) in enumerate(((k_s, v_s), (k_w, v_w))):
                        gate = gates[:, :, 3 * hd + 1 + i]
                        jobs.append(dict(
                            scores=[(qT[r:r + 64, c, :], kk[r:r + 64, g, :])], add=bias[:, hd, :],
                            coef=gates[:, ::-1, 3 * hd + 1 + i], first=i == 0, last=i == 1, evict=i == 1 and hd % 2 == 1,
                            extra=(vcm[:, g, :], pTc[:, hd, :]),
                            outs=[(c, r, 64, lambda kb, vv=vv, g=g: vv[:, kb, g * 64:g * 64 + 64])]))
                attention(jobs, oT, 8)
                linear_stage("nsa_o", oT, DC, DC, add_to_h)

        def two_branches():
            with scope() as s:
                x = s("normed", [P, DC, T])
                norm(h, x, lambda c: vec("mix_pre", c), DC, 1e-6)
                mixed = s("mixed", [P, DC, T])
                gate = s("gate", [P, 2 * DC, T])
                with scope() as s2:
                    qk = s2("qk", [P, 16, T])
                    v = s2("v", [P, 2, D])
                    neg_lam = s2("neg_lambda", [P, 2])
                    prod = s2("lambda_products", [64, 2])
                    ex = s2("lambda_exps", [P, 2])
                    linear_stage("da_qk", x, DC, 16, lambda dve, j, o: dve.tensor_scalar(
                        qk[:, j, :], o, 0.125 if j < 8 else 1.0, None, ALU.mult))
                    token_major_stage("da_v", x, DC, 4, lambda dve, j, o: dve.tensor_copy(v[:, :, j * 256:(j + 1) * 256], o))
                    lam, d_step = semaphores("lambda", "lam_step")
                    with block() as b:
                        @b.vector
                        def _(dve):
                            steps = Steps(d_step)
                            at, _ = VECS["lam"]
                            dve.tensor_tensor(prod[:, :], vecs[0:64, at:at + 4:2], vecs[0:64, at + 1:at + 4:2], ALU.mult).then_inc(lam, 1)
                            dve.wait_ge(lam, 3)
                            for i in range(2):
                                steps.step(dve, dve.tensor_tensor(neg_lam[:, i:i + 1], ex[:, 1:2], ex[:, 0:1], ALU.subtract))
                            dve.tensor_scalar(neg_lam[:, :], neg_lam[:, :], LAM_INIT, None, ALU.subtract)

                        @b.tensor
                        def _(pe):
                            pe.wait_ge(lam, 1)
                            pe.matmul(bank[0][:, 0:2], ones[0:64, :], prod[:, :], start=True, stop=True).then_inc(lam, 1)

                        @b.scalar
                        def _(act):
                            act.wait_ge(lam, 2)
                            act.activation(ex[:, :], bank[0][:, 0:2], ACT.Exp).then_inc(lam, 1)
                    oT = s2("heads_out", [P, DC, T])
                    jobs = []
                    for hd in range(DA_HEADS):
                        for i in range(2):
                            r = 64 * i
                            jobs.append(dict(
                                scores=[(qk[r:r + 64, hd, :], qk[r:r + 64, 8 + hd, :])], add=const("mask"),
                                coef=neg_lam[:, :] if i else None, first=i == 0, last=i == 1, evict=i == 1,
                                outs=[(hd, 0, P, lambda kb, hd=hd: v[:, kb, hd * P:(hd + 1) * P])]))
                    attention(jobs, oT, 8)
                    on = s2("subln_out", [P, DC, T])
                    g_sub = s2("subln_gain", [P, 1])
                    with block() as b:
                        @b.vector
                        def _(dve):
                            dve.tensor_scalar(g_sub[:, :], vec("subln"), 1.0 - LAM_INIT, None, ALU.mult)
                    norm(oT, on, lambda c: g_sub[:, :], 1, 1e-5, groups=8)
                    free, = semaphores("left")
                    with block() as b:
                        @b.sync
                        def _(sp):
                            ring.loads(sp, "gate")

                        @b.tensor
                        def _(pe):
                            pe_linear(pe, "gate", lambda c: x[:, c, :], DC, 16, free)

                        @b.scalar
                        def _(act):
                            for j in range(16):
                                act.wait_ge(mm_done, ring.chunk0["gate"] + j + 1)
                                act.activation(gate[:, j, :], bank[j % 4][:, 0:T], ACT.Sigmoid, bias=vec("b_gate", j)).then_inc(free, 1)
                    linear_stage("br_attn", on, DC, DC, lambda dve, j, o: dve.tensor_tensor(mixed[:, j, :], o, gate[:, j, :], ALU.mult))
                if done("attn_branch"):
                    return mixed
                z = s("z", [P, SC, T])
                y = s("y", [P, SC, T])
                ssd(x, z, y)
                with block() as b:
                    @b.vector
                    def _(dve):
                        for c in range(SC):
                            dve.tensor_tensor(y[:, c, :], y[:, c, :], z[:, c, :], ALU.mult)
                norm(y, z, lambda c: vec("ssd_g", c), SC // SSD_GROUPS, 1e-5, groups=SSD_GROUPS)
                tmp = s("tmp", [P, T])
                d_step, free = semaphores("mix_step", "left")
                with block() as b:
                    @b.sync
                    def _(sp):
                        ring.loads(sp, "br_ssd")

                    @b.tensor
                    def _(pe):
                        pe_linear(pe, "br_ssd", lambda c: z[:, c, :], SC, DC, free)

                    @b.vector
                    def _(dve):
                        steps = Steps(d_step)
                        for j in range(DC):
                            dve.wait_ge(mm_done, ring.chunk0["br_ssd"] + j + 1)
                            steps.step(dve, dve.tensor_tensor(tmp[:, :], bank[j % 4][:, 0:T], gate[:, DC + j, :], ALU.mult))
                            dve.tensor_tensor(mixed[:, j, :], mixed[:, j, :], tmp[:, :], ALU.add).then_inc(free, 1)
                            dve.wait_ge(free, j + 1)
                linear_stage("mix_out", mixed, DC, DC, lambda dve, j, o: dve.tensor_copy(x[:, j, :], o))
                norm(x, h, lambda c: vec("mix_post", c), DC, 1e-6, residual=1.0)

        def ssd(x, z, y):
            with scope() as s:
                xs = s("xs", [P, SC, T])
                bcT = s("b_and_c", [P, 2 * SSD_GROUPS, T])
                free, = semaphores("left")
                with block() as b:
                    @b.sync
                    def _(sp):
                        ring.loads(sp, "z")

                    @b.tensor
                    def _(pe):
                        pe_linear(pe, "z", lambda c: x[:, c, :], DC, SC, free)

                    @b.scalar
                    def _(act):
                        for j in range(SC):
                            act.wait_ge(mm_done, ring.chunk0["z"] + j + 1)
                            act.activation(z[:, j, :], bank[j % 4][:, 0:T], ACT.Silu).then_inc(free, 1)
                dt_raw = s("dt_raw", [P, 2, SSD_HEADS])
                with scope() as s2:
                    padded = s2("padded", [P, 2, CONV - 1 + T])
                    acc = s2("conv", [P, 2, T])
                    pad, free, conv, fin, d_step = semaphores("pad", "left", "conv", "conv_out", "conv_step")
                    c0 = ring.chunk0["xbc"]
                    with block() as b:
                        @b.sync
                        def _(sp):
                            ring.loads(sp, "xbc")
                            ring.loads(sp, "dt")

                        @b.gpsimd
                        def _(pool):
                            pool.memset(padded[:, :, :], 0.0).then_inc(pad, 1)

                        @b.tensor
                        def _(pe):
                            pe_linear(pe, "xbc", lambda c: x[:, c, :], DC, XBC, free)
                            pe_token_major(pe, "dt", lambda c: x[:, c, :], DC, 1, SSD_HEADS, free, base=XBC)

                        @b.scalar
                        def _(act):
                            act.wait_ge(pad, 1)
                            for j in range(XBC + 1):
                                if j < XBC:
                                    act.wait_ge(mm_done, c0 + j + 1)
                                    if j >= 2:
                                        act.wait_ge(conv, j - 1)
                                    act.activation(padded[:, j % 2, CONV - 1:], bank[j % 4][:, 0:T], ACT.Copy).then_inc(free, 1)
                                if j >= 1:
                                    i = j - 1
                                    act.wait_ge(conv, i + 1)
                                    dst = xs[:, i, :] if i < SC else bcT[:, i - SC, :]
                                    act.activation(dst, acc[:, i % 2, :], ACT.Silu).then_inc(fin, 1)
                            act.wait_ge(mm_done, c0 + XBC + 1)
                            act.activation(dt_raw[:, :, :], bank[XBC % 4][:, 0:2 * SSD_HEADS].rearrange("p (t c) -> p t c", t=2), ACT.Copy)

                        @b.vector
                        def _(dve):
                            steps = Steps(d_step)
                            for j in range(XBC):
                                dve.wait_ge(free, j + 1)
                                if j >= 2:
                                    dve.wait_ge(fin, j - 1)
                                a = acc[:, j % 2, :]
                                for i in range(CONV):
                                    u = padded[:, j % 2, i:i + T]
                                    wi = vec("conv_w", j * CONV + i)
                                    if i == 0:
                                        steps.step(dve, dve.tensor_scalar(a, u, wi, vec("conv_b", j), ALU.mult, ALU.add))
                                    else:
                                        last = dve.scalar_tensor_tensor(out=a, in0=u, scalar=wi, in1=a, op0=ALU.mult, op1=ALU.add)
                                        if i < CONV - 1:
                                            steps.step(dve, last)
                                last.then_inc(conv, 1)
                H = SSD_HEADS
                xt = s("x_tokens", [P, 2, SSD_INNER])
                bt = s("b_tokens", [P, SSD_GROUPS, P])
                dt = s("dt", [P, 2, H])
                adt = s("a_dt", [P, 2, H])
                neg_cs = s("neg_cumsum", [P, 2, H])
                decay = s("decay", [P, H])
                cbm = s("masked_cb", [P, 2, SSD_GROUPS, P])
                st = s("states", [P, SSD_INNER])
                u = s("tmp", [P, 2, 2, H])
                a_neg = s("a", [P, H])
                step_a, step_d, dt_ok, cs_ok, tr, cp, cb_ok, stt = semaphores(
                    "ssd_a", "ssd_d", "dt_ok", "cs_ok", "x_turned", "x_copied", "cb_ok", "state")
                at_b, _ = VECS["dt_bias"]
                at_a, _ = VECS["A_log"]
                row = lambda at: bass.AP(vecs[:, at:at + H].tensor, vecs[:, at:at + H].offset, [vecs[:, at:at + H].ap[0], [0, 2], [1, H]])
                both = lambda t: bass.AP(t[:, :].tensor, t[:, :].offset, [t[:, :].ap[0], [0, 2], [1, H]])
                with block() as b:
                    @b.scalar
                    def _(act):
                        steps = Steps(step_a)
                        steps.step(act, act.activation(a_neg[:, :], vecs[:, at_a:at_a + H], ACT.Exp))
                        act.wait_ge(dt_ok, 1)
                        steps.step(act, act.activation(u[:, 1], u[:, 1], ACT.Exp))
                        act.activation(u[:, 1], u[:, 1], ACT.Ln, bias=1.0).then_inc(dt_ok, 1)
                        act.wait_ge(cs_ok, 2)
                        act.activation(decay[:, :], decay[:, :], ACT.Exp).then_inc(cs_ok, 1)

                    @b.vector
                    def _(dve):
                        steps = Steps(step_d)
                        steps.step(dve, dve.tensor_tensor(dt_raw[:, :, :], dt_raw[:, :, :], row(at_b), ALU.add))
                        steps.step(dve, dve.tensor_scalar(u[:, 0], dt_raw[:, :, :], -1.0, None, ALU.mult))
                        dve.tensor_tensor(u[:, 1], u[:, 0], dt_raw[:, :, :], ALU.min).then_inc(dt_ok, 1)
                        dve.wait_ge(dt_ok, 2)
                        steps.step(dve, dve.scalar_tensor_tensor(out=dt[:, :, :], in0=dt_raw[:, :, :], scalar=0.0, in1=u[:, 1],
                                                                 op0=ALU.max, op1=ALU.add))
                        dve.wait_ge(step_a, 1)
                        dve.scalar_tensor_tensor(out=adt[:, :, :], in0=dt[:, :, :], scalar=-1.0, in1=both(a_neg),
                                                 op0=ALU.mult, op1=ALU.mult).then_inc(dt_ok, 1)
                        dve.wait_ge(cs_ok, 1)
                        steps.step(dve, dve.tensor_scalar(neg_cs[:, :, :], bank[7][:, 0:2 * H].rearrange("p (t c) -> p t c", t=2), -1.0, None, ALU.mult))
                        dve.tensor_tensor(decay[:, :], bank[7][:, 2 * H:3 * H], neg_cs[:, 0, :], ALU.add).then_inc(cs_ok, 1)
                        dt_wide = dt[:, :, :].rearrange("p t (h o) -> p t h o", o=1)
                        for j in range(8):
                            t, c4 = divmod(j, 4)
                            dve.wait_ge(tr, j + 1)
                            dve.tensor_tensor(xt[:, t, c4 * 512:(c4 + 1) * 512].rearrange("p (h d) -> p h d", d=SSD_P),
                                              bank[j % 4][:, :].rearrange("p (h d) -> p h d", d=SSD_P),
                                              dt_wide[:, t, c4 * 8:(c4 + 1) * 8, :].to_broadcast([P, 8, SSD_P]), ALU.mult).then_inc(cp, 1)
                        dve.wait_ge(tr, 9)
                        dve.tensor_copy(bt[:, :, :], bank[4][:, :].rearrange("p (g c) -> p g c", g=4)).then_inc(cp, 1)
                        for t in range(2):
                            dve.wait_ge(cb_ok, t + 1)
                            tri_w = bass.AP(tri.tensor, tri.offset, [tri.ap[0], [0, SSD_GROUPS], [1, P]])
                            dve.tensor_tensor(cbm[:, t, :, :], bank[5 + t][:, :].rearrange("p (g c) -> p g c", g=4), tri_w, ALU.mult)
                        dve.wait_ge(cs_ok, 3)
                        dve.wait_ge(cp, 9)
                        dec = decay[:, :].rearrange("p (h o) -> p h o", o=1)
                        dve.tensor_tensor(st[:, :].rearrange("p (h d) -> p h d", d=SSD_P),
                                          xt[:, 0, :].rearrange("p (h d) -> p h d", d=SSD_P),
                                          dec.to_broadcast([P, H, SSD_P]), ALU.mult).then_inc(stt, 1)
                        for g in range(SSD_GROUPS):
                            dve.wait_ge(stt, 2 + g)
                            if g == 0:
                                dve.wait_ge(stt, 5)
                            dve.tensor_copy(st[:, g * 512:(g + 1) * 512], bank[g][:, :])

                    @b.tensor
                    def _(pe):
                        for j in range(8):
                            t, c4 = divmod(j, 4)
                            if j >= 4:
                                pe.wait_ge(cp, j - 3)
                            for i in range(4):
                                last = pe.transpose(bank[j % 4][:, i * P:(i + 1) * P], xs[:, 4 * c4 + i, t * P:(t + 1) * P], ident)
                            last.then_inc(tr, 1)
                            if j == 3:
                                pe.wait_ge(dt_ok, 3)
                                for t2 in range(2):
                                    pe.matmul(bank[7][:, t2 * H:(t2 + 1) * H], tri, adt[:, t2, :], start=True, stop=True)
                                pe.matmul(bank[7][:, 2 * H:3 * H], ones, adt[:, 0, :], start=True, stop=True).then_inc(cs_ok, 1)
                        for g in range(SSD_GROUPS):
                            last = pe.transpose(bank[4][:, g * P:(g + 1) * P], bcT[:, g, 0:P], ident)
                        last.then_inc(tr, 1)
                        for t in range(2):
                            for g in range(SSD_GROUPS):
                                last = pe.matmul(bank[5 + t][:, g * P:(g + 1) * P], bcT[:, g, t * P:(t + 1) * P],
                                                 bcT[:, SSD_GROUPS + g, t * P:(t + 1) * P], start=True, stop=True)
                            last.then_inc(cb_ok, 1)
                        pe.wait_ge(cp, 9)
                        pe.wait_ge(stt, 1)
                        for g in range(SSD_GROUPS):
                            pe.matmul(bank[g][:, :], bt[:, g, :], st[:, g * 512:(g + 1) * 512], start=True, stop=True).then_inc(stt, 1)
                Q = 4
                seg_ok, seg_min, l_ok, m_ok, y_ok, y_out, carry, step_d = semaphores(
                    "seg_ok", "seg_min", "l_ok", "m_ok", "y_ok", "y_out", "carry", "ssd_d2")
                seg = s("segments", [P, 2, 2, Q, P])
                cs1 = s("carried_c", [P, 2, Q, P])
                quads = H // Q
                with block() as b:
                    @b.tensor
                    def _(pe):
                        def sums(k):
                            if k >= 1:
                                pe.wait_ge(seg_min, 8 * k)
                                pe.wait_ge(carry, k)
                            for t in range(2):
                                for i in range(Q):
                                    a = adt[:, t, Q * k + i:Q * k + i + 1]
                                    col = bass.AP(a.tensor, a.offset, [a.ap[0], [0, P]])
                                    last = pe.matmul(bank[t][:, i * P:(i + 1) * P], col, tri, start=True, stop=True)
                            last.then_inc(seg_ok, 1)

                        def outputs(k):
                            pe.wait_ge(m_ok, 2 * (k + 1))
                            if k >= 2:
                                pe.wait_ge(y_out, 2 * (k - 1))
                            for i in range(Q):
                                hd = Q * k + i
                                r = 64 * (i % 2)
                                o = bank[4 + 2 * (k % 2) + i // 2]
                                cols = slice(hd * SSD_P, (hd + 1) * SSD_P)
                                pe.matmul(o[r:r + 64, 0:P], xt[:, 0, cols], seg[:, k % 2, 0, i, :], start=True, stop=True)
                                pe.matmul(o[r:r + 64, P:T], xt[:, 1, cols], seg[:, k % 2, 1, i, :], start=True, stop=False)
                                last = pe.matmul(o[r:r + 64, P:T], st[:, cols], cs1[:, k % 2, i, :], start=False, stop=True)
                            last.then_inc(y_ok, 1)

                        for k in range(quads + 1):
                            if k < quads:
                                sums(k)
                            if k >= 1:
                                outputs(k - 1)

                    @b.vector
                    def _(dve):
                        steps = Steps(step_d)

                        def minus(k):
                            dve.wait_ge(seg_ok, k + 1)
                            if k >= 2:
                                dve.wait_ge(y_ok, k - 1)
                            for t in range(2):
                                if t == 1:
                                    dve.wait_ge(carry, k + 1)
                                for i in range(Q):
                                    hd = Q * k + i
                                    dve.tensor_scalar(seg[:, k % 2, t, i, :], bank[t][:, i * P:(i + 1) * P],
                                                      neg_cs[:, t, hd:hd + 1], 0.0, ALU.add, ALU.min).then_inc(seg_min, 1)

                        def times(k):
                            dve.wait_ge(l_ok, k + 1)
                            g = k // 2
                            for t in range(2):
                                cb = cbm[:, t, g, :]
                                wide = bass.AP(cb.tensor, cb.offset, [cb.ap[0], [0, Q], [1, P]])
                                last = dve.tensor_tensor(seg[:, k % 2, t, :, :], seg[:, k % 2, t, :, :], wide, ALU.mult)
                            last.then_inc(m_ok, 1)
                            c = bcT[:, SSD_GROUPS + g, P:T]
                            wide = bass.AP(c.tensor, c.offset, [c.ap[0], [0, Q], [1, P]])
                            dve.wait_ge(carry, k + 1)
                            dve.tensor_tensor(cs1[:, k % 2, :, :], cs1[:, k % 2, :, :], wide, ALU.mult).then_inc(m_ok, 1)

                        def leave(k):
                            dve.wait_ge(y_ok, k + 1)
                            for i in range(2):
                                c = 2 * k + i
                                dve.scalar_tensor_tensor(out=y[:, c, :], in0=xs[:, c, :], scalar=vec("ssd_D", c),
                                                         in1=bank[4 + 2 * (k % 2) + i][:, 0:T], op0=ALU.mult,
                                                         op1=ALU.add).then_inc(y_out, 1)

                        for k in range(quads + 2):
                            if k < quads:
                                minus(k)
                            if 0 <= k - 1 < quads:
                                times(k - 1)
                            if 0 <= k - 2 < quads:
                                leave(k - 2)

                    @b.scalar
                    def _(act):
                        for k in range(quads):
                            act.wait_ge(seg_ok, k + 1)
                            if k >= 2:
                                act.wait_ge(y_ok, k - 1)
                            act.activation(cs1[:, k % 2, :, :], bank[1][:, :].rearrange("p (i c) -> p i c", i=Q), ACT.Exp).then_inc(carry, 1)
                            act.wait_ge(seg_min, 8 * (k + 1))
                            act.activation(seg[:, k % 2, :, :, :], seg[:, k % 2, :, :, :], ACT.Exp).then_inc(l_ok, 1)

        def cross_attention():
            with scope() as s:
                x = s("normed", [P, DC, T])
                mem = s("memory", [P, DC, T])
                mn = s("memory_normed", [P, DC, T])
                q = s("q", [P, DC, T])
                k = s("k", [P, DC, T])
                v = s("v", [P, 2, D])
                oT = s("heads_out", [P, DC, T])
                m_in, = semaphores("memory_in")
                with block() as b:
                    @b.sync
                    def _(sp):
                        sp.dma_start(mem[:, :, :], w["memT"]).then_inc(m_in, 16)
                        sp.wait_ge(m_in, 16)
                norm(mem, mn, lambda c: vec("mem", c), DC, 1e-6)
                norm(h, x, lambda c: vec("xa_pre", c), DC, 1e-6)
                linear_stage("xa_q", x, DC, DC, lambda dve, j, o: dve.tensor_scalar(q[:, j, :], o, 1 / 16, None, ALU.mult))
                linear_stage("xa_k", mn, DC, DC, lambda dve, j, o: dve.tensor_copy(k[:, j, :], o))
                token_major_stage("xa_v", mn, DC, 4, lambda dve, j, o: dve.tensor_copy(v[:, :, j * 256:(j + 1) * 256], o))
                jobs = []
                for hd in range(XA_HEADS):
                    jobs.append(dict(
                        scores=[(q[:, 2 * hd + i, :], k[:, 2 * hd + i, :]) for i in range(2)], add=None,
                        first=True, last=True, evict=True,
                        outs=[(2 * hd + i, 0, P, lambda kb, c=2 * hd + i: v[:, kb, c * P:(c + 1) * P]) for i in range(2)]))
                attention(jobs, oT, 8, causal=False)
                linear_stage("xa_o", oT, DC, DC, lambda dve, j, o: dve.tensor_copy(x[:, j, :], o))
                norm(x, h, lambda c: vec("xa_post", c), DC, 1e-6, residual=1.0)

        steps_list = [
            ("ffn_a0", lambda: full_ffn("ffn_a0", "ffn_a0")),
            ("mla", mla),
            ("ffn_b0", lambda: full_ffn("ffn_b0", "ffn_b0")),
            ("ffn_a1", lambda: full_ffn("ffn_a1", "ffn_a1")),
            ("nsa", nsa),
            ("ffn_b1", lambda: full_ffn("ffn_b1", "ffn_b1")),
            ("final", lambda: norm(h, h, lambda c: vec("final", c), DC, 1e-6)),
            ("ffn1", lambda: full_ffn("ffn1", "ffn1_pre", post="ffn1_post")),
            ("mix", two_branches),
            ("xa", cross_attention),
            ("ffn2", lambda: full_ffn("ffn2", "ffn2_pre", post="ffn2_post")),
        ]
        for name, f in steps_list:
            f()
            if done(name):
                break
            if name in ("ffn_a1", "final", "ffn1", "mix"):
                recycle()
        stored, = semaphores("stored")
        with block() as b:
            @b.sync
            def _(sp):
                sp.dma_start(out, h[:, :, :]).then_inc(stored, 16)
                sp.wait_ge(stored, 16)




def kernel(**inputs):
    import concourse.bacc as bacc
    from concourse.bass_utils import run_bass_kernel_spmd

    nc = bacc.Bacc("TRN2", target_bir_lowering=False, num_devices=1)
    arrays = lay_out({k: np.asarray(v) for k, v in inputs.items()})
    w = {n: nc.dram_tensor(f"in_{n}", a.shape, mybir.dt.from_np(a.dtype), kind="ExternalInput").ap() for n, a in arrays.items()}
    w["scratch"] = nc.dram_tensor("bias_rows", [P, HEADS, T], F32, kind="Internal").ap()
    out = nc.dram_tensor("out_dram", (P, DC, T), F32, kind="ExternalOutput").ap()
    emit(nc, w, out)
    r = run_bass_kernel_spmd(nc, [{f"in_{n}": a for n, a in arrays.items()}], core_ids=[0])
    got = r.results[0]["out_dram"]
    return np.ascontiguousarray(got.transpose(2, 1, 0)).reshape(1, T, D)
```

```python
from contextlib import ExitStack, contextmanager

import numpy as np
import concourse.bass as bass
from concourse import mybir

F32 = mybir.dt.float32
F32R = mybir.dt.float32r
ACT = mybir.ActivationFunctionType
ALU = mybir.AluOpType
AX = mybir.AxisListType

P = 128
T = 256
D = 1024
DC = D // P
FF = 2816
FC = FF // P
HEADS = 16
NEG = -1e30
RAW = 3
CUT = 3
SLOT_TILES = 16
HALF = FC // 2
MLA_Q, MLA_KV, MLA_NOPE, MLA_ROPE, MLA_V = 384, 256, 64, 32, 64
NSA_GROUPS, CMP_BLOCK, CMP_STRIDE = 4, 32, 16
N_CMP = (T - CMP_BLOCK) // CMP_STRIDE + 1
N_CMP0 = (P - CMP_BLOCK) // CMP_STRIDE + 1
REL_BUCKETS, REL_MAX_DIST = 32, 128
TOEP = 2 * T - P - 1
DA_HEADS = 8
SSD_HEADS, SSD_GROUPS, SSD_INNER = 32, 4, 2048
SSD_P = SSD_INNER // SSD_HEADS
SC = SSD_INNER // P
XBC = (SSD_INNER + 2 * SSD_GROUPS * P) // P
CONV = 4
XA_HEADS = 4
LAM_INIT = 0.8 - 0.6
NSA_QK, DA_QK, XA_HEAD_DIM = 64, 64, D // XA_HEADS



def plan():
    ffn = lambda n: [(n + "_gu", FC, 2 * DC, 1), (n + "_dn", 2 * DC, HALF, 1)]
    return (
        ffn("ffn_a0") + [("mla_in", 7, 8, 1), ("mla_uq", 4, 12, 4), ("mla_uk", 1, 16, 8), ("mla_uv", 1, 16, 4),
                         ("mla_o", 4, 16, 2)]
        + ffn("ffn_b0") + ffn("ffn_a1")
        + [("nsa_in", 8, 16, 2), ("nsa_v", 2, 16, 1), ("nsa_g", 1, 3, 1), ("nsa_o", 4, 16, 2)]
        + ffn("ffn_b1") + ffn("ffn1")
        + [("da_qk", 8, 16, 2), ("da_v", 4, 16, 1), ("gate_a", 4, 16, 2), ("br_attn", 4, 16, 2),
           ("xbc", 12, 16, 2), ("dt", 1, 2, 1), ("z", 8, 16, 2), ("gate_s", 4, 16, 2), ("br_ssd", 8, 16, 1), ("mix_out", 4, 16, 2),
           ("xa_q", 4, 16, 2), ("xa_k", 4, 16, 2), ("xa_v", 4, 16, 1), ("xa_o", 4, 16, 2)]
        + ffn("ffn2"))


VECS = {}


def vec_layout():
    at = 0
    for name, n in (("ffn_a0", 8), ("mix0", 8), ("ffn_b0", 8), ("ffn_a1", 8), ("mix1", 8), ("ffn_b1", 8), ("final", 8),
                    ("cq", 3), ("ckv", 2), ("pos_k", 16), ("pos_v", 16),
                    ("ffn1_pre", 8), ("ffn1_post", 8), ("mix_pre", 8), ("mix_post", 8), ("b_gate", 16), ("subln", 1),
                    ("conv_w", XBC * CONV), ("conv_b", XBC), ("ssd_D", SC), ("ssd_g", SC),
                    ("xa_pre", 8), ("xa_post", 8), ("mem", 8), ("ffn2_pre", 8), ("ffn2_post", 8),
                    ("dt_bias", 32), ("A_log", 32), ("lam", 4)):
        VECS[name] = (at, n)
        at += n
    return at


N_VEC = vec_layout()
CONSTS = {}


def const_layout():
    at = 0
    for name, n in (("ident", P), ("ones", P), ("tri", P), ("mask", T), ("cos", T), ("sin", T), ("valid", 2 * N_CMP),
                    ("bucket", TOEP)):
        CONSTS[name] = (at, n)
        at += n
    return at


N_CONST = const_layout()


def shape_constants():
    c = np.zeros((P, N_CONST), np.float32)

    def put(name, a):
        at, n = CONSTS[name]
        c[:a.shape[0], at:at + n] = a

    p = np.arange(P)
    put("ident", np.eye(P))
    put("ones", np.ones((P, P)))
    put("tri", p[:, None] <= p[None, :])
    put("mask", np.where(np.arange(T)[None, :] > P + p[:, None], NEG, 0.0))
    half = MLA_ROPE // 2
    inv = np.float32(10000.0) ** (-np.arange(half, dtype=np.float32) * np.float32(2.0 / MLA_ROPE))
    ang = np.arange(T, dtype=np.float32)[:, None] * inv[None, :]
    row = p % half
    sign = np.where(p % MLA_ROPE < half, -1.0, 1.0)[:, None]
    put("cos", np.cos(ang).T[row])
    put("sin", np.sin(ang).T[row] * sign)
    ends = np.arange(N_CMP) * CMP_STRIDE + CMP_BLOCK - 1
    valid = [(q0 + p[:, None] >= ends[None, :]) for q0 in (0, P)]
    put("valid", np.concatenate(valid, axis=1))
    dist = T - 1 - np.arange(TOEP)
    n = np.maximum(dist, 0)
    exact = REL_BUCKETS // 2
    large = exact + (np.log(np.maximum(n, 1).astype(np.float32) / np.float32(exact)) / np.float32(np.log(REL_MAX_DIST / exact))
                     * np.float32(REL_BUCKETS - exact)).astype(np.int32)
    bucket = np.where(n < exact, n, np.minimum(large, REL_BUCKETS - 1))
    hot = np.zeros((REL_BUCKETS + 1, TOEP))
    hot[:REL_BUCKETS] = (bucket[None, :] == np.arange(REL_BUCKETS)[:, None]) & (dist >= 0)
    hot[REL_BUCKETS] = np.where(dist < 0, NEG, 0.0)
    put("bucket", hot)
    return c


def m_major(w, per_block):
    k, m = w.shape[0] // P, w.shape[1] // P
    t = w.reshape(k, P, m // per_block, per_block, P).transpose(2, 1, 3, 0, 4)
    return np.ascontiguousarray(t).reshape(m // per_block, P, per_block * k * P)


def k_major(w, cols):
    k, n = w.shape[0] // P, w.shape[1] // cols
    t = w.reshape(k, P, n, cols).transpose(2, 1, 0, 3)
    return np.ascontiguousarray(t).reshape(n, P, k * cols)


def lay_out(x):
    a = {}

    def ffn(name, g, u, d):
        gu = np.concatenate([g.reshape(D, FC, 1, P), u.reshape(D, FC, 1, P)], axis=2).reshape(D, 2 * FF)
        a[name + "_gu"] = m_major(gu, 2)
        a[name + "_dn"] = np.ascontiguousarray(m_major(d, 1).reshape(DC, P, 2, HALF * P).transpose(0, 2, 1, 3)).reshape(
            2 * DC, P, HALF * P)

    for l in range(2):
        for s in "ab":
            ffn(f"ffn_{s}{l}", x[f"ffn_{s}_w_gate"][l], x[f"ffn_{s}_w_up"][l], x[f"ffn_{s}_w_down"][l])
    for n in ("1", "2"):
        gu = x[f"ffn{n}_w_gu_2"][0]
        ffn(f"ffn{n}", gu[:, :FF], gu[:, FF:], x[f"ffn{n}_w_down_2"][0])
    half = MLA_ROPE // 2
    turned = lambda w: np.concatenate([w[..., half:], w[..., :half]], axis=-1)
    w = x["mla_w_in"][0]
    kr = w[:, MLA_Q + MLA_KV:]
    w = np.concatenate([w[:, :MLA_Q + MLA_KV]] + [kr] * 4 + [turned(kr)] * 4, axis=1)
    a["mla_in"] = m_major(w, 1)
    w = x["mla_w_uq"][0].reshape(MLA_Q, HEADS, MLA_NOPE + MLA_ROPE)
    rope = w[:, :, MLA_NOPE:]
    both = np.concatenate([rope.reshape(MLA_Q, 4, 1, P), turned(rope).reshape(MLA_Q, 4, 1, P)], axis=2)
    w = np.concatenate([w[:, :, :MLA_NOPE].reshape(MLA_Q, -1), both.reshape(MLA_Q, -1)], axis=1)
    a["mla_uq"] = m_major(w, 4)
    w = x["mla_w_ukv"][0].reshape(MLA_KV, HEADS, MLA_NOPE + MLA_V)
    a["mla_uk"] = m_major(w[:, :, :MLA_NOPE].reshape(MLA_KV, -1), 8)
    a["mla_uv"] = k_major(w[:, :, MLA_NOPE:].reshape(MLA_KV, -1), D)
    a["mla_o"] = m_major(x["mla_w_o"][0], 2)
    w = x["nsa_w_in"][0]
    q, kc, vc, ks, vs, kw, vw, g = np.split(w, np.cumsum([D] + [256] * 6), axis=1)
    a["nsa_in"] = m_major(np.concatenate([q, kc, vc, ks, kw], axis=1), 2)
    a["nsa_v"] = k_major(np.concatenate([vs, vw], axis=1), 256)
    a["nsa_g"] = k_major(g, 48)
    a["nsa_w1"] = np.concatenate([k_major(x["nsa_cmp_w1_k"][0], P), k_major(x["nsa_cmp_w1_v"][0], P)])
    w2k, w2v = x["nsa_cmp_w2_k"][0], x["nsa_cmp_w2_v"][0]
    a["nsa_w2"] = np.concatenate([w2k, w2k, w2v, w2v], axis=1)
    a["nsa_o"] = m_major(x["nsa_w_o"][0], 2)
    w = x["w_in_2"][0]
    q, k, v, z, xbc, dt, gate = np.split(w, np.cumsum([D, D, D, SSD_INNER, XBC * P, SSD_HEADS]), axis=1)
    a["da_qk"] = m_major(np.concatenate([q, k], axis=1), 2)
    a["da_v"] = k_major(v, 256)
    a["gate_a"] = m_major(gate[:, :D], 2)
    a["gate_s"] = m_major(gate[:, D:], 2)
    a["z"] = m_major(z, 2)
    a["xbc"] = m_major(xbc, 2)
    a["dt"] = k_major(dt, SSD_HEADS)
    a["br_attn"] = m_major(x["w_branch_attn_2"][0], 2)
    a["br_ssd"] = m_major(x["w_branch_ssd_2"][0], 1)
    a["mix_out"] = m_major(x["w_mix_out_2"][0], 2)
    a["xa_q"] = m_major(x["xa_w_q_2"][0], 2)
    kv = x["xa_w_kv_2"][0]
    a["xa_k"] = m_major(kv[:, :D], 2)
    a["xa_v"] = k_major(kv[:, D:], 256)
    a["xa_o"] = m_major(x["xa_w_o_2"][0], 2)

    cols = lambda v: v.reshape(-1, P).T
    wide = lambda v: np.broadcast_to(v, (P, v.shape[-1]))
    vec = {
        "ffn_a0": cols(x["ffn_norm_a"][0]), "ffn_a1": cols(x["ffn_norm_a"][1]),
        "mix0": cols(x["mix_norm"][0]), "mix1": cols(x["mix_norm"][1]),
        "ffn_b0": cols(x["ffn_norm_b"][0]), "ffn_b1": cols(x["ffn_norm_b"][1]),
        "final": cols(x["final_norm"]), "cq": cols(x["mla_q_norm"]), "ckv": cols(x["mla_kv_norm"]),
        "pos_k": cols(x["nsa_cmp_pos_k"]), "pos_v": cols(x["nsa_cmp_pos_v"]),
        "ffn1_pre": cols(x["ffn1_pre_g_2"]), "ffn1_post": cols(x["ffn1_post_g_2"]),
        "mix_pre": cols(x["mix_pre_g_2"]), "mix_post": cols(x["mix_post_g_2"]),
        "b_gate": cols(x["b_gate_2"]), "subln": cols(x["da_subln_g_2"]),
        "conv_w": x["ssd_conv_w_2"][0].reshape(CONV, XBC, P).transpose(2, 1, 0).reshape(P, -1),
        "conv_b": cols(x["ssd_conv_b_2"]),
        "ssd_D": cols(np.repeat(x["ssd_D_2"][0], SSD_P)), "ssd_g": cols(x["ssd_norm_g_2"]),
        "xa_pre": cols(x["xa_pre_g_2"]), "xa_post": cols(x["xa_post_g_2"]), "mem": cols(x["mem_norm_g_2"]),
        "ffn2_pre": cols(x["ffn2_pre_g_2"]), "ffn2_post": cols(x["ffn2_post_g_2"]),
        "dt_bias": wide(x["ssd_dt_bias_2"]), "A_log": wide(x["ssd_A_log_2"]),
    }
    vecs = np.zeros((P, N_VEC), np.float32)
    for name, v in vec.items():
        at, n = VECS[name]
        vecs[:, at:at + n] = v
    at = VECS["lam"][0]
    for i, name in enumerate(("q1", "k1", "q2", "k2")):
        vecs[:64, at + i] = x[f"da_lambda_{name}_2"][0]
    a["vecs"] = vecs
    a["consts"] = shape_constants()
    a["rel_bias"] = x["rel_bias"]
    feature_major = lambda v: np.ascontiguousarray(v[0].reshape(T, DC, P).transpose(2, 1, 0))
    a["xT"] = feature_major(x["x"])
    a["memT"] = feature_major(x["mem_2"])
    return a




class Steps:

    def __init__(self, sem):
        self.sem, self.n = sem, 0

    def step(self, engine, instruction):
        self.n += 1
        instruction.then_inc(self.sem, 1)
        engine.wait_ge(self.sem, self.n)


class Ring:

    def __init__(self, nc, ctx, w):
        def tiles(name, dt, n):
            return [ctx.enter_context(nc.sbuf_tensor(f"{name}{s}", [P, SLOT_TILES * P], dt)) for s in range(n)]

        self.raw, self.hi, self.lo = tiles("w_raw", F32, RAW), tiles("w_hi", F32R, CUT), tiles("w_lo", F32R, CUT)
        self.loaded = [ctx.enter_context(nc.semaphore(f"w_loaded{s}")) for s in range(RAW)]
        self.hi_done, self.lo_done, self.mm_done = (
            ctx.enter_context(nc.semaphore(n)) for n in ("w_hi_done", "w_lo_done", "mm_done"))
        self.source, self.first, self.chunk0, self.end, chunks = [], {}, {}, [], 0
        for name, n, tiles, per in plan():
            self.first[name], self.chunk0[name] = len(self.source), chunks
            for i in range(n):
                self.source.append((w[name], i))
                chunks += per
                self.end.append(chunks)
        self.blocks = len(self.source)

    def size(self, n):
        return self.source[n][0].shape[2]

    def load(self, sp, n):
        if n >= self.blocks:
            return
        if n >= RAW:
            sp.wait_ge(self.lo_done, n - RAW + 1)
        ap, i = self.source[n]
        sp.dma_start(self.raw[n % RAW][:, 0:self.size(n)], ap[i]).then_inc(self.loaded[n % RAW], 16)

    def cut_hi(self, act, n):
        if n >= self.blocks:
            return
        act.wait_ge(self.loaded[n % RAW], 16 * (n // RAW + 1))
        if n >= CUT:
            act.wait_ge(self.mm_done, self.end[n - CUT])
        act.activation(self.hi[n % CUT][:, 0:self.size(n)], self.raw[n % RAW][:, 0:self.size(n)],
                       ACT.Copy).then_inc(self.hi_done, 1)

    def cut_lo(self, dve, n):
        if n >= self.blocks:
            return
        dve.wait_ge(self.hi_done, n + 1)
        dve.tensor_tensor(self.lo[n % CUT][:, 0:self.size(n)], self.raw[n % RAW][:, 0:self.size(n)],
                          self.hi[n % CUT][:, 0:self.size(n)].bitcast(F32), ALU.subtract).then_inc(self.lo_done, 1)

    def ready(self, pe, n):
        pe.wait_ge(self.lo_done, n + 1)

    def part(self, n, at, cols=P):
        return self.hi[n % CUT][:, at:at + cols], self.lo[n % CUT][:, at:at + cols]


def product(pe, out, still, moving, start, stop):
    pe.matmul(out, still[0], moving[0], start=start, stop=False)
    pe.matmul(out, still[0], moving[1], start=False, stop=False)
    return pe.matmul(out, still[1], moving[0], start=False, stop=stop)


class Pair:

    def __init__(self, hi, lo):
        self.hi, self.lo = hi, lo

    def at(self, c, t=slice(0, T)):
        return self.hi[:, c, t], self.lo[:, c, t]


def emit(nc, w, out, stop=None):
    root = ExitStack()
    uid = [0]
    in_use = []
    with root:
        def make(ctx):
            def sb(name, shape, dt=F32):
                uid[0] += 1
                return ctx.enter_context(nc.sbuf_tensor(f"{name}_{uid[0]}", shape, dt))
            return sb

        @contextmanager
        def scope():
            with ExitStack() as c:
                yield make(c)

        def semaphores(*names):
            uid[0] += 1
            new = [nc.alloc_semaphore(name=f"{n}_{uid[0]}") for n in names]
            in_use.extend(new)
            return new

        def recycle():
            nc.clear_and_free_semaphores(list(in_use))
            nc.all_engine_barrier()
            in_use.clear()

        def block():
            return nc.Block(no_gpsimd_drain=True)

        ring = Ring(nc, root, w)
        mm_done = ring.mm_done
        sb = make(root)
        pair = lambda s, name, n: Pair(s(name + "_hi", [P, n, T], F32R), s(name + "_lo", [P, n, T], F32R))
        h = sb("residual", [P, DC, T])
        xn = pair(sb, "x", DC)
        sq = sb("squares", [P, 2, T])
        h_sum = sb("sum_of_squares", [P, T])
        inv = sb("inverse_rms", [P, T])
        inv_tok = sb("inverse_rms_tokens", [P, 2])
        root_t = sb("rms", [P, T + 2])
        vecs = sb("vecs", [P, N_VEC])
        consts = sb("consts", [P, N_CONST])
        eps_t = sb("eps", [P, 2])
        EPS = {1e-6: eps_t[:, 0:1], 1e-5: eps_t[:, 1:2]}
        bank = [root.enter_context(nc.psum_tensor(f"bank{i}", [P, 512], F32)) for i in range(8)]

        def const(name):
            at, n = CONSTS[name]
            return consts[:, at:at + n]

        def vec(name, i=0, n=1):
            at, _ = VECS[name]
            return vecs[:, at + i:at + i + n]

        ident, ones, tri = const("ident"), const("ones"), const("tri")

        class Tail:

            def __init__(self, gain=None, dst=None, total=h_sum, offset=0, squares=sq):
                self.gain, self.dst, self.total, self.offset, self.sq = gain, dst, total, offset, squares
                self.given, self.hi, self.added = semaphores("given", "tail_hi", "added")

            def act(self, act, m, src):
                act.wait_ge(self.given, m + 1)
                if m >= 2:
                    act.wait_ge(self.added, m - 1)
                last = act.activation(self.sq[:, m % 2, :], src, ACT.Square)
                if self.gain:
                    last = act.activation(self.dst.hi[:, m + self.offset, :], src, ACT.Copy, scale=self.gain(m))
                last.then_inc(self.hi, 1)

            def dve(self, dve, m, src):
                dve.wait_ge(self.hi, m + 1)
                if self.gain:
                    dve.scalar_tensor_tensor(out=self.dst.lo[:, m + self.offset, :], in0=src, scalar=self.gain(m),
                                             in1=self.dst.hi[:, m + self.offset, :].bitcast(F32), op0=ALU.mult,
                                             op1=ALU.subtract)
                if m == 0:
                    dve.tensor_copy(self.total[:, :], self.sq[:, 0, :]).then_inc(self.added, 1)
                else:
                    dve.wait_ge(self.added, m)
                    dve.tensor_tensor(self.total[:, :], self.total[:, :], self.sq[:, m % 2, :], ALU.add).then_inc(self.added, 1)

        class Inverse:

            def __init__(self, n, eps=1e-6, total=h_sum, out=inv, tok=None, b=7):
                self.n, self.eps, self.total, self.out, self.tok, self.bank = n, eps, total, out, tok, bank[b]
                self.root = root_t
                self.summed, self.rooted, self.inverted = semaphores("summed", "rooted", "inverted")

            def pe(self, pe):
                last = pe.matmul(self.bank[:, 0:T], ones, self.total[:, :], start=True, stop=True)
                if self.tok is not None:
                    for t in range(2):
                        last = pe.matmul(self.bank[:, T + t:T + t + 1], self.total[:, t * P:(t + 1) * P], ones[:, 0:1],
                                         start=True, stop=True)
                last.then_inc(self.summed, 1)

            def act(self, act, used=None):
                act.wait_ge(self.summed, 1)
                if used:
                    act.wait_ge(used, 1)
                n = T if self.tok is None else T + 2
                act.activation(self.root[:, 0:n], self.bank[:, 0:n], ACT.Sqrt, bias=EPS[self.eps],
                               scale=1.0 / self.n).then_inc(self.rooted, 1)

            def dve(self, dve):
                dve.wait_ge(self.rooted, 1)
                last = dve.reciprocal(self.out[:, :], self.root[:, 0:T])
                if self.tok is not None:
                    last = dve.reciprocal(self.tok[:, :], self.root[:, T:T + 2])
                last.then_inc(self.inverted, 1)
                dve.wait_ge(self.inverted, 1)

        class Part:

            def __init__(self, name, kind, x, k, chunks, cols=T):
                self.name, self.kind, self.x, self.k, self.chunks, self.cols = name, kind, x, k, chunks, cols

            def run(self, pe, j, psum):
                chunk = ring.chunk0[self.name] + j
                n = next(i for i in range(ring.first[self.name], ring.blocks) if ring.end[i] > chunk)
                start = ring.end[n - 1] if n else 0
                per = ring.end[n] - start
                if chunk == start:
                    ring.ready(pe, n)
                if self.kind == "f":
                    for c in range(self.k):
                        last = product(pe, psum[:, 0:T], ring.part(n, ((chunk - start) * self.k + c) * P), self.x(c),
                                       c == 0, c == self.k - 1)
                    return last
                for t in range(2):
                    for c in range(self.k):
                        at = (c * per + chunk - start) * self.cols
                        hi, lo = self.x(c)
                        last = product(pe, psum[:, t * self.cols:(t + 1) * self.cols],
                                       (hi[:, t * P:(t + 1) * P], lo[:, t * P:(t + 1) * P]),
                                       ring.part(n, at, self.cols), c == 0, c == self.k - 1)
                return last

            def view(self, psum):
                if self.kind == "f":
                    return psum[:, 0:T]
                return psum[:, 0:2 * self.cols].rearrange("p (t c) -> p t c", t=2)

        def project(parts, leave, inverses=(), post=None, later=None, tail=None, tail_src=None, sp_first=None,
                    pe_first=None, act_first=None, pool=None):
            chunks = [(p, j) for p in parts for j in range(p.chunks)]
            c0 = ring.chunk0[parts[0].name]
            ends = {ring.end[n] - c0 - 1: n for n in range(ring.blocks)}
            left, posted, step_d = semaphores("left", "posted", "step")
            tails = tail if isinstance(tail, dict) else {i: (tail, i) for i in range(len(chunks))} if tail else {}
            first_n = ring.first[parts[0].name]
            last_n = ends[len(chunks) - 1]
            with block() as b:
                @b.sync
                def _(sp):
                    if sp_first:
                        sp_first(sp)
                    for n in range(first_n + RAW, last_n + RAW + 1):
                        ring.load(sp, n)

                if pool:
                    @b.gpsimd
                    def _(eng):
                        pool(eng)

                @b.tensor
                def _(pe):
                    for v in inverses:
                        v.pe(pe)
                    if pe_first:
                        pe_first(pe)
                    for i, (p, j) in enumerate(chunks):
                        if i >= 4:
                            pe.wait_ge(left, i - 3)
                        p.run(pe, j, bank[i % 4]).then_inc(mm_done, 1)

                @b.scalar
                def _(act):
                    for k, v in enumerate(inverses):
                        v.act(act, inverses[k - 1].inverted if k else None)
                    if act_first:
                        act_first(act)
                    for i in range(len(chunks)):
                        if post:
                            post(act, i, left, posted)
                        if i in tails:
                            t, m = tails[i]
                            t.act(act, m, tail_src(i))
                        if i in ends:
                            ring.cut_hi(act, ends[i] + CUT)

                @b.vector
                def _(dve):
                    steps = Steps(step_d)
                    steps.left = left
                    for v in inverses:
                        v.dve(dve)
                    for i, (p, j) in enumerate(chunks):
                        dve.wait_ge(mm_done, c0 + i + 1)
                        last = leave(dve, steps, i, p.view(bank[i % 4]), posted)
                        if i in tails:
                            t, m = tails[i]
                            last.then_inc(t.given, 1)
                            dve.wait_ge(t.given, m + 1)
                            dve.sem_inc(left, 1)
                        else:
                            last.then_inc(left, 1)
                        if i in ends:
                            ring.cut_lo(dve, ends[i] + CUT - 1)
                        if later and i >= 1:
                            later(dve, steps, i - 1, left)
                        if i - 1 in tails:
                            t, m = tails[i - 1]
                            t.dve(dve, m, tail_src(i - 1))
                    if later:
                        later(dve, steps, len(chunks) - 1, left)
                    if len(chunks) - 1 in tails:
                        t, m = tails[len(chunks) - 1]
                        t.dve(dve, m, tail_src(len(chunks) - 1))

        def ffn(name, y=None, next_gain=None):
            gu0, dn0 = ring.first[name + "_gu"], ring.first[name + "_dn"]
            gu_c, dn_c = ring.chunk0[name + "_gu"], ring.chunk0[name + "_dn"]
            scaled, silu_done, prod_done, hid_hi, hid_lo, out_done = semaphores(
                "scaled", "silu_done", "prod_done", "hid_hi", "hid_lo", "out_done")
            one = Inverse(D)
            dst = h if y is None else y
            tail = Tail(next_gain, xn) if next_gain else Tail()
            N = 3
            size = 2 * DC * P
            hi_i = lambda j: (gu0 + j) % CUT
            raw_i = lambda j: (gu0 + j) % RAW
            with scope() as s:
                gur = s("gate_up", [P, N, 2 * T])
                sg = s("silu", [P, N, T])
                prod = s("product", [P, N, T])
                hh = s("hidden_hi", [P, FC * T], F32R)
                hl = s("hidden_lo", [P, FC * T], F32R)
                with block() as b:
                    @b.sync
                    def _(sp):
                        loads = FC - RAW
                        with sp.Fori(0, loads // RAW) as t:
                            for j in range(RAW):
                                i = t * RAW + j
                                sp.wait_ge(ring.lo_done, i + (gu0 + 1))
                                sp.dma_start(ring.raw[raw_i(j)][:, :],
                                             w[name + "_gu"][bass.ds(i + RAW, 1)].rearrange("a p c -> (a p) c")
                                             ).then_inc(ring.loaded[raw_i(j)], 16)
                        for n in range(gu0 + RAW + loads // RAW * RAW, dn0 + 2 * DC + RAW):
                            ring.load(sp, n)

                    @b.tensor
                    def _(pe):
                        def gate_up(i, j):
                            pe.wait_ge(ring.lo_done, i + (gu0 + 1))
                            pe.wait_ge(scaled, i + 1)
                            for half in range(2):
                                for c in range(DC):
                                    at = (half * DC + c) * P
                                    last = product(pe, bank[j][:, half * T:half * T + T],
                                                   (ring.hi[hi_i(j)][:, at:at + P], ring.lo[hi_i(j)][:, at:at + P]),
                                                   xn.at(c), c == 0, c == DC - 1)
                            last.then_inc(mm_done, 1)

                        one.pe(pe)
                        with pe.Fori(0, FC // N) as t:
                            for j in range(N):
                                gate_up(t * N + j, j)
                        for i in range(FC // N * N, FC):
                            gate_up(i, i % N)
                        for m in range(DC):
                            if m >= 2:
                                pe.wait_ge(out_done, m - 1)
                            for half in range(2):
                                n = dn0 + 2 * m + half
                                ring.ready(pe, n)
                                if m == 0:
                                    pe.wait_ge(hid_lo, (half + 1) * HALF)
                                for c in range(HALF):
                                    k = half * HALF + c
                                    last = product(pe, bank[4 + m % 2][:, 0:T], ring.part(n, c * P),
                                                   (hh[:, k * T:(k + 1) * T], hl[:, k * T:(k + 1) * T]),
                                                   k == 0, k == FC - 1)
                                last.then_inc(mm_done, 1)

                    @b.scalar
                    def _(act):
                        def silu(i, j):
                            act.wait_ge(scaled, i + (N + 1))
                            act.wait_ge(prod_done, i + 1)
                            act.activation(sg[:, j, :], gur[:, j, 0:T], ACT.Silu).then_inc(silu_done, 1)

                        def hidden_hi(i, j):
                            act.wait_ge(prod_done, i + (N + 1))
                            act.activation(hh[:, bass.ds(i * T, T)], prod[:, j, :], ACT.Copy).then_inc(hid_hi, 1)

                        one.act(act)
                        with act.Fori(0, (FC - CUT) // N) as t:
                            for j in range(N):
                                i = t * N + j
                                silu(i, j)
                                n_loads = (gu0 + CUT + j) // RAW + 1
                                act.wait_ge(ring.loaded[raw_i(j)], t * 16 + 16 * n_loads)
                                act.wait_ge(mm_done, i + (gu_c + 1))
                                act.activation(ring.hi[hi_i(j)][:, 0:size], ring.raw[raw_i(j)][:, 0:size], ACT.Copy
                                               ).then_inc(ring.hi_done, 1)
                                hidden_hi(i, j)
                        for i in range((FC - CUT) // N * N, FC):
                            silu(i, i % N)
                            ring.cut_hi(act, gu0 + i + CUT)
                            hidden_hi(i, i % N)
                        for m in range(DC):
                            ring.cut_hi(act, dn0 + 2 * m + CUT)
                            tail.act(act, m, dst[:, m, :])
                            ring.cut_hi(act, dn0 + 2 * m + 1 + CUT)

                    @b.vector
                    def _(dve):
                        dve.sem_inc(scaled, N)
                        dve.sem_inc(prod_done, N)
                        one.dve(dve)
                        r = inv[:, :]
                        twice = bass.AP(r.tensor, r.offset, [r.ap[0], [0, 2], [1, T]])

                        def scale(i, j):
                            dve.wait_ge(mm_done, i + (gu_c + 1))
                            dve.tensor_tensor(gur[:, j, :].rearrange("p (a t) -> p a t", a=2),
                                              bank[j][:, :].rearrange("p (a t) -> p a t", a=2), twice,
                                              ALU.mult).then_inc(scaled, 1)

                        def hidden_lo(i, j):
                            dve.wait_ge(hid_hi, i + 1)
                            dve.tensor_tensor(hl[:, bass.ds(i * T, T)], prod[:, j, :],
                                              hh[:, bass.ds(i * T, T)].bitcast(F32), ALU.subtract).then_inc(hid_lo, 1)

                        def gated(i, j):
                            dve.wait_ge(silu_done, i + 1)
                            dve.tensor_tensor(prod[:, j, :], sg[:, j, :], gur[:, j, T:2 * T], ALU.mult).then_inc(prod_done, 1)

                        def straight(i):
                            scale(i, i % N)
                            if i:
                                hidden_lo(i - 1, (i - 1) % N)
                            ring.cut_lo(dve, gu0 + i + CUT - 1)
                            gated(i, i % N)

                        for i in range(N):
                            straight(i)
                        trips = (FC - CUT) // N
                        with dve.Fori(1, trips) as t:
                            for j in range(N):
                                i = t * N + j
                                scale(i, j)
                                hidden_lo(i - 1, (j - 1) % N)
                                at = (gu0 + j + CUT - 1)
                                dve.wait_ge(ring.hi_done, i + (gu0 + CUT))
                                dve.tensor_tensor(ring.lo[at % CUT][:, 0:size], ring.raw[at % RAW][:, 0:size],
                                                  ring.hi[at % CUT][:, 0:size].bitcast(F32), ALU.subtract
                                                  ).then_inc(ring.lo_done, 1)
                                gated(i, j)
                        for i in range(trips * N, FC):
                            straight(i)
                        hidden_lo(FC - 1, (FC - 1) % N)
                        for m in range(DC):
                            ring.cut_lo(dve, dn0 + 2 * m + CUT - 1)
                            dve.wait_ge(mm_done, dn_c + 2 * m + 2)
                            o = bank[4 + m % 2][:, 0:T]
                            if y is None:
                                dve.scalar_tensor_tensor(out=h[:, m, :], in0=o, scalar=0.5, in1=h[:, m, :],
                                                         op0=ALU.mult, op1=ALU.add).then_inc(tail.given, 1)
                            else:
                                dve.tensor_copy(y[:, m, :], o).then_inc(tail.given, 1)
                            dve.wait_ge(tail.given, m + 1)
                            dve.sem_inc(out_done, 1)
                            tail.dve(dve, m, dst[:, m, :])
                            ring.cut_lo(dve, dn0 + 2 * m + 1 + CUT - 1)

        def add_normed(y, gain, factor, next_gain, n=D):
            one = Inverse(n)
            tail = Tail(next_gain, xn) if next_gain else None
            normed, out_ready, stored = semaphores("normed", "out_ready", "stored")
            given = tail.given if tail else out_ready
            with block() as b:
                @b.tensor
                def _(pe):
                    one.pe(pe)

                @b.scalar
                def _(act):
                    one.act(act)
                    for c in range(DC):
                        if tail:
                            tail.act(act, c, h[:, c, :])

                @b.vector
                def _(dve):
                    one.dve(dve)

                    def add(c):
                        dve.wait_ge(normed, c + 1)
                        dve.scalar_tensor_tensor(out=h[:, c, :], in0=y[:, c, :], scalar=factor, in1=h[:, c, :],
                                                 op0=ALU.mult, op1=ALU.add).then_inc(given, 1)

                    for c in range(DC + 2):
                        if c < DC:
                            dve.scalar_tensor_tensor(out=y[:, c, :], in0=y[:, c, :], scalar=gain(c), in1=inv[:, :],
                                                     op0=ALU.mult, op1=ALU.mult).then_inc(normed, 1)
                        if 0 <= c - 1 < DC:
                            add(c - 1)
                        if tail and 0 <= c - 2:
                            tail.dve(dve, c - 2, h[:, c - 2, :])

                if not tail:
                    @b.sync
                    def _(sp):
                        for c in range(DC):
                            sp.wait_ge(out_ready, c + 1)
                            sp.dma_start(out[:, c, :], h[:, c, :]).then_inc(stored, 16)
                        sp.wait_ge(stored, 16 * DC)

        def norm_groups(src, dst, gain, chunks, groups, eps):
            n = chunks * groups
            squared, summed, rooted, scaled, hi_done, d_step = semaphores(
                "squared", "summed", "rooted", "scaled", "cut_hi", "norm_step")
            with scope() as s:
                sqs = s("group_squares", [P, 4, T])
                rt = s("root", [P, groups, T])
                with block() as b:
                    @b.scalar
                    def _(act):
                        for c in range(n):
                            if c >= 4:
                                act.wait_ge(summed, c - 3)
                            act.activation(sqs[:, c % 4, :], src[:, c, :], ACT.Square).then_inc(squared, 1)
                        for g in range(groups):
                            act.wait_ge(summed, (g + 1) * chunks)
                            act.activation(rt[:, g, :], bank[g][:, 0:T], ACT.Sqrt, bias=EPS[eps],
                                           scale=1.0 / (chunks * P)).then_inc(rooted, 1)
                        for c in range(n):
                            act.wait_ge(scaled, c + 1)
                            act.activation(dst.hi[:, c, :], src[:, c, :], ACT.Copy).then_inc(hi_done, 1)

                    @b.tensor
                    def _(pe):
                        for c in range(n):
                            pe.wait_ge(squared, c + 1)
                            pe.matmul(bank[c // chunks][:, 0:T], ones, sqs[:, c % 4, :], start=c % chunks == 0,
                                      stop=c % chunks == chunks - 1).then_inc(summed, 1)

                    @b.vector
                    def _(dve):
                        steps = Steps(d_step)

                        def lo(c):
                            dve.wait_ge(hi_done, c + 1)
                            dve.tensor_tensor(dst.lo[:, c, :], src[:, c, :], dst.hi[:, c, :].bitcast(F32), ALU.subtract)

                        for g in range(groups):
                            dve.wait_ge(rooted, g + 1)
                            steps.step(dve, dve.reciprocal(rt[:, g, :], rt[:, g, :]))
                            for c in range(g * chunks, (g + 1) * chunks):
                                dve.scalar_tensor_tensor(out=src[:, c, :], in0=src[:, c, :], scalar=gain(c), in1=rt[:, g, :],
                                                         op0=ALU.mult, op1=ALU.mult).then_inc(scaled, 1)
                                if c >= 2:
                                    lo(c - 2)
                        for c in range(max(n - 2, 0), n):
                            lo(c)

        def attention(jobs, oT, scale=1.0, causal=True):
            (s_ready, s_max, exp_done, p_ready, t_ready, pt_ready, v_done, o_ready, o_hi, o_done, d_step) = semaphores(
                "s_ready", "s_max", "exp_done", "p_ready", "t_ready", "pt_ready", "v_done", "o_ready", "o_hi", "o_done",
                "attn_step")
            n = len(jobs)
            w0 = P if causal else T
            width = T + w0
            NP, NT = 4, 3
            rows = ((1, 0, T), (0, T, w0))
            cuts = [(T, 0), (0, P)] + ([(P, 2 * P)] if causal else [(T + P, 2 * P), (P, 3 * P)])
            chunks_of = lambda j: sorted({o[0] for o in jobs[j]["outs"]}) if jobs[j]["evict"] else []
            with scope() as s:
                sc = s("scores", [P, 2, width])
                pr = s("probs", [P, NP, width])
                pt = s("probsT", [P, NT, width])
                nm = s("neg_max", [P, 2, 2])
                sm = s("sums", [P, NP, 2])
                cf = s("coef", [P, 2, 2])
                zero = s("no_mask", [P, T])
                with block() as b:
                    @b.gpsimd
                    def _(pool):
                        pool.memset(zero[:, :], 0.0).then_inc(d_step, 1)

                    @b.tensor
                    def _(pe):
                        def score(j):
                            if j >= 2:
                                pe.wait_ge(s_max, 2 * (j - 1))
                            for q, at, keys in rows:
                                parts = jobs[j]["scores"]
                                for i, (qf, kf) in enumerate(parts):
                                    last = pe.matmul(bank[j % 2][:, at:at + keys], qf[:, q * P:(q + 1) * P],
                                                     kf[:, 0:keys], start=i == 0, stop=i == len(parts) - 1)
                            last.then_inc(s_ready, 1)

                        def turn(j):
                            pe.wait_ge(p_ready, j + 1)
                            if j >= 2:
                                pe.wait_ge(pt_ready, j - 1)
                            for a, c in cuts:
                                last = pe.transpose(bank[2 + j % 2][:, c:c + P], pr[:, j % NP, a:a + P], ident)
                            last.then_inc(t_ready, 1)

                        def values(j):
                            job = jobs[j]
                            pe.wait_ge(pt_ready, j + 1)
                            for i, (chunk, r0, rn, v) in enumerate(job["outs"]):
                                o = bank[4 + chunk % 4]
                                if job["first"] and chunk >= 4:
                                    pe.wait_ge(o_done, chunk - 3)
                                x = job.get("extra") if job["first"] else None
                                if x:
                                    pe.matmul(o[r0:r0 + rn, 0:T], x[0], x[1], start=True, stop=False)
                                pe.matmul(o[r0:r0 + rn, 0:T], v(0), pt[:, j % NT, 0:T],
                                          start=job["first"] and not x, stop=False)
                                a, c = (P, T) if causal else (0, T)
                                last = pe.matmul(o[r0:r0 + rn, a:T], v(1), pt[:, j % NT, c:width], start=False,
                                                 stop=job["last"])
                                if i < len(job["outs"]) - 1:
                                    last.then_inc(o_ready, 1)
                            last.then_inc(v_done, 1)
                            if job["evict"]:
                                pe.wait_ge(v_done, j + 1)
                                pe.sem_inc(o_ready, 1)

                        for j in range(n + 3):
                            if j < n:
                                score(j)
                            if 0 <= j - 2 < n:
                                turn(j - 2)
                            if 0 <= j - 3 < n:
                                values(j - 3)

                    @b.vector
                    def _(dve):
                        steps = Steps(d_step)
                        steps.n = 1
                        dve.wait_ge(d_step, 1)

                        def peak(j):
                            dve.wait_ge(s_ready, j + 1)
                            if j >= 2:
                                dve.wait_ge(exp_done, 2 * (j - 1))
                            for i, (q, at, keys) in enumerate(rows):
                                add = jobs[j]["add"]
                                m = zero[:, 0:keys] if add is None else add[:, T - keys:T]
                                dve.tensor_tensor_reduce(
                                    out=sc[:, j % 2, at:at + keys], in0=bank[j % 2][:, at:at + keys], in1=m,
                                    scale=-scale, scalar=3e38, op0=ALU.add, op1=ALU.min,
                                    accum_out=nm[:, j % 2, i:i + 1]).then_inc(s_max, 1)

                        def weigh(j):
                            dve.wait_ge(exp_done, 2 * (j + 1))
                            steps.step(dve, dve.reciprocal(cf[:, j % 2, :], sm[:, j % NP, :]))
                            if jobs[j].get("coef") is not None:
                                steps.step(dve, dve.tensor_tensor(cf[:, j % 2, :], cf[:, j % 2, :], jobs[j]["coef"], ALU.mult))
                            for i, (q, at, keys) in enumerate(rows):
                                last = dve.tensor_scalar(pr[:, j % NP, at:at + keys], pr[:, j % NP, at:at + keys],
                                                         cf[:, j % 2, i:i + 1], None, ALU.mult)
                            last.then_inc(p_ready, 1)

                        def leave(j):
                            for chunk in chunks_of(j):
                                dve.wait_ge(o_hi, chunk + 1)
                                dve.tensor_tensor(oT.lo[:, chunk, :], bank[4 + chunk % 4][:, 0:T],
                                                  oT.hi[:, chunk, :].bitcast(F32), ALU.subtract).then_inc(o_done, 1)

                        for j in range(n + 4):
                            if j < n:
                                peak(j)
                            if 0 <= j - 1 < n:
                                weigh(j - 1)
                            if 0 <= j - 4 < n:
                                leave(j - 4)

                    @b.scalar
                    def _(act):
                        def exps(j):
                            if j >= NP:
                                act.wait_ge(t_ready, j - NP + 1)
                            for i, (q, at, keys) in enumerate(rows):
                                act.wait_ge(s_max, 2 * j + i + 1)
                                act.activation(pr[:, j % NP, at:at + keys], sc[:, j % 2, at:at + keys], ACT.Exp,
                                               bias=nm[:, j % 2, i:i + 1], scale=-1.0,
                                               accum_out=sm[:, j % NP, i:i + 1]).then_inc(exp_done, 1)

                        def copies(j):
                            act.wait_ge(t_ready, j + 1)
                            if j >= NT:
                                act.wait_ge(v_done, j - NT + 1)
                            act.activation(pt[:, j % NT, :], bank[2 + j % 2][:, 0:width], ACT.Copy).then_inc(pt_ready, 1)

                        def leave(j):
                            for chunk in chunks_of(j):
                                act.wait_ge(o_ready, chunk + 1)
                                act.activation(oT.hi[:, chunk, :], bank[4 + chunk % 4][:, 0:T], ACT.Copy).then_inc(o_hi, 1)

                        for j in range(n + 3):
                            if j < n:
                                exps(j)
                            if 0 <= j - 2 < n:
                                copies(j - 2)
                            if 0 <= j - 3 < n:
                                leave(j - 3)


        def times(dve, dst, o, r=inv, factor=1.0):
            if factor == 1.0:
                return dve.tensor_tensor(dst, o, r[:, :], ALU.mult)
            return dve.scalar_tensor_tensor(out=dst, in0=o, scalar=factor, in1=r[:, :], op0=ALU.mult, op1=ALU.mult)

        def times_tok(dve, dst, o, r=inv_tok):
            for t in range(2):
                last = dve.tensor_scalar(dst[:, t, :], o[:, t, :], r[:, t:t + 1], None, ALU.mult)
            return last

        def add_to_h(dve, steps, i, o, posted):
            return dve.tensor_tensor(h[:, i, :], o, h[:, i, :], ALU.add)

        def to_residual(name, src, k, next_gain):
            project([Part(name, "f", src.at, k, DC)], add_to_h, tail=Tail(next_gain, xn), tail_src=lambda i: h[:, i, :])

        gain = lambda name: (lambda c: vec(name, c))


        def start():
            at_start, = semaphores("at_start")
            tail = Tail(gain("ffn_a0"), xn)
            with block() as b:
                @b.sync
                def _(sp):
                    sp.dma_start(h[:, :, :], w["xT"]).then_inc(at_start, 16)
                    sp.dma_start(vecs[:, :], w["vecs"]).then_inc(at_start, 16)
                    for n in range(2):
                        ring.load(sp, n)
                    sp.dma_start(consts[:, :], w["consts"]).then_inc(at_start, 16)
                    ring.load(sp, 2)
                    sp.wait_ge(at_start, 48)

                @b.scalar
                def _(act):
                    act.wait_ge(at_start, 48)
                    for m in range(DC):
                        tail.act(act, m, h[:, m, :])
                        if m < CUT:
                            ring.cut_hi(act, m)

                @b.vector
                def _(dve):
                    for i, e in enumerate((1e-6, 1e-5)):
                        dve.memset(eps_t[:, i:i + 1], e)
                    dve.wait_ge(at_start, 48)
                    dve.sem_inc(tail.given, DC)
                    for m in range(DC):
                        tail.dve(dve, m, h[:, m, :])
                        if m < CUT - 1:
                            ring.cut_lo(dve, m)


        def mla(next_gain):
            with scope() as s:
                c_in = s("latents", [P, 5, T])
                cn = pair(s, "latents", 5)
                k_rope = s("k_rope", [P, T])
                tmp = s("tmp", [P, 2, T])
                kv_sum = s("kv_sum", [P, T])
                inv_kv = s("inv_kv", [P, T])
                q_sum = s("q_sum", [P, T])
                kv_squares = s("kv_squares", [P, 2, T])
                tail_q = Tail(lambda c: vec("cq", c), cn, total=q_sum)
                tail_kv = Tail(lambda c: vec("ckv", c), cn, total=kv_sum, offset=3, squares=kv_squares)

                def leave(dve, steps, i, o, posted):
                    if i < 5:
                        return times(dve, c_in[:, i, :], o)
                    turned = i - 5
                    if not turned:
                        dve.wait_ge(steps.left, i)
                    last = dve.tensor_tensor(tmp[:, turned, :], o, const(("cos", "sin")[turned]), ALU.mult)
                    if turned:
                        steps.step(dve, last)
                        steps.step(dve, dve.tensor_tensor(tmp[:, 0, :], tmp[:, 0, :], tmp[:, 1, :], ALU.add))
                        last = times(dve, k_rope[:, :], tmp[:, 0, :])
                    return last

                project([Part("mla_in", "f", xn.at, DC, 7)], leave, inverses=[Inverse(D)],
                        tail={0: (tail_q, 0), 1: (tail_q, 1), 2: (tail_q, 2), 3: (tail_kv, 0), 4: (tail_kv, 1)},
                        tail_src=lambda i: c_in[:, i, :])
                q_n = s("q_nope", [P, 8, T])
                q_r = s("q_rope", [P, 4, T])
                k_n = s("k_nope", [P, 8, T])
                v = s("v", [P, 2, D])

                def leave(dve, steps, i, o, posted):
                    if i < 8:
                        return times(dve, q_n[:, i, :], o)
                    if i < 16:
                        turned = (i - 8) % 2
                        if not turned:
                            dve.wait_ge(steps.left, i)
                        last = dve.tensor_tensor(tmp[:, turned, :], o, const(("cos", "sin")[turned]), ALU.mult)
                        if turned:
                            steps.step(dve, last)
                            steps.step(dve, dve.tensor_tensor(tmp[:, 0, :], tmp[:, 0, :], tmp[:, 1, :], ALU.add))
                            last = times(dve, q_r[:, (i - 8) // 2, :], tmp[:, 0, :])
                        return last
                    if i < 24:
                        return times(dve, k_n[:, i - 16, :], o, inv_kv)
                    return times_tok(dve, v[:, :, (i - 24) * 256:(i - 23) * 256], o)

                kv_at = lambda c: cn.at(3 + c)
                project([Part("mla_uq", "f", cn.at, 3, 16), Part("mla_uk", "f", kv_at, 2, 8),
                         Part("mla_uv", "t", kv_at, 2, 4, 256)], leave,
                        inverses=[Inverse(MLA_Q, total=q_sum),
                                  Inverse(MLA_KV, total=kv_sum, out=inv_kv, tok=inv_tok, b=6)])
                oT = pair(s, "heads_out", DC)
                jobs = []
                for hd in range(HEADS):
                    c, r = hd // 2, 64 * (hd % 2)
                    rr = 32 * (hd % 4)
                    jobs.append(dict(
                        scores=[(q_n[r:r + 64, c, :], k_n[r:r + 64, c, :]),
                                (q_r[rr:rr + 32, hd // 4, :], k_rope[rr:rr + 32, :])],
                        add=const("mask"), first=True, last=True, evict=hd % 2 == 1,
                        outs=[(c, r, 64, lambda kb, hd=hd: v[:, kb, hd * 64:hd * 64 + 64])]))
                attention(jobs, oT, scale=(MLA_NOPE + MLA_ROPE) ** -0.5)
                to_residual("mla_o", oT, DC, next_gain)

        def nsa(next_gain):
            with scope() as s:
                qT = s("q", [P, DC, T])
                k_s = s("k_sel", [P, NSA_GROUPS, T])
                k_w = s("k_win", [P, NSA_GROUPS, T])
                v_s = s("v_sel", [P, 2, 256])
                v_w = s("v_win", [P, 2, 256])
                gates = s("gates", [P, 2, 48])
                bias = s("bias", [P, HEADS, T])
                vcm = s("v_cmp", [N_CMP, NSA_GROUPS, 64])
                pTc = s("probsT_cmp", [N_CMP, HEADS, T])
                with scope() as s2:
                    kc2 = s2("k_c", [P, NSA_GROUPS, T])
                    vc2 = s2("v_c", [P, NSA_GROUPS, T])
                    rel = s2("rel_bias", [REL_BUCKETS + 1, HEADS])
                    ext = s2("bias_by_distance", [HEADS, TOEP])
                    tmp = s2("tmp", [P, 2, T])
                    w1 = s2("w1", [P, 2, 16, P])
                    w2 = s2("w2", [P, 4, 64])
                    rel_in, rel_mm, rel_out, rel_stored, bias_in, w_in = semaphores(
                        "rel_in", "rel_mm", "rel_out", "rel_stored", "bias_in", "cmp_weights")

                    def sp_first(sp):
                        sp.dma_start(rel[0:REL_BUCKETS, :], w["rel_bias"]).then_inc(rel_in, 16)
                        sp.dma_start(rel[REL_BUCKETS:REL_BUCKETS + 1, :],
                                     w["consts"][0:1, CONSTS["ones"][0]:CONSTS["ones"][0] + HEADS]).then_inc(rel_in, 16)
                        sp.dma_start(w1[:, :, :, :], w["nsa_w1"].rearrange("a p (c m) -> p a c m", m=P)).then_inc(w_in, 16)
                        sp.dma_start(w2[:, :, :], w["nsa_w2"].rearrange("p (a m) -> p a m", m=64)).then_inc(w_in, 16)

                    def pool(eng):
                        eng.wait_ge(rel_out, 1)
                        line = ext[:, :]
                        rows = bass.AP(line.tensor, T - 1 - P, [line.ap[0], [-1, P], [1, T]])
                        eng.dma_start(w["scratch"].rearrange("q h k -> h q k"), rows).then_inc(rel_stored, 16)
                        eng.wait_ge(rel_stored, 16)
                        eng.dma_start(bias[:, :, :], w["scratch"]).then_inc(bias_in, 16)
                        eng.wait_ge(bias_in, 16)

                    def pe_first(pe):
                        pe.wait_ge(rel_in, 32)
                        pe.matmul(bank[4][0:HEADS, 0:TOEP], rel[:, :], const("bucket")[0:REL_BUCKETS + 1, :],
                                  start=True, stop=True).then_inc(rel_mm, 1)

                    def act_first(act):
                        act.wait_ge(rel_mm, 1)
                        act.activation(ext[:, :], bank[4][0:HEADS, 0:TOEP], ACT.Copy).then_inc(rel_out, 1)

                    def place(i):
                        kind, half = divmod(i - 8, 2)
                        return ((kc2, 1), (vc2, 1), (k_s, 0), (k_w, 0))[kind] + (half,)

                    def leave(dve, steps, i, o, posted):
                        if i < 8:
                            return times(dve, qT[:, i, :], o, factor=NSA_QK ** -0.5)
                        if i < 16:
                            if i >= 10:
                                dve.wait_ge(posted, i - 9)
                            steps.step(dve, times(dve, tmp[:, i % 2, :], o))
                            dst, shift, half = place(i)
                            dve.tensor_copy(dst[64:128, 2 * half, 0:T - shift], tmp[0:64, i % 2, shift:T])
                            return dve.tensor_copy(dst[64:128, 2 * half + 1, 0:T - shift], tmp[64:128, i % 2, shift:T])
                        if i < 18:
                            return times_tok(dve, (v_s, v_w)[i - 16], o)
                        return times_tok(dve, gates, o)

                    def post(act, i, left, posted):
                        if 8 <= i < 16:
                            act.wait_ge(left, i + 1)
                            dst, _, half = place(i)
                            act.activation(dst[0:64, 2 * half, :], tmp[0:64, i % 2, :], ACT.Copy)
                            act.activation(dst[0:64, 2 * half + 1, :], tmp[64:128, i % 2, :], ACT.Copy).then_inc(posted, 1)
                        if i == 18:
                            act.wait_ge(left, i + 1)
                            act.activation(gates[:, :, :], gates[:, :, :], ACT.Sigmoid)

                    project([Part("nsa_in", "f", xn.at, DC, 16), Part("nsa_v", "t", xn.at, DC, 2, 256),
                             Part("nsa_g", "t", xn.at, DC, 1, 48)], leave, inverses=[Inverse(D, tok=inv_tok)],
                            post=post, sp_first=sp_first, pe_first=pe_first, act_first=act_first, pool=pool)
                    flat = s2("flat", [P, 2, 16, NSA_GROUPS * N_CMP])
                    hid = s2("cmp_hidden", [P, 2, NSA_GROUPS * N_CMP])
                    kcm = s2("k_cmp", [P, NSA_GROUPS * N_CMP])
                    pc = s2("probs_cmp", [P, HEADS * 2, N_CMP])
                    bc = s2("bias_cmp", [P, HEADS, 2, N_CMP])
                    mx = s2("max_cmp", [P, HEADS * 2])
                    sm = s2("sum_cmp", [P, HEADS * 2])
                    fl, mm, hd_, cm, sc_, ex, tr, cp, d_step = semaphores(
                        "flat", "cmp_mm", "hidden", "cmp", "cmp_scores", "cmp_exp", "cmp_turned", "cmp_copied", "cmp_step")
                    with block() as b:
                        @b.tensor
                        def _(pe):
                            pe.wait_ge(w_in, 32)
                            for i in range(2):
                                pe.wait_ge(fl, i + 1)
                                for c in range(16):
                                    last = pe.matmul(bank[i][:, 0:60], w1[:, i, c, :], flat[:, i, c, :], start=c == 0, stop=c == 15)
                                last.then_inc(mm, 1)
                            pe.wait_ge(hd_, 2)
                            pe.matmul(bank[2][:, 0:60], w2[:, 0:2, :].rearrange("p a m -> p (a m)"), hid[:, 0, :],
                                      start=True, stop=True).then_inc(mm, 1)
                            for g in range(NSA_GROUPS):
                                last = pe.matmul(bank[3][0:N_CMP, g * 64:g * 64 + 64], hid[:, 1, g * N_CMP:(g + 1) * N_CMP],
                                                 w2[:, 2, :], start=True, stop=True)
                            last.then_inc(mm, 1)
                            pe.wait_ge(cm, 1)
                            for hd in range(HEADS):
                                r, g = 64 * (hd % 2), hd // 4
                                for q in range(2):
                                    at = (hd // 2 * 2 + q) * N_CMP
                                    last = pe.matmul(bank[4 + hd % 2][:, at:at + N_CMP],
                                                     qT[r:r + 64, hd // 2, q * P:(q + 1) * P],
                                                     kcm[r:r + 64, g * N_CMP:(g + 1) * N_CMP], start=True, stop=True)
                            last.then_inc(sc_, 1)
                            pe.wait_ge(ex, 2)
                            for pair_ in range(8):
                                if pair_ >= 4:
                                    pe.wait_ge(cp, pair_ - 3)
                                for i in range(4):
                                    last = pe.transpose(bank[pair_ % 4][0:N_CMP, i * P:(i + 1) * P], pc[:, 4 * pair_ + i, :], ident)
                                last.then_inc(tr, 1)

                        @b.scalar
                        def _(act):
                            for i in range(2):
                                act.wait_ge(mm, i + 1)
                                act.activation(hid[:, i, :], bank[i][:, 0:60], ACT.Gelu_apprx_tanh).then_inc(hd_, 1)
                            act.wait_ge(mm, 3)
                            act.activation(kcm[:, :], bank[2][:, 0:60], ACT.Copy).then_inc(cm, 1)
                            act.wait_ge(mm, 4)
                            act.activation(vcm[:, :, :], bank[3][0:N_CMP, 0:256].rearrange("p (g c) -> p g c", g=4), ACT.Copy)
                            act.wait_ge(sc_, 2)
                            act.activation(pc[:, :, :], pc[:, :, :], ACT.Exp).then_inc(ex, 1)
                            for pair_ in range(8):
                                act.wait_ge(tr, pair_ + 1)
                                act.activation(pTc[:, 2 * pair_:2 * pair_ + 2, :],
                                               bank[pair_ % 4][0:N_CMP, :].rearrange("p (h t) -> p h t", h=2), ACT.Copy).then_inc(cp, 1)

                        @b.vector
                        def _(dve):
                            steps = Steps(d_step)
                            for i, (src, pos) in enumerate(((kc2, "pos_k"), (vc2, "pos_v"))):
                                a = src[:, :, :]
                                v0 = vec(pos)
                                view = bass.AP(a.tensor, a.offset, [a.ap[0], [2, 16], [T, NSA_GROUPS], [CMP_STRIDE, N_CMP]])
                                pos_view = bass.AP(v0.tensor, v0.offset, [v0.ap[0], [1, 16], [0, NSA_GROUPS], [0, N_CMP]])
                                dve.tensor_tensor(flat[:, i, :, :].rearrange("p c (g n) -> p c g n", g=NSA_GROUPS), view, pos_view,
                                                  ALU.add).then_inc(fl, 1)
                            late, early = CMP_BLOCK - 1, P + CMP_BLOCK - 1
                            steps.step(dve, dve.memset(bc[:, :, 0, :], NEG))
                            steps.step(dve, dve.tensor_copy(bc[:, :, 0, 0:N_CMP0], bias[:, :, early:early + CMP_STRIDE * (N_CMP0 - 1) + 1:CMP_STRIDE]))
                            steps.step(dve, dve.tensor_copy(bc[:, :, 1, :], bias[:, :, late:late + CMP_STRIDE * (N_CMP - 1) + 1:CMP_STRIDE]))
                            dve.wait_ge(sc_, 1)
                            rows = lambda t: t[:, :].rearrange("p (a b) -> p a b", b=1).to_broadcast([P, HEADS * 2, N_CMP])
                            for par in range(2):
                                odd = lambda t: t.rearrange("p (a o b) n -> p a o (b n)", o=2, b=2)[:, :, par, :]
                                steps.step(dve, dve.tensor_tensor(
                                    odd(pc[:, :, :]), bank[4 + par][:, 0:HEADS * N_CMP].rearrange("p (a n) -> p a n", a=8),
                                    odd(bc[:, :, :, :].rearrange("p h q n -> p (h q) n")), ALU.add))
                            steps.step(dve, dve.tensor_reduce(mx[:, :], pc[:, :, :], AX.X, ALU.max))
                            dve.tensor_tensor(pc[:, :, :], pc[:, :, :], rows(mx), ALU.subtract).then_inc(sc_, 1)
                            dve.wait_ge(ex, 1)
                            steps.step(dve, dve.tensor_reduce(sm[:, :], pc[:, :, :], AX.X, ALU.add))
                            steps.step(dve, dve.reciprocal(sm[:, :], sm[:, :]))
                            by_q = lambda t: t[:, :].rearrange("p (h q) -> p h q", q=2)
                            steps.step(dve, dve.tensor_tensor(by_q(sm), by_q(sm), gates[:, :, 0:48:3].rearrange("p q h -> p h q"), ALU.mult))
                            vv = const("valid")
                            ok = bass.AP(vv.tensor, vv.offset, [vv.ap[0], [0, HEADS], [N_CMP, 2], [1, N_CMP]])
                            pc4 = pc[:, :, :].rearrange("p (h q) n -> p h q n", q=2)
                            steps.step(dve, dve.tensor_tensor(pc4, pc4, ok, ALU.mult))
                            dve.tensor_tensor(pc[:, :, :], pc[:, :, :], rows(sm), ALU.mult).then_inc(ex, 1)
                oT = pair(s, "heads_out", DC)
                jobs = []
                for hd in range(HEADS):
                    c, r, g = hd // 2, 64 * (hd % 2), hd // 4
                    for i, (kk, vv) in enumerate(((k_s, v_s), (k_w, v_w))):
                        jobs.append(dict(
                            scores=[(qT[r:r + 64, c, :], kk[r:r + 64, g, :])], add=bias[:, hd, :],
                            coef=gates[:, ::-1, 3 * hd + 1 + i], first=i == 0, last=i == 1, evict=i == 1 and hd % 2 == 1,
                            extra=(vcm[:, g, :], pTc[:, hd, :]),
                            outs=[(c, r, 64, lambda kb, vv=vv, g=g: vv[:, kb, g * 64:g * 64 + 64])]))
                attention(jobs, oT)
                to_residual("nsa_o", oT, DC, next_gain)

        def activated(name, dst, func, bias=None):
            def leave(dve, steps, i, o, posted):
                return times(dve, dst[:, i, :], o)

            def post(act, i, left, posted):
                act.wait_ge(left, i + 1)
                act.activation(dst[:, i, :], dst[:, i, :], func, bias=bias(i)).then_inc(posted, 1)
            return leave, post

        def two_branches(next_gain):
            with scope() as s:
                mixed = s("mixed", [P, DC, T])
                with scope() as s2:
                    gate = s2("gate", [P, DC, T])
                    qk = s2("qk", [P, 16, T])
                    v = s2("v", [P, 2, D])
                    neg_lam = s2("neg_lambda", [P, 2])
                    prod = s2("lambda_products", [64, 2])
                    ex = s2("lambda_exps", [P, 2])

                    def leave(dve, steps, i, o, posted):
                        if i < 16:
                            return times(dve, qk[:, i, :], o, factor=DA_QK ** -0.5 if i < 8 else 1.0)
                        return times_tok(dve, v[:, :, (i - 16) * 256:(i - 15) * 256], o)

                    project([Part("da_qk", "f", xn.at, DC, 16), Part("da_v", "t", xn.at, DC, 4, 256)], leave,
                            inverses=[Inverse(D, tok=inv_tok)])
                    lam, d_step = semaphores("lambda", "lam_step")
                    g_sub = s2("subln_gain", [P, 1])
                    with block() as b:
                        @b.vector
                        def _(dve):
                            steps = Steps(d_step)
                            at, _ = VECS["lam"]
                            dve.tensor_tensor(prod[:, :], vecs[0:64, at:at + 4:2], vecs[0:64, at + 1:at + 4:2], ALU.mult).then_inc(lam, 1)
                            dve.tensor_scalar(g_sub[:, :], vec("subln"), 1.0 - LAM_INIT, None, ALU.mult)
                            dve.wait_ge(lam, 3)
                            for i in range(2):
                                steps.step(dve, dve.tensor_tensor(neg_lam[:, i:i + 1], ex[:, 1:2], ex[:, 0:1], ALU.subtract))
                            dve.tensor_scalar(neg_lam[:, :], neg_lam[:, :], LAM_INIT, None, ALU.subtract)

                        @b.tensor
                        def _(pe):
                            pe.wait_ge(lam, 1)
                            pe.matmul(bank[0][:, 0:2], ones[0:64, :], prod[:, :], start=True, stop=True).then_inc(lam, 1)

                        @b.scalar
                        def _(act):
                            act.wait_ge(lam, 2)
                            act.activation(ex[:, :], bank[0][:, 0:2], ACT.Exp).then_inc(lam, 1)
                    oT = s2("heads_out", [P, DC, T])
                    on = pair(s2, "subln", DC)
                    jobs = []
                    for hd in range(DA_HEADS):
                        for i in range(2):
                            r = 64 * i
                            jobs.append(dict(
                                scores=[(qk[r:r + 64, hd, :], qk[r:r + 64, 8 + hd, :])], add=const("mask"),
                                coef=neg_lam[:, :] if i else None, first=i == 0, last=i == 1, evict=i == 1,
                                outs=[(hd, 0, P, lambda kb, hd=hd: v[:, kb, hd * P:(hd + 1) * P])]))
                    attention(jobs, on)
                    with block() as b:
                        @b.vector
                        def _(dve):
                            dve.tensor_tensor(oT[:, :, :], on.hi[:, :, :].bitcast(F32), on.lo[:, :, :].bitcast(F32), ALU.add)
                    norm_groups(oT, on, lambda c: g_sub[:, :], 1, DA_HEADS, 1e-5)

                    def leave(dve, steps, i, o, posted):
                        if i < DC:
                            return times(dve, gate[:, i, :], o)
                        if i == DC:
                            dve.wait_ge(posted, DC)
                        return dve.tensor_tensor(mixed[:, i - DC, :], o, gate[:, i - DC, :], ALU.mult)

                    def post(act, i, left, posted):
                        if i < DC:
                            act.wait_ge(left, i + 1)
                            act.activation(gate[:, i, :], gate[:, i, :], ACT.Sigmoid, bias=vec("b_gate", i)).then_inc(posted, 1)

                    project([Part("gate_a", "f", xn.at, DC, DC), Part("br_attn", "f", on.at, DC, DC)], leave, post=post)
                y = s("y", [P, SC, T])
                ssd(y)
                yn = pair(s, "y", SC)
                with scope() as s2:
                    gate = s2("gate", [P, DC, T])
                    tmp = s2("tmp", [P, 2, T])
                    zt = s2("z", [P, 2, T])

                    def leave(dve, steps, i, o, posted):
                        if i >= 2:
                            dve.wait_ge(posted, i - 1)
                        if i >= SC:
                            return times(dve, gate[:, i - SC, :], o)
                        return times(dve, tmp[:, i % 2, :], o)

                    def post(act, i, left, posted):
                        act.wait_ge(left, i + 1)
                        if i >= SC:
                            act.activation(gate[:, i - SC, :], gate[:, i - SC, :], ACT.Sigmoid,
                                           bias=vec("b_gate", DC + i - SC)).then_inc(posted, 1)
                            return
                        if i >= 2:
                            act.wait_ge(multiplied, i - 1)
                        act.activation(zt[:, i % 2, :], tmp[:, i % 2, :], ACT.Silu).then_inc(posted, 1)

                    multiplied, posted_all = semaphores("multiplied", "posted_z")

                    def later(dve, steps, i, left):
                        if i < SC:
                            dve.wait_ge(later.posted, i + 1)
                            dve.tensor_tensor(y[:, i, :], y[:, i, :], zt[:, i % 2, :], ALU.mult).then_inc(multiplied, 1)

                    def leave_z(dve, steps, i, o, posted):
                        later.posted = posted
                        return leave(dve, steps, i, o, posted)

                    project([Part("z", "f", xn.at, DC, SC), Part("gate_s", "f", xn.at, DC, DC)], leave_z, post=post, later=later)
                    norm_groups(y, yn, lambda c: vec("ssd_g", c), SC // SSD_GROUPS, SSD_GROUPS, 1e-5)
                    mp = pair(s2, "mixed", DC)
                    hi_done, lo_tmp = semaphores("mixed_hi", "mixed_ready")

                    def leave(dve, steps, i, o, posted):
                        if i >= 2:
                            dve.wait_ge(steps.left, i - 1)
                        steps.step(dve, dve.tensor_tensor(tmp[:, i % 2, :], o, gate[:, i, :], ALU.mult))
                        return dve.tensor_tensor(mixed[:, i, :], mixed[:, i, :], tmp[:, i % 2, :], ALU.add)

                    def post(act, i, left, posted):
                        act.wait_ge(left, i + 1)
                        act.activation(mp.hi[:, i, :], mixed[:, i, :], ACT.Copy).then_inc(hi_done, 1)

                    def later(dve, steps, i, left):
                        dve.wait_ge(hi_done, i + 1)
                        dve.tensor_tensor(mp.lo[:, i, :], mixed[:, i, :], mp.hi[:, i, :].bitcast(F32), ALU.subtract)

                    project([Part("br_ssd", "f", yn.at, SC, DC)], leave, post=post, later=later)
                    project([Part("mix_out", "f", mp.at, DC, DC)], lambda dve, steps, i, o, posted: dve.tensor_copy(y[:, i, :], o),
                            tail=Tail(), tail_src=lambda i: y[:, i, :])
                add_normed(y, gain("mix_post"), 1.0, next_gain)

        def ssd(y):
            xs = y
            with scope() as s:
                bcT = s("b_and_c", [P, 2 * SSD_GROUPS, T])
                dt_raw = s("dt_raw", [P, 2, SSD_HEADS])
                with scope() as s2:
                    padded = s2("padded", [P, 2, CONV - 1 + T])
                    acc = s2("conv", [P, 2, T])
                    pad, tapped, conv, fin = semaphores("pad", "tapped", "conv", "conv_out")

                    def pool(eng):
                        eng.memset(padded[:, :, :], 0.0).then_inc(pad, 1)

                    def leave(dve, steps, i, o, posted):
                        if i == XBC:
                            return times_tok(dve, dt_raw, o)
                        if i == 0:
                            dve.wait_ge(pad, 1)
                        if i >= 2:
                            dve.wait_ge(conv, i - 1)
                        return times(dve, padded[:, i % 2, CONV - 1:], o)

                    def post(act, i, left, posted):
                        if i < XBC:
                            act.wait_ge(left, i + 1)
                            if i >= 2:
                                act.wait_ge(fin, i - 1)
                            act.activation(acc[:, i % 2, :], padded[:, i % 2, 0:T], ACT.Identity,
                                           scale=vec("conv_w", i * CONV), bias=vec("conv_b", i)).then_inc(tapped, 1)
                        if 1 <= i:
                            k = i - 1
                            act.wait_ge(conv, k + 1)
                            act.activation(xs[:, k, :] if k < SC else bcT[:, k - SC, :], acc[:, k % 2, :], ACT.Silu).then_inc(fin, 1)

                    def later(dve, steps, i, left):
                        if i >= XBC:
                            return
                        a = acc[:, i % 2, :]
                        dve.wait_ge(tapped, i + 1)
                        dve.wait_ge(left, i + 1)
                        for tap in range(1, CONV):
                            last = dve.scalar_tensor_tensor(out=a, in0=padded[:, i % 2, tap:tap + T],
                                                            scalar=vec("conv_w", i * CONV + tap), in1=a, op0=ALU.mult, op1=ALU.add)
                            if tap < CONV - 1:
                                steps.step(dve, last)
                        last.then_inc(conv, 1)

                    project([Part("xbc", "f", xn.at, DC, XBC), Part("dt", "t", xn.at, DC, 1, SSD_HEADS)], leave,
                            post=post, later=later, pool=pool)
                scan(s, xs, y, bcT, dt_raw)

        def scan(s, xs, y, bcT, dt_raw):
            H = SSD_HEADS
            xt = s("x_tokens", [P, 2, SSD_INNER])
            bt = s("b_tokens", [P, SSD_GROUPS, P])
            dt = s("dt", [P, 2, H])
            adt = s("a_dt", [P, 2, H])
            neg_cs = s("neg_cumsum", [P, 2, H])
            decay = s("decay", [P, H])
            cbm = s("masked_cb", [P, 2, SSD_GROUPS, P])
            st = s("states", [P, SSD_INNER])
            u = s("tmp", [P, 2, 2, H])
            a_neg = s("a", [P, H])
            step_a, step_d, dt_ok, cs_ok, tr, cp, cb_ok, stt = semaphores(
                "ssd_a", "ssd_d", "dt_ok", "cs_ok", "x_turned", "x_copied", "cb_ok", "state")
            spread = lambda t: bass.AP(t.tensor, t.offset, [t.ap[0], [0, 2], [1, H]])
            with block() as b:
                @b.scalar
                def _(act):
                    steps = Steps(step_a)
                    steps.step(act, act.activation(a_neg[:, :], vec("A_log", 0, H), ACT.Exp))
                    act.wait_ge(dt_ok, 1)
                    steps.step(act, act.activation(u[:, 1], u[:, 1], ACT.Exp))
                    act.activation(u[:, 1], u[:, 1], ACT.Ln, bias=1.0).then_inc(dt_ok, 1)
                    act.wait_ge(cs_ok, 2)
                    act.activation(decay[:, :], decay[:, :], ACT.Exp).then_inc(cs_ok, 1)

                @b.vector
                def _(dve):
                    steps = Steps(step_d)
                    steps.step(dve, dve.tensor_tensor(dt_raw[:, :, :], dt_raw[:, :, :], spread(vec("dt_bias", 0, H)), ALU.add))
                    steps.step(dve, dve.tensor_scalar(u[:, 0], dt_raw[:, :, :], -1.0, None, ALU.mult))
                    dve.tensor_tensor(u[:, 1], u[:, 0], dt_raw[:, :, :], ALU.min).then_inc(dt_ok, 1)
                    dve.wait_ge(dt_ok, 2)
                    steps.step(dve, dve.scalar_tensor_tensor(out=dt[:, :, :], in0=dt_raw[:, :, :], scalar=0.0, in1=u[:, 1],
                                                             op0=ALU.max, op1=ALU.add))
                    dve.wait_ge(step_a, 1)
                    dve.scalar_tensor_tensor(out=adt[:, :, :], in0=dt[:, :, :], scalar=-1.0, in1=spread(a_neg[:, :]),
                                             op0=ALU.mult, op1=ALU.mult).then_inc(dt_ok, 1)
                    dve.wait_ge(cs_ok, 1)
                    steps.step(dve, dve.tensor_scalar(neg_cs[:, :, :], bank[7][:, 0:2 * H].rearrange("p (t c) -> p t c", t=2), -1.0, None, ALU.mult))
                    dve.tensor_tensor(decay[:, :], bank[7][:, 2 * H:3 * H], neg_cs[:, 0, :], ALU.add).then_inc(cs_ok, 1)
                    dt_wide = dt[:, :, :].rearrange("p t (h o) -> p t h o", o=1)
                    heads = lambda t: t.rearrange("p (h d) -> p h d", d=SSD_P)
                    for j in range(8):
                        t, c4 = divmod(j, 4)
                        dve.wait_ge(tr, j + 1)
                        dve.tensor_tensor(heads(xt[:, t, c4 * 512:(c4 + 1) * 512]), heads(bank[j % 4][:, :]),
                                          dt_wide[:, t, c4 * 8:(c4 + 1) * 8, :].to_broadcast([P, 8, SSD_P]), ALU.mult).then_inc(cp, 1)
                    dve.wait_ge(tr, 9)
                    dve.tensor_copy(bt[:, :, :], bank[4][:, :].rearrange("p (g c) -> p g c", g=4)).then_inc(cp, 1)
                    for t in range(2):
                        dve.wait_ge(cb_ok, t + 1)
                        tri_w = bass.AP(tri.tensor, tri.offset, [tri.ap[0], [0, SSD_GROUPS], [1, P]])
                        dve.tensor_tensor(cbm[:, t, :, :], bank[5 + t][:, :].rearrange("p (g c) -> p g c", g=4), tri_w, ALU.mult)
                    dve.wait_ge(cs_ok, 3)
                    dve.wait_ge(cp, 9)
                    dec = decay[:, :].rearrange("p (h o) -> p h o", o=1)
                    dve.tensor_tensor(heads(st[:, :]), heads(xt[:, 0, :]), dec.to_broadcast([P, H, SSD_P]), ALU.mult).then_inc(stt, 1)
                    dve.wait_ge(stt, 5)
                    for g in range(SSD_GROUPS):
                        dve.tensor_copy(st[:, g * 512:(g + 1) * 512], bank[g][:, :])

                @b.tensor
                def _(pe):
                    for j in range(8):
                        t, c4 = divmod(j, 4)
                        if j >= 4:
                            pe.wait_ge(cp, j - 3)
                        for i in range(4):
                            last = pe.transpose(bank[j % 4][:, i * P:(i + 1) * P], xs[:, 4 * c4 + i, t * P:(t + 1) * P], ident)
                        last.then_inc(tr, 1)
                        if j == 3:
                            pe.wait_ge(dt_ok, 3)
                            for t2 in range(2):
                                pe.matmul(bank[7][:, t2 * H:(t2 + 1) * H], tri, adt[:, t2, :], start=True, stop=True)
                            pe.matmul(bank[7][:, 2 * H:3 * H], ones, adt[:, 0, :], start=True, stop=True).then_inc(cs_ok, 1)
                    for g in range(SSD_GROUPS):
                        last = pe.transpose(bank[4][:, g * P:(g + 1) * P], bcT[:, g, 0:P], ident)
                    last.then_inc(tr, 1)
                    for t in range(2):
                        for g in range(SSD_GROUPS):
                            last = pe.matmul(bank[5 + t][:, g * P:(g + 1) * P], bcT[:, g, t * P:(t + 1) * P],
                                             bcT[:, SSD_GROUPS + g, t * P:(t + 1) * P], start=True, stop=True)
                        last.then_inc(cb_ok, 1)
                    pe.wait_ge(cp, 9)
                    pe.wait_ge(stt, 1)
                    for g in range(SSD_GROUPS):
                        pe.matmul(bank[g][:, :], bt[:, g, :], st[:, g * 512:(g + 1) * 512], start=True, stop=True).then_inc(stt, 1)
            Q, NB = 4, 3
            seg_ok, seg_min, l_ok, m_ok, y_ok, y_out, carry = semaphores(
                "seg_ok", "seg_min", "l_ok", "m_ok", "y_ok", "y_out", "carry")
            seg = s("segments", [P, NB, 2, Q, P])
            cs1 = s("carried_c", [P, NB, Q, P])
            quads = H // Q
            with block() as b:
                @b.tensor
                def _(pe):
                    def sums(k):
                        if k >= 2:
                            pe.wait_ge(seg_min, 8 * (k - 1))
                            pe.wait_ge(carry, k - 1)
                        for t in range(2):
                            for i in range(Q):
                                a = adt[:, t, Q * k + i:Q * k + i + 1]
                                col = bass.AP(a.tensor, a.offset, [a.ap[0], [0, P]])
                                last = pe.matmul(bank[2 * (k % 2) + t][:, i * P:(i + 1) * P], col, tri, start=True, stop=True)
                        last.then_inc(seg_ok, 1)

                    def outputs(k):
                        pe.wait_ge(m_ok, 2 * (k + 1))
                        if k >= 2:
                            pe.wait_ge(y_out, 2 * (k - 1))
                        for i in range(Q):
                            hd = Q * k + i
                            r = 64 * (i % 2)
                            o = bank[4 + 2 * (k % 2) + i // 2]
                            cols = slice(hd * SSD_P, (hd + 1) * SSD_P)
                            pe.matmul(o[r:r + 64, 0:P], xt[:, 0, cols], seg[:, k % NB, 0, i, :], start=True, stop=True)
                            pe.matmul(o[r:r + 64, P:T], xt[:, 1, cols], seg[:, k % NB, 1, i, :], start=True, stop=False)
                            last = pe.matmul(o[r:r + 64, P:T], st[:, cols], cs1[:, k % NB, i, :], start=False, stop=True)
                        last.then_inc(y_ok, 1)

                    for k in range(quads + 2):
                        if k < quads:
                            sums(k)
                        if k >= 2:
                            outputs(k - 2)

                @b.vector
                def _(dve):
                    def minus(k):
                        dve.wait_ge(seg_ok, k + 1)
                        if k >= NB:
                            dve.wait_ge(y_ok, k - NB + 1)
                        for t in range(2):
                            if t == 1:
                                dve.wait_ge(carry, k + 1)
                            for i in range(Q):
                                hd = Q * k + i
                                dve.tensor_scalar(seg[:, k % NB, t, i, :], bank[2 * (k % 2) + t][:, i * P:(i + 1) * P],
                                                  neg_cs[:, t, hd:hd + 1], 0.0, ALU.add, ALU.min).then_inc(seg_min, 1)

                    def masked(k):
                        dve.wait_ge(l_ok, k + 1)
                        g = k // 2
                        for t in range(2):
                            cb = cbm[:, t, g, :]
                            wide = bass.AP(cb.tensor, cb.offset, [cb.ap[0], [0, Q], [1, P]])
                            last = dve.tensor_tensor(seg[:, k % NB, t, :, :], seg[:, k % NB, t, :, :], wide, ALU.mult)
                        last.then_inc(m_ok, 1)
                        c = bcT[:, SSD_GROUPS + g, P:T]
                        wide = bass.AP(c.tensor, c.offset, [c.ap[0], [0, Q], [1, P]])
                        dve.tensor_tensor(cs1[:, k % NB, :, :], cs1[:, k % NB, :, :], wide, ALU.mult).then_inc(m_ok, 1)

                    def leave(k):
                        dve.wait_ge(y_ok, k + 1)
                        for i in range(2):
                            c = 2 * k + i
                            dve.scalar_tensor_tensor(out=y[:, c, :], in0=xs[:, c, :], scalar=vec("ssd_D", c),
                                                     in1=bank[4 + 2 * (k % 2) + i][:, 0:T], op0=ALU.mult,
                                                     op1=ALU.add).then_inc(y_out, 1)

                    for k in range(quads + 3):
                        if k < quads:
                            minus(k)
                        if 0 <= k - 1 < quads:
                            masked(k - 1)
                        if 0 <= k - 3 < quads:
                            leave(k - 3)

                @b.scalar
                def _(act):
                    for k in range(quads):
                        act.wait_ge(seg_ok, k + 1)
                        if k >= NB:
                            act.wait_ge(y_ok, k - NB + 1)
                        act.activation(cs1[:, k % NB, :, :], bank[2 * (k % 2) + 1][:, :].rearrange("p (i c) -> p i c", i=Q),
                                       ACT.Exp).then_inc(carry, 1)
                        act.wait_ge(seg_min, 8 * (k + 1))
                        act.activation(seg[:, k % NB, :, :, :], seg[:, k % NB, :, :, :], ACT.Exp).then_inc(l_ok, 1)

        def cross_attention(next_gain):
            with scope() as s:
                q = s("q", [P, DC, T])
                k = s("k", [P, DC, T])
                v = s("v", [P, 2, D])
                with scope() as s2:
                    mem = s2("memory", [P, DC, T])
                    mn = pair(s2, "memory", DC)
                    m_in, = semaphores("memory_in")

                    def sp_first(sp):
                        sp.dma_start(mem[:, :, :], w["memT"]).then_inc(m_in, 16)
                        sp.wait_ge(m_in, 16)

                    project([Part("xa_q", "f", xn.at, DC, DC)],
                            lambda dve, steps, i, o, posted: times(dve, q[:, i, :], o, factor=XA_HEAD_DIM ** -0.5),
                            inverses=[Inverse(D)], sp_first=sp_first)
                    norm_groups(mem, mn, lambda c: vec("mem", c), DC, 1, 1e-6)

                    def leave(dve, steps, i, o, posted):
                        if i < DC:
                            return dve.tensor_copy(k[:, i, :], o)
                        return dve.tensor_copy(v[:, :, (i - DC) * 256:(i - DC + 1) * 256], o)

                    project([Part("xa_k", "f", mn.at, DC, DC), Part("xa_v", "t", mn.at, DC, 4, 256)], leave)
                oT = pair(s, "heads_out", DC)
                y = s("y", [P, DC, T])
                jobs = []
                for hd in range(XA_HEADS):
                    jobs.append(dict(
                        scores=[(q[:, 2 * hd + i, :], k[:, 2 * hd + i, :]) for i in range(2)], add=None,
                        first=True, last=True, evict=True,
                        outs=[(2 * hd + i, 0, P, lambda kb, c=2 * hd + i: v[:, kb, c * P:(c + 1) * P]) for i in range(2)]))
                attention(jobs, oT, causal=False)
                project([Part("xa_o", "f", oT.at, DC, DC)], lambda dve, steps, i, o, posted: dve.tensor_copy(y[:, i, :], o),
                        tail=Tail(), tail_src=lambda i: y[:, i, :])
                add_normed(y, gain("xa_post"), 1.0, next_gain)

        def final_norm(next_gain):
            one, tail = Inverse(D), Tail(next_gain, xn)
            with block() as b:
                @b.tensor
                def _(pe):
                    one.pe(pe)

                @b.scalar
                def _(act):
                    one.act(act)
                    for c in range(DC):
                        tail.act(act, c, h[:, c, :])

                @b.vector
                def _(dve):
                    one.dve(dve)
                    for c in range(DC + 1):
                        if c < DC:
                            dve.scalar_tensor_tensor(out=h[:, c, :], in0=h[:, c, :], scalar=vec("final", c), in1=inv[:, :],
                                                     op0=ALU.mult, op1=ALU.mult).then_inc(tail.given, 1)
                        if c:
                            tail.dve(dve, c - 1, h[:, c - 1, :])

        def ffn_post(name, post, next_gain):
            with scope() as s:
                y = s("ffn_out", [P, DC, T])
                ffn(name, y)
                add_normed(y, gain(post), 0.5, next_gain)

        stages = [
            ("start", start),
            ("ffn_a0", lambda: ffn("ffn_a0", None, gain("mix0"))),
            ("mla", lambda: mla(gain("ffn_b0"))),
            ("ffn_b0", lambda: ffn("ffn_b0", None, gain("ffn_a1"))),
            ("ffn_a1", lambda: ffn("ffn_a1", None, gain("mix1"))),
            ("nsa", lambda: nsa(gain("ffn_b1"))),
            ("ffn_b1", lambda: ffn("ffn_b1")),
            ("final", lambda: final_norm(gain("ffn1_pre"))),
            ("ffn1", lambda: ffn_post("ffn1", "ffn1_post", gain("mix_pre"))),
            ("mix", lambda: two_branches(gain("xa_pre"))),
            ("xa", lambda: cross_attention(gain("ffn2_pre"))),
            ("ffn2", lambda: ffn_post("ffn2", "ffn2_post", None)),
        ]
        for name, stage in stages:
            stage()
            if stop == name and name != "ffn2":
                stored, = semaphores("stored")
                with block() as b:
                    @b.sync
                    def _(sp):
                        sp.dma_start(out, h[:, :, :]).then_inc(stored, 16)
                        sp.wait_ge(stored, 16)
                break
            if name != "ffn2":
                recycle()




def kernel(**inputs):
    import concourse.bacc as bacc
    from concourse.bass_utils import run_bass_kernel_spmd

    nc = bacc.Bacc("TRN2", target_bir_lowering=False, num_devices=1)
    arrays = lay_out({k: np.asarray(v) for k, v in inputs.items()})
    w = {n: nc.dram_tensor(f"in_{n}", a.shape, mybir.dt.from_np(a.dtype), kind="ExternalInput").ap() for n, a in arrays.items()}
    w["scratch"] = nc.dram_tensor("bias_rows", [P, HEADS, T], F32, kind="Internal").ap()
    out = nc.dram_tensor("out_dram", (P, DC, T), F32, kind="ExternalOutput").ap()
    emit(nc, w, out)
    r = run_bass_kernel_spmd(nc, [{f"in_{n}": a for n, a in arrays.items()}], core_ids=[0])
    got = r.results[0]["out_dram"]
    return np.ascontiguousarray(got.transpose(2, 1, 0)).reshape(1, T, D)
```

```python
from contextlib import ExitStack, contextmanager

import numpy as np
import concourse.bass as bass
from concourse import mybir

F32 = mybir.dt.float32
F32R = mybir.dt.float32r
ACT = mybir.ActivationFunctionType
ALU = mybir.AluOpType
AX = mybir.AxisListType

P = 128
T = 256
D = 1024
DC = D // P
FF = 2816
FC = FF // P
HEADS = 16
NEG = -1e30
RAW = 3
CUT = 3
SLOT_TILES = 16
HALF = FC // 2
MLA_Q, MLA_KV, MLA_NOPE, MLA_ROPE, MLA_V = 384, 256, 64, 32, 64
NSA_GROUPS, CMP_BLOCK, CMP_STRIDE = 4, 32, 16
N_CMP = (T - CMP_BLOCK) // CMP_STRIDE + 1
N_CMP0 = (P - CMP_BLOCK) // CMP_STRIDE + 1
REL_BUCKETS, REL_MAX_DIST = 32, 128
TOEP = 2 * T - P - 1
DA_HEADS = 8
SSD_HEADS, SSD_GROUPS, SSD_INNER = 32, 4, 2048
SSD_P = SSD_INNER // SSD_HEADS
SC = SSD_INNER // P
XBC = (SSD_INNER + 2 * SSD_GROUPS * P) // P
CONV = 4
XA_HEADS = 4
LAM_INIT = 0.8 - 0.6
NSA_QK, DA_QK, XA_HEAD_DIM = 64, 64, D // XA_HEADS



def plan():
    ffn = lambda n: [(n + "_gu", FC, 2 * DC, 1), (n + "_dn", 2 * DC, HALF, 1)]
    return (
        ffn("ffn_a0") + [("mla_in", 7, 8, 1), ("mla_uq", 4, 12, 4), ("mla_uk", 1, 16, 8), ("mla_uv", 1, 16, 4),
                         ("mla_o", 4, 16, 2)]
        + ffn("ffn_b0") + ffn("ffn_a1")
        + [("nsa_g", 1, 8, 1), ("nsa_in", 8, 16, 2), ("nsa_v", 2, 16, 1), ("nsa_o", 4, 16, 2)]
        + ffn("ffn_b1") + ffn("ffn1")
        + [("da_qk", 8, 16, 2), ("da_v", 4, 16, 1), ("gate_a", 4, 16, 2), ("br_attn", 4, 16, 2),
           ("xbc", 12, 16, 2), ("dt", 1, 2, 1), ("z", 8, 16, 2), ("gate_s", 4, 16, 2), ("br_ssd", 8, 16, 1), ("mix_out", 4, 16, 2),
           ("xa_q", 4, 16, 2), ("xa_k", 4, 16, 2), ("xa_v", 4, 16, 1), ("xa_o", 4, 16, 2)]
        + ffn("ffn2"))


VECS = {}


def vec_layout():
    at = 0
    for name, n in (("ffn_a0", 8), ("mix0", 8), ("ffn_b0", 8), ("ffn_a1", 8), ("mix1", 8), ("ffn_b1", 8), ("final", 8),
                    ("cq", 3), ("ckv", 2), ("pos_k", 16), ("pos_v", 16),
                    ("ffn1_pre", 8), ("ffn1_post", 8), ("mix_pre", 8), ("mix_post", 8), ("b_gate", 16), ("subln", 1),
                    ("conv_w", XBC * CONV), ("conv_b", XBC), ("ssd_D", SC), ("ssd_g", SC),
                    ("xa_pre", 8), ("xa_post", 8), ("mem", 8), ("ffn2_pre", 8), ("ffn2_post", 8),
                    ("dt_bias", 32), ("A_log", 32), ("lam", 4)):
        VECS[name] = (at, n)
        at += n
    return at


N_VEC = vec_layout()
CONSTS = {}


def const_layout():
    at = 0
    for name, n in (("ident", P), ("ones", P), ("tri", P), ("mask", T), ("cos", T), ("sin", T), ("rotate", T), ("valid", 2 * N_CMP),
                    ("bucket", TOEP)):
        CONSTS[name] = (at, n)
        at += n
    return at


N_CONST = const_layout()


def shape_constants():
    c = np.zeros((P, N_CONST), np.float32)

    def put(name, a):
        at, n = CONSTS[name]
        c[:a.shape[0], at:at + n] = a

    p = np.arange(P)
    put("ident", np.eye(P))
    put("ones", np.ones((P, P)))
    put("tri", p[:, None] <= p[None, :])
    put("mask", np.where(np.arange(T)[None, :] > P + p[:, None], NEG, 0.0))
    half = MLA_ROPE // 2
    inv = np.float32(10000.0) ** (-np.arange(half, dtype=np.float32) * np.float32(2.0 / MLA_ROPE))
    ang = np.arange(T, dtype=np.float32)[:, None] * inv[None, :]
    row = p % half
    sign = np.where(p % MLA_ROPE < half, -1.0, 1.0)[:, None]
    put("cos", np.cos(ang).T[row])
    put("sin", np.sin(ang).T[row] * sign)
    rotate = np.ones((P, T))
    rotate[MLA_NOPE:MLA_NOPE + MLA_ROPE] = np.cos(ang).T[row[:MLA_ROPE]]
    rotate[MLA_NOPE + MLA_ROPE:] = (np.sin(ang).T[row] * sign)[:MLA_ROPE]
    put("rotate", rotate)
    ends = np.arange(N_CMP) * CMP_STRIDE + CMP_BLOCK - 1
    valid = [(q0 + p[:, None] >= ends[None, :]) for q0 in (0, P)]
    put("valid", np.concatenate(valid, axis=1))
    dist = T - 1 - np.arange(TOEP)
    n = np.maximum(dist, 0)
    exact = REL_BUCKETS // 2
    large = exact + (np.log(np.maximum(n, 1).astype(np.float32) / np.float32(exact)) / np.float32(np.log(REL_MAX_DIST / exact))
                     * np.float32(REL_BUCKETS - exact)).astype(np.int32)
    bucket = np.where(n < exact, n, np.minimum(large, REL_BUCKETS - 1))
    hot = np.zeros((REL_BUCKETS + 1, TOEP))
    hot[:REL_BUCKETS] = (bucket[None, :] == np.arange(REL_BUCKETS)[:, None]) & (dist >= 0)
    hot[REL_BUCKETS] = np.where(dist < 0, NEG, 0.0)
    put("bucket", hot)
    return c


def m_major(w, per_block):
    k, m = w.shape[0] // P, w.shape[1] // P
    t = w.reshape(k, P, m // per_block, per_block, P).transpose(2, 1, 3, 0, 4)
    return np.ascontiguousarray(t).reshape(m // per_block, P, per_block * k * P)


def k_major(w, cols):
    k, n = w.shape[0] // P, w.shape[1] // cols
    t = w.reshape(k, P, n, cols).transpose(2, 1, 0, 3)
    return np.ascontiguousarray(t).reshape(n, P, k * cols)


def lay_out(x):
    a = {}

    def ffn(name, g, u, d):
        gu = np.concatenate([g.reshape(D, FC, 1, P), u.reshape(D, FC, 1, P)], axis=2).reshape(D, 2 * FF)
        a[name + "_gu"] = m_major(gu, 2)
        a[name + "_dn"] = np.ascontiguousarray(m_major(d, 1).reshape(DC, P, 2, HALF * P).transpose(0, 2, 1, 3)).reshape(
            2 * DC, P, HALF * P)

    for l in range(2):
        for s in "ab":
            ffn(f"ffn_{s}{l}", x[f"ffn_{s}_w_gate"][l], x[f"ffn_{s}_w_up"][l], x[f"ffn_{s}_w_down"][l])
    for n in ("1", "2"):
        gu = x[f"ffn{n}_w_gu_2"][0]
        ffn(f"ffn{n}", gu[:, :FF], gu[:, FF:], x[f"ffn{n}_w_down_2"][0])
    half = MLA_ROPE // 2
    turned = lambda w: np.concatenate([w[..., half:], w[..., :half]], axis=-1)
    w = x["mla_w_in"][0]
    kr = w[:, MLA_Q + MLA_KV:]
    w = np.concatenate([w[:, :MLA_Q + MLA_KV]] + [kr] * 4 + [turned(kr)] * 4, axis=1)
    a["mla_in"] = m_major(w, 1)
    w = x["mla_w_uq"][0].reshape(MLA_Q, HEADS, MLA_NOPE + MLA_ROPE)
    w = np.concatenate([w, turned(w[:, :, MLA_NOPE:])], axis=2)
    a["mla_uq"] = m_major(w.reshape(MLA_Q, -1), 4)
    w = x["mla_w_ukv"][0].reshape(MLA_KV, HEADS, MLA_NOPE + MLA_V)
    a["mla_uk"] = m_major(w[:, :, :MLA_NOPE].reshape(MLA_KV, -1), 8)
    a["mla_uv"] = k_major(w[:, :, MLA_NOPE:].reshape(MLA_KV, -1), D)
    a["mla_o"] = m_major(x["mla_w_o"][0], 2)
    w = x["nsa_w_in"][0]
    q, kc, vc, ks, vs, kw, vw, g = np.split(w, np.cumsum([D] + [256] * 6), axis=1)
    a["nsa_in"] = m_major(np.concatenate([kc, vc, q, ks, kw], axis=1), 2)
    a["nsa_v"] = k_major(np.concatenate([vs, vw], axis=1), 256)
    a["nsa_g"] = m_major(np.concatenate([g, np.zeros((D, P - g.shape[1]), g.dtype)], axis=1), 1)
    a["nsa_w1"] = np.concatenate([k_major(x["nsa_cmp_w1_k"][0], P), k_major(x["nsa_cmp_w1_v"][0], P)])
    w2k, w2v = x["nsa_cmp_w2_k"][0], x["nsa_cmp_w2_v"][0]
    a["nsa_w2"] = np.concatenate([w2k, w2k, w2v, w2v], axis=1)
    a["nsa_o"] = m_major(x["nsa_w_o"][0], 2)
    w = x["w_in_2"][0]
    q, k, v, z, xbc, dt, gate = np.split(w, np.cumsum([D, D, D, SSD_INNER, XBC * P, SSD_HEADS]), axis=1)
    a["da_qk"] = m_major(np.concatenate([q, k], axis=1), 2)
    a["da_v"] = k_major(v, 256)
    a["gate_a"] = m_major(gate[:, :D], 2)
    a["gate_s"] = m_major(gate[:, D:], 2)
    a["z"] = m_major(z, 2)
    a["xbc"] = m_major(xbc, 2)
    a["dt"] = k_major(dt, SSD_HEADS)
    a["br_attn"] = m_major(x["w_branch_attn_2"][0], 2)
    a["br_ssd"] = m_major(x["w_branch_ssd_2"][0], 1)
    a["mix_out"] = m_major(x["w_mix_out_2"][0], 2)
    a["xa_q"] = m_major(x["xa_w_q_2"][0], 2)
    kv = x["xa_w_kv_2"][0]
    a["xa_k"] = m_major(kv[:, :D], 2)
    a["xa_v"] = k_major(kv[:, D:], 256)
    a["xa_o"] = m_major(x["xa_w_o_2"][0], 2)

    cols = lambda v: v.reshape(-1, P).T
    wide = lambda v: np.broadcast_to(v, (P, v.shape[-1]))
    vec = {
        "ffn_a0": cols(x["ffn_norm_a"][0]), "ffn_a1": cols(x["ffn_norm_a"][1]),
        "mix0": cols(x["mix_norm"][0]), "mix1": cols(x["mix_norm"][1]),
        "ffn_b0": cols(x["ffn_norm_b"][0]), "ffn_b1": cols(x["ffn_norm_b"][1]),
        "final": cols(x["final_norm"]), "cq": cols(x["mla_q_norm"]), "ckv": cols(x["mla_kv_norm"]),
        "pos_k": cols(x["nsa_cmp_pos_k"]), "pos_v": cols(x["nsa_cmp_pos_v"]),
        "ffn1_pre": cols(x["ffn1_pre_g_2"]), "ffn1_post": cols(x["ffn1_post_g_2"]),
        "mix_pre": cols(x["mix_pre_g_2"]), "mix_post": cols(x["mix_post_g_2"]),
        "b_gate": cols(x["b_gate_2"]), "subln": cols(x["da_subln_g_2"]),
        "conv_w": x["ssd_conv_w_2"][0].reshape(CONV, XBC, P).transpose(2, 1, 0).reshape(P, -1),
        "conv_b": cols(x["ssd_conv_b_2"]),
        "ssd_D": cols(np.repeat(x["ssd_D_2"][0], SSD_P)), "ssd_g": cols(x["ssd_norm_g_2"]),
        "xa_pre": cols(x["xa_pre_g_2"]), "xa_post": cols(x["xa_post_g_2"]), "mem": cols(x["mem_norm_g_2"]),
        "ffn2_pre": cols(x["ffn2_pre_g_2"]), "ffn2_post": cols(x["ffn2_post_g_2"]),
        "dt_bias": wide(x["ssd_dt_bias_2"]), "A_log": wide(x["ssd_A_log_2"]),
    }
    vecs = np.zeros((P, N_VEC), np.float32)
    for name, v in vec.items():
        at, n = VECS[name]
        vecs[:, at:at + n] = v
    at = VECS["lam"][0]
    for i, name in enumerate(("q1", "k1", "q2", "k2")):
        vecs[:64, at + i] = x[f"da_lambda_{name}_2"][0]
    a["vecs"] = vecs
    a["consts"] = shape_constants()
    a["rel_bias"] = x["rel_bias"]
    feature_major = lambda v: np.ascontiguousarray(v[0].reshape(T, DC, P).transpose(2, 1, 0))
    a["xT"] = feature_major(x["x"])
    a["memT"] = feature_major(x["mem_2"])
    return a




class Steps:

    def __init__(self, sem):
        self.sem, self.n = sem, 0

    def step(self, engine, instruction):
        self.n += 1
        instruction.then_inc(self.sem, 1)
        engine.wait_ge(self.sem, self.n)


class Ring:

    def __init__(self, nc, ctx, w):
        def tiles(name, dt, n):
            return [ctx.enter_context(nc.sbuf_tensor(f"{name}{s}", [P, SLOT_TILES * P], dt)) for s in range(n)]

        self.raw, self.hi, self.lo = tiles("w_raw", F32, RAW), tiles("w_hi", F32R, CUT), tiles("w_lo", F32R, CUT)
        self.loaded = [ctx.enter_context(nc.semaphore(f"w_loaded{s}")) for s in range(RAW)]
        self.hi_done, self.lo_done, self.mm_done = (
            ctx.enter_context(nc.semaphore(n)) for n in ("w_hi_done", "w_lo_done", "mm_done"))
        self.source, self.first, self.chunk0, self.end, chunks = [], {}, {}, [], 0
        for name, n, tiles, per in plan():
            self.first[name], self.chunk0[name] = len(self.source), chunks
            for i in range(n):
                self.source.append((w[name], i))
                chunks += per
                self.end.append(chunks)
        self.blocks = len(self.source)
        self.left_hi = self.left_lo = None

    def size(self, n):
        return self.source[n][0].shape[2]

    def load(self, sp, n):
        if n >= self.blocks:
            return
        if n >= RAW:
            sp.wait_ge(self.lo_done, n - RAW + 1)
        ap, i = self.source[n]
        sp.dma_start(self.raw[n % RAW][:, 0:self.size(n)], ap[i]).then_inc(self.loaded[n % RAW], 16)

    def cut_hi(self, act, n):
        if n >= self.blocks:
            return
        act.wait_ge(self.loaded[n % RAW], 16 * (n // RAW + 1))
        if n >= CUT:
            act.wait_ge(self.mm_done, self.end[n - CUT])
        act.activation(self.hi[n % CUT][:, 0:self.size(n)], self.raw[n % RAW][:, 0:self.size(n)],
                       ACT.Copy).then_inc(self.hi_done, 1)

    def cut_lo(self, dve, n):
        if n >= self.blocks:
            return
        dve.wait_ge(self.hi_done, n + 1)
        dve.tensor_tensor(self.lo[n % CUT][:, 0:self.size(n)], self.raw[n % RAW][:, 0:self.size(n)],
                          self.hi[n % CUT][:, 0:self.size(n)].bitcast(F32), ALU.subtract).then_inc(self.lo_done, 1)

    def flush_hi(self, act):
        if self.left_hi is not None:
            self.cut_hi(act, self.left_hi)
            self.left_hi = None

    def flush_lo(self, dve):
        if self.left_lo is not None:
            self.cut_lo(dve, self.left_lo)
            self.left_lo = None

    def ready(self, pe, n):
        pe.wait_ge(self.lo_done, n + 1)

    def part(self, n, at, cols=P):
        return self.hi[n % CUT][:, at:at + cols], self.lo[n % CUT][:, at:at + cols]


def product(pe, out, still, moving, start, stop):
    pe.matmul(out, still[0], moving[0], start=start, stop=False)
    pe.matmul(out, still[0], moving[1], start=False, stop=False)
    return pe.matmul(out, still[1], moving[0], start=False, stop=stop)


class Pair:

    def __init__(self, hi, lo):
        self.hi, self.lo = hi, lo

    def at(self, c, t=slice(0, T)):
        return self.hi[:, c, t], self.lo[:, c, t]


def emit(nc, w, out, stop=None):
    root = ExitStack()
    uid = [0]
    in_use = []
    opening = []
    with root:
        def make(ctx):
            def sb(name, shape, dt=F32):
                uid[0] += 1
                return ctx.enter_context(nc.sbuf_tensor(f"{name}_{uid[0]}", shape, dt))
            return sb

        @contextmanager
        def scope():
            with ExitStack() as c:
                yield make(c)

        def semaphores(*names):
            uid[0] += 1
            new = [nc.alloc_semaphore(name=f"{n}_{uid[0]}") for n in names]
            in_use.extend(new)
            return new

        def recycle():
            if len(in_use) < MANY:
                return
            kept = [x for o in opening for x in o.semaphores]
            nc.clear_and_free_semaphores([x for x in in_use if x not in kept])
            nc.all_engine_barrier()
            in_use[:] = kept

        MANY = 80

        def block():
            return nc.Block(no_gpsimd_drain=True)

        ring = Ring(nc, root, w)
        mm_done = ring.mm_done
        sb = make(root)
        pair = lambda s, name, n: Pair(s(name + "_hi", [P, n, T], F32R), s(name + "_lo", [P, n, T], F32R))
        h = sb("residual", [P, DC, T])
        y8 = sb("layer_out", [P, DC, T])
        xn = pair(sb, "x", DC)
        sq = sb("squares", [P, 2, T])
        h_sum = sb("sum_of_squares", [P, T])
        inv = sb("inverse_rms", [P, T])
        inv_tok = sb("inverse_rms_tokens", [P, 2])
        root_t = sb("rms", [P, T + 2])
        vecs = sb("vecs", [P, N_VEC])
        consts = sb("consts", [P, N_CONST])
        eps_t = sb("eps", [P, 2])
        EPS = {1e-6: eps_t[:, 0:1], 1e-5: eps_t[:, 1:2]}
        bank = [root.enter_context(nc.psum_tensor(f"bank{i}", [P, 512], F32)) for i in range(8)]

        def const(name):
            at, n = CONSTS[name]
            return consts[:, at:at + n]

        def vec(name, i=0, n=1):
            at, _ = VECS[name]
            return vecs[:, at + i:at + i + n]

        ident, tri = const("ident"), const("tri")
        ones = sb("ones", [P, P])[:, :]
        consts_in = root.enter_context(nc.semaphore("consts_in"))

        class Tail:

            def __init__(self, gain=None, dst=None, total=h_sum, offset=0, squares=sq):
                self.gain, self.dst, self.total, self.offset, self.sq = gain, dst, total, offset, squares
                self.semaphores = self.given, self.hi, self.added = semaphores("given", "tail_hi", "added")

            def need(self, pe, c):
                pe.wait_ge(self.added, c + 1)

            def act(self, act, m, src):
                act.wait_ge(self.given, m + 1)
                if m >= 2:
                    act.wait_ge(self.added, m - 1)
                last = act.activation(self.sq[:, m % 2, :], src, ACT.Square)
                if self.gain:
                    last = act.activation(self.dst.hi[:, m + self.offset, :], src, ACT.Copy, scale=self.gain(m))
                last.then_inc(self.hi, 1)

            def dve(self, dve, m, src):
                dve.wait_ge(self.hi, m + 1)
                if self.gain:
                    dve.scalar_tensor_tensor(out=self.dst.lo[:, m + self.offset, :], in0=src, scalar=self.gain(m),
                                             in1=self.dst.hi[:, m + self.offset, :].bitcast(F32), op0=ALU.mult,
                                             op1=ALU.subtract)
                if m == 0:
                    dve.tensor_copy(self.total[:, :], self.sq[:, 0, :]).then_inc(self.added, 1)
                else:
                    dve.wait_ge(self.added, m)
                    dve.tensor_tensor(self.total[:, :], self.total[:, :], self.sq[:, m % 2, :], ALU.add).then_inc(self.added, 1)

        class Inverse:

            def __init__(self, n, eps=1e-6, total=h_sum, out=inv, tok=None, b=7):
                self.n, self.eps, self.total, self.out, self.tok, self.bank = n, eps, total, out, tok, bank[b]
                self.root = root_t
                self.semaphores = self.summed, self.rooted, self.inverted = semaphores("summed", "rooted", "inverted")

            def pe(self, pe):
                last = pe.matmul(self.bank[:, 0:T], ones, self.total[:, :], start=True, stop=True)
                if self.tok is not None:
                    for t in range(2):
                        last = pe.matmul(self.bank[:, T + t:T + t + 1], self.total[:, t * P:(t + 1) * P], ones[:, 0:1],
                                         start=True, stop=True)
                last.then_inc(self.summed, 1)

            def act(self, act, used=None):
                act.wait_ge(self.summed, 1)
                if used:
                    act.wait_ge(used, 1)
                n = T if self.tok is None else T + 2
                act.activation(self.root[:, 0:n], self.bank[:, 0:n], ACT.Sqrt, bias=EPS[self.eps],
                               scale=1.0 / self.n).then_inc(self.rooted, 1)

            def dve(self, dve):
                dve.wait_ge(self.rooted, 1)
                last = dve.reciprocal(self.out[:, :], self.root[:, 0:T])
                if self.tok is not None:
                    last = dve.reciprocal(self.tok[:, :], self.root[:, T:T + 2])
                last.then_inc(self.inverted, 1)
                dve.wait_ge(self.inverted, 1)

        class LastTail:

            def __init__(self, tail, m, src):
                self.tail, self.m, self.src = tail, m, src
                self.semaphores = tail.semaphores

            def pe(self, pe):
                pass

            def act(self, act):
                self.tail.act(act, self.m, self.src)

            def dve(self, dve):
                self.tail.dve(dve, self.m, self.src)

        class AddNormed:

            def __init__(self, before, gain, factor, next_gain):
                self.before, self.gain, self.factor = before, gain, factor
                self.one, self.tail = Inverse(D), Tail(next_gain, xn)
                self.normed, = semaphores("normed")
                self.semaphores = [*before.semaphores, *self.one.semaphores, *self.tail.semaphores, self.normed]

            def pe(self, pe):
                self.before.need(pe, DC - 1)
                self.one.pe(pe)

            def act(self, act):
                self.one.act(act)
                ring.flush_hi(act)
                for c in range(DC):
                    self.tail.act(act, c, h[:, c, :])

            def dve(self, dve):
                ring.flush_lo(dve)
                self.one.dve(dve)
                for c in range(DC + 2):
                    if c < DC:
                        dve.scalar_tensor_tensor(out=y8[:, c, :], in0=y8[:, c, :], scalar=self.gain(c), in1=inv[:, :],
                                                 op0=ALU.mult, op1=ALU.mult).then_inc(self.normed, 1)
                    if 0 <= c - 1 < DC:
                        dve.wait_ge(self.normed, c)
                        dve.scalar_tensor_tensor(out=h[:, c - 1, :], in0=y8[:, c - 1, :], scalar=self.factor,
                                                 in1=h[:, c - 1, :], op0=ALU.mult, op1=ALU.add).then_inc(self.tail.given, 1)
                    if c >= 2:
                        self.tail.dve(dve, c - 2, h[:, c - 2, :])

        class FinalNorm(AddNormed):

            def dve(self, dve):
                ring.flush_lo(dve)
                self.one.dve(dve)
                for c in range(DC + 1):
                    if c < DC:
                        dve.scalar_tensor_tensor(out=h[:, c, :], in0=h[:, c, :], scalar=self.gain(c), in1=inv[:, :],
                                                 op0=ALU.mult, op1=ALU.mult).then_inc(self.tail.given, 1)
                    if c:
                        self.tail.dve(dve, c - 1, h[:, c - 1, :])
                dve.wait_ge(self.tail.given, DC)

        def take_opening():
            taken = list(opening)
            opening.clear()
            return taken, (taken[-1].tail if taken else None)

        def finish_opening():
            taken, _ = take_opening()
            with block() as b:
                @b.tensor
                def _(pe):
                    for o in taken:
                        o.pe(pe)

                @b.scalar
                def _(act):
                    for o in taken:
                        o.act(act)

                @b.vector
                def _(dve):
                    for o in taken:
                        o.dve(dve)

        class Part:

            def __init__(self, name, kind, x, k, chunks, cols=T, need=None):
                self.name, self.kind, self.x, self.k, self.chunks, self.cols = name, kind, x, k, chunks, cols
                self.need = need

            def run(self, pe, j, psum, need=None):
                need = need or self.need
                chunk = ring.chunk0[self.name] + j
                n = next(i for i in range(ring.first[self.name], ring.blocks) if ring.end[i] > chunk)
                start = ring.end[n - 1] if n else 0
                per = ring.end[n] - start
                if chunk == start:
                    ring.ready(pe, n)
                if self.kind == "f":
                    for c in range(self.k):
                        if need and j == 0:
                            need(pe, c)
                        last = product(pe, psum[:, 0:T], ring.part(n, ((chunk - start) * self.k + c) * P), self.x(c),
                                       c == 0, c == self.k - 1)
                    return last
                for c in range(self.k if need and j == 0 else 0):
                    need(pe, c)
                for t in range(2):
                    for c in range(self.k):
                        at = (c * per + chunk - start) * self.cols
                        hi, lo = self.x(c)
                        last = product(pe, psum[:, t * self.cols:(t + 1) * self.cols],
                                       (hi[:, t * P:(t + 1) * P], lo[:, t * P:(t + 1) * P]),
                                       ring.part(n, at, self.cols), c == 0, c == self.k - 1)
                return last

            def abreast(self, pe, n, need, inverses):
                first, chunk0 = ring.first[self.name], ring.chunk0[self.name]
                per = ring.end[first] - chunk0
                for b in range(-(-n // per)):
                    ring.ready(pe, first + b)
                for c in range(self.k):
                    need(pe, c)
                    for v in inverses if c == self.k - 1 else ():
                        v.pe(pe)
                    for j in range(n):
                        last = product(pe, bank[j][:, 0:T], ring.part(first + j // per, (j % per * self.k + c) * P), self.x(c),
                                       c == 0, c == self.k - 1)
                        if c == self.k - 1:
                            last.then_inc(mm_done, 1)

            def view(self, psum):
                if self.kind == "f":
                    return psum[:, 0:T]
                return psum[:, 0:2 * self.cols].rearrange("p (t c) -> p t c", t=2)

        def project(parts, leave, inverses=(), post=None, later=None, tail=None, tail_src=None, sp_first=None,
                    pe_first=None, act_first=None, pool=None, between=None):
            pe_at, act_at, dve_at = between or ({}, {}, {})
            taken, x_tail = take_opening()
            chunks = [(p, j) for p in parts for j in range(p.chunks)]
            c0 = ring.chunk0[parts[0].name]
            ends = {ring.end[n] - c0 - 1: n for n in range(ring.blocks)}
            left, posted, step_d = semaphores("left", "posted", "step")
            project.left, project.posted = left, posted
            tails = tail if isinstance(tail, dict) else {i: (tail, i) for i in range(len(chunks))} if tail else {}
            first_n = ring.first[parts[0].name]
            end = len(chunks) - 1
            last_n = ends[end]
            with block() as b:
                @b.sync
                def _(sp):
                    if sp_first:
                        sp_first(sp)
                    for n in range(first_n + RAW, last_n + RAW + 1):
                        ring.load(sp, n)

                if pool:
                    @b.gpsimd
                    def _(eng):
                        pool(eng)

                @b.tensor
                def _(pe):
                    if pe_first:
                        pe_first(pe)
                    for o in taken:
                        o.pe(pe)
                    side = 0
                    if len(taken) > 1:
                        side = min(3, ring.end[first_n + 1] - c0)
                        parts[0].abreast(pe, side, x_tail.need, inverses)
                    elif taken:
                        parts[0].run(pe, 0, bank[0], x_tail.need).then_inc(mm_done, 1)
                        side = 1
                    for v in inverses if len(taken) < 2 else ():
                        v.pe(pe)
                    for i, (p, j) in enumerate(chunks):
                        if i < side:
                            continue
                        if i >= 4:
                            pe.wait_ge(left, i - 3)
                        for work in pe_at.get(i, ()):
                            work(pe)
                        p.run(pe, j, bank[i % 4]).then_inc(mm_done, 1)
                    for work in pe_at.get(end + 1, ()):
                        work(pe)

                @b.scalar
                def _(act):
                    for o in taken:
                        o.act(act)
                    ring.flush_hi(act)
                    for k, v in enumerate(inverses):
                        v.act(act, inverses[k - 1].inverted if k else None)
                    if act_first:
                        act_first(act)
                    for i in range(len(chunks)):
                        if post:
                            post(act, i, left, posted)
                        if i in tails and i < end:
                            t, m = tails[i]
                            t.act(act, m, tail_src(i))
                        if i == len(chunks) - 1:
                            ring.left_hi = ends[i] + CUT
                        elif i in ends:
                            ring.cut_hi(act, ends[i] + CUT)
                        for work in act_at.get(i, ()):
                            work(act)

                @b.vector
                def _(dve):
                    steps = Steps(step_d)
                    steps.left, steps.posted = left, posted
                    for o in taken:
                        o.dve(dve)
                    ring.flush_lo(dve)
                    ring.cut_lo(dve, first_n + CUT - 1)
                    for v in inverses:
                        v.dve(dve)
                    for i, (p, j) in enumerate(chunks):
                        dve.wait_ge(mm_done, c0 + i + 1)
                        last = leave(dve, steps, i, p.view(bank[i % 4]), posted)
                        if i in tails:
                            t, m = tails[i]
                            last.then_inc(t.given, 1)
                            dve.wait_ge(t.given, m + 1)
                            dve.sem_inc(left, 1)
                        else:
                            last.then_inc(left, 1)
                        if later and i >= 1:
                            later(dve, steps, i - 1, left)
                        for work in dve_at.get(i, ()):
                            work(dve)
                        if i == len(chunks) - 1:
                            ring.left_lo = ends[i] + CUT - 1
                        elif i in ends and ends[i] > first_n:
                            ring.cut_lo(dve, ends[i] + CUT - 1)
                        if i - 1 in tails:
                            t, m = tails[i - 1]
                            t.dve(dve, m, tail_src(i - 1))
                    if later:
                        later(dve, steps, len(chunks) - 1, left)
                    if end in tails:
                        opening.append(LastTail(*tails[end], tail_src(end)))

        def ffn(name, y=None, next_gain=None):
            gu0, dn0 = ring.first[name + "_gu"], ring.first[name + "_dn"]
            gu_c, dn_c = ring.chunk0[name + "_gu"], ring.chunk0[name + "_dn"]
            scaled, silu_done, prod_done, hid_hi, hid_lo, out_done = semaphores(
                "scaled", "silu_done", "prod_done", "hid_hi", "hid_lo", "out_done")
            one = Inverse(D)
            taken, x_tail = take_opening()
            dst = h if y is None else y
            tail = Tail(next_gain, xn) if next_gain else Tail()
            N = 3
            size = 2 * DC * P
            hi_i = lambda j: (gu0 + j) % CUT
            raw_i = lambda j: (gu0 + j) % RAW
            with scope() as s:
                gur = s("gate_up", [P, N, 2 * T])
                sg = s("silu", [P, N, T])
                prod = s("product", [P, N, T])
                hh = s("hidden_hi", [P, FC * T], F32R)
                hl = s("hidden_lo", [P, FC * T], F32R)
                with block() as b:
                    @b.sync
                    def _(sp):
                        loads = FC - RAW
                        with sp.Fori(0, loads // RAW) as t:
                            for j in range(RAW):
                                i = t * RAW + j
                                sp.wait_ge(ring.lo_done, i + (gu0 + 1))
                                sp.dma_start(ring.raw[raw_i(j)][:, :],
                                             w[name + "_gu"][bass.ds(i + RAW, 1)].rearrange("a p c -> (a p) c")
                                             ).then_inc(ring.loaded[raw_i(j)], 16)
                        for n in range(gu0 + RAW + loads // RAW * RAW, dn0 + 2 * DC + RAW):
                            ring.load(sp, n)
                        if name == "ffn_a0":
                            sp.wait_ge(consts_in, 16)

                    @b.tensor
                    def _(pe):
                        def gate_up(i, j):
                            pe.wait_ge(ring.lo_done, i + (gu0 + 1))
                            pe.wait_ge(scaled, i + 1)
                            for half in range(2):
                                for c in range(DC):
                                    at = (half * DC + c) * P
                                    last = product(pe, bank[j][:, half * T:half * T + T],
                                                   (ring.hi[hi_i(j)][:, at:at + P], ring.lo[hi_i(j)][:, at:at + P]),
                                                   xn.at(c), c == 0, c == DC - 1)
                            last.then_inc(mm_done, 1)

                        for o in taken:
                            o.pe(pe)

                        def half_block(j, half, c):
                            at = (half * DC + c) * P
                            return product(pe, bank[j][:, half * T:half * T + T],
                                           (ring.hi[hi_i(j)][:, at:at + P], ring.lo[hi_i(j)][:, at:at + P]),
                                           xn.at(c), c == 0, c == DC - 1)

                        side = 2 if len(taken) > 1 else 1
                        for j in range(side):
                            pe.wait_ge(ring.lo_done, j + (gu0 + 1))
                        for c in range(DC):
                            x_tail.need(pe, c)
                            if c == DC - 1:
                                one.pe(pe)
                            for j in range(side):
                                half_block(j, 0, c)
                        for j in range(side):
                            for c in range(DC):
                                last = half_block(j, 1, c)
                            last.then_inc(mm_done, 1)
                        for i in range(side, N):
                            gate_up(i, i)
                        with pe.Fori(1, FC // N) as t:
                            for j in range(N):
                                gate_up(t * N + j, j)
                        for i in range(FC // N * N, FC):
                            gate_up(i, i % N)
                        for m in range(DC):
                            if m >= 2:
                                pe.wait_ge(out_done, m - 1)
                            for half in range(2):
                                n = dn0 + 2 * m + half
                                ring.ready(pe, n)
                                if m == 0:
                                    pe.wait_ge(hid_lo, (half + 1) * HALF)
                                for c in range(HALF):
                                    k = half * HALF + c
                                    last = product(pe, bank[4 + m % 2][:, 0:T], ring.part(n, c * P),
                                                   (hh[:, k * T:(k + 1) * T], hl[:, k * T:(k + 1) * T]),
                                                   k == 0, k == FC - 1)
                                last.then_inc(mm_done, 1)

                    @b.scalar
                    def _(act):
                        def silu(i, j):
                            act.wait_ge(scaled, i + (N + 1))
                            act.wait_ge(prod_done, i + 1)
                            act.activation(sg[:, j, :], gur[:, j, 0:T], ACT.Silu).then_inc(silu_done, 1)

                        def hidden_hi(i, j):
                            act.wait_ge(prod_done, i + (N + 1))
                            act.activation(hh[:, bass.ds(i * T, T)], prod[:, j, :], ACT.Copy).then_inc(hid_hi, 1)

                        for o in taken:
                            o.act(act)
                        ring.flush_hi(act)
                        one.act(act)
                        with act.Fori(0, (FC - CUT) // N) as t:
                            for j in range(N):
                                i = t * N + j
                                silu(i, j)
                                n_loads = (gu0 + CUT + j) // RAW + 1
                                act.wait_ge(ring.loaded[raw_i(j)], t * 16 + 16 * n_loads)
                                act.wait_ge(mm_done, i + (gu_c + 1))
                                act.activation(ring.hi[hi_i(j)][:, 0:size], ring.raw[raw_i(j)][:, 0:size], ACT.Copy
                                               ).then_inc(ring.hi_done, 1)
                                hidden_hi(i, j)
                        for i in range((FC - CUT) // N * N, FC):
                            silu(i, i % N)
                            ring.cut_hi(act, gu0 + i + CUT)
                            hidden_hi(i, i % N)
                        for m in range(DC):
                            ring.cut_hi(act, dn0 + 2 * m + CUT)
                            if m < DC - 1:
                                tail.act(act, m, dst[:, m, :])
                                ring.cut_hi(act, dn0 + 2 * m + 1 + CUT)
                        ring.left_hi = dn0 + 2 * DC - 1 + CUT

                    @b.vector
                    def _(dve):
                        dve.sem_inc(scaled, N)
                        dve.sem_inc(prod_done, N)
                        for o in taken:
                            o.dve(dve)
                        ring.flush_lo(dve)
                        ring.cut_lo(dve, gu0 + CUT - 1)
                        one.dve(dve)
                        r = inv[:, :]
                        twice = bass.AP(r.tensor, r.offset, [r.ap[0], [0, 2], [1, T]])

                        def scale(i, j):
                            dve.wait_ge(mm_done, i + (gu_c + 1))
                            dve.tensor_tensor(gur[:, j, :].rearrange("p (a t) -> p a t", a=2),
                                              bank[j][:, :].rearrange("p (a t) -> p a t", a=2), twice,
                                              ALU.mult).then_inc(scaled, 1)

                        def hidden_lo(i, j):
                            dve.wait_ge(hid_hi, i + 1)
                            dve.tensor_tensor(hl[:, bass.ds(i * T, T)], prod[:, j, :],
                                              hh[:, bass.ds(i * T, T)].bitcast(F32), ALU.subtract).then_inc(hid_lo, 1)

                        def gated(i, j):
                            dve.wait_ge(silu_done, i + 1)
                            dve.tensor_tensor(prod[:, j, :], sg[:, j, :], gur[:, j, T:2 * T], ALU.mult).then_inc(prod_done, 1)

                        def straight(i):
                            scale(i, i % N)
                            if i:
                                hidden_lo(i - 1, (i - 1) % N)
                                ring.cut_lo(dve, gu0 + i + CUT - 1)
                            gated(i, i % N)

                        for i in range(N):
                            straight(i)
                        trips = (FC - CUT) // N
                        with dve.Fori(1, trips) as t:
                            for j in range(N):
                                i = t * N + j
                                scale(i, j)
                                hidden_lo(i - 1, (j - 1) % N)
                                at = (gu0 + j + CUT - 1)
                                dve.wait_ge(ring.hi_done, i + (gu0 + CUT))
                                dve.tensor_tensor(ring.lo[at % CUT][:, 0:size], ring.raw[at % RAW][:, 0:size],
                                                  ring.hi[at % CUT][:, 0:size].bitcast(F32), ALU.subtract
                                                  ).then_inc(ring.lo_done, 1)
                                gated(i, j)
                        for i in range(trips * N, FC):
                            straight(i)
                        hidden_lo(FC - 1, (FC - 1) % N)
                        for m in range(DC):
                            ring.cut_lo(dve, dn0 + 2 * m + CUT - 1)
                            dve.wait_ge(mm_done, dn_c + 2 * m + 2)
                            o = bank[4 + m % 2][:, 0:T]
                            if y is None:
                                dve.scalar_tensor_tensor(out=h[:, m, :], in0=o, scalar=0.5, in1=h[:, m, :],
                                                         op0=ALU.mult, op1=ALU.add).then_inc(tail.given, 1)
                            else:
                                dve.tensor_copy(y[:, m, :], o).then_inc(tail.given, 1)
                            dve.wait_ge(tail.given, m + 1)
                            dve.sem_inc(out_done, 1)
                            if m < DC - 1:
                                ring.cut_lo(dve, dn0 + 2 * m + 1 + CUT - 1)
                                tail.dve(dve, m, dst[:, m, :])
                        opening.append(LastTail(tail, DC - 1, dst[:, DC - 1, :]))
                        ring.left_lo = dn0 + 2 * DC - 1 + CUT - 1

        def add_and_store(y, gain, factor):
            taken, y_tail = take_opening()
            one = Inverse(D)
            normed, out_ready, stored = semaphores("normed", "out_ready", "stored")
            with block() as b:
                @b.tensor
                def _(pe):
                    y_tail.need(pe, DC - 1)
                    one.pe(pe)

                @b.scalar
                def _(act):
                    for o in taken:
                        o.act(act)
                    one.act(act)

                @b.vector
                def _(dve):
                    for o in taken:
                        o.dve(dve)
                    one.dve(dve)

                    def add(c):
                        dve.wait_ge(normed, c + 1)
                        dve.scalar_tensor_tensor(out=h[:, c, :], in0=y[:, c, :], scalar=factor, in1=h[:, c, :],
                                                 op0=ALU.mult, op1=ALU.add).then_inc(out_ready, 1)

                    for c in range(DC + 1):
                        if c < DC:
                            dve.scalar_tensor_tensor(out=y[:, c, :], in0=y[:, c, :], scalar=gain(c), in1=inv[:, :],
                                                     op0=ALU.mult, op1=ALU.mult).then_inc(normed, 1)
                        if 0 <= c - 1 < DC:
                            add(c - 1)

                @b.sync
                def _(sp):
                    for c in range(DC):
                        sp.wait_ge(out_ready, c + 1)
                        sp.dma_start(out[:, c, :], h[:, c, :]).then_inc(stored, 16)
                    sp.wait_ge(stored, 16 * DC)

        class GroupNorm:

            def __init__(self, s, src, dst, gain, chunks, groups, eps, first=0, buffers=8,
                         before=None):
                self.src, self.dst, self.gain, self.chunks, self.groups = src, dst, gain, chunks, groups
                self.eps, self.first, self.n, self.buffers, self.before = eps, first, chunks * groups, buffers, before
                self.sqs = s("group_squares", [P, buffers, T])
                self.tok = s("group_inverse_tokens", [P, 2, groups])
                self.row = s("group_inverse_rows", [groups, T])
                (self.squared, self.summed, self.rooted, self.inverted, self.turned, self.rows, self.spread_, self.scaled,
                 self.hi, self.lo) = semaphores("squared", "summed", "rooted", "inverted", "turned", "rows", "spread",
                                                "scaled", "norm_hi", "norm_lo")

            def square(self, c):
                def act(act):
                    if c >= self.buffers:
                        act.wait_ge(self.summed, c - self.buffers + 1)
                    act.activation(self.sqs[:, c % self.buffers, :], self.src[:, self.first + c, :], ACT.Square
                                   ).then_inc(self.squared, 1)
                return act

            def sums(self, c):
                def pe(pe):
                    pe.wait_ge(self.squared, c + 1)
                    g = c // self.chunks
                    for t in range(2):
                        last = pe.matmul(bank[4 + t][:, g:g + 1], self.sqs[:, c % self.buffers, t * P:(t + 1) * P],
                                         ones[:, 0:1], start=c % self.chunks == 0, stop=c % self.chunks == self.chunks - 1)
                    last.then_inc(self.summed, 1)
                return pe

            def root(self, act):
                act.wait_ge(self.summed, self.n)
                for t in range(2):
                    last = act.activation(self.tok[:, t, :], bank[4 + t][:, 0:self.groups], ACT.Sqrt, bias=EPS[self.eps],
                                          scale=1.0 / (self.chunks * P))
                last.then_inc(self.rooted, 1)

            def invert(self, dve):
                dve.wait_ge(self.rooted, 1)
                dve.reciprocal(self.tok[:, :, :], self.tok[:, :, :]).then_inc(self.inverted, 1)

            def turn(self, pe):
                pe.wait_ge(self.inverted, 1)
                if self.before:
                    pe.wait_ge(self.before.scaled, self.before.n)
                for t in range(2):
                    last = pe.transpose(bank[6][0:self.groups, t * P:(t + 1) * P], self.tok[:, t, :], ident)
                last.then_inc(self.turned, 1)

            def copy(self, act):
                act.wait_ge(self.turned, 1)
                act.activation(self.row[:, :], bank[6][0:self.groups, 0:T], ACT.Copy).then_inc(self.rows, 1)

            def spread(self, g):
                def pe(pe):
                    pe.wait_ge(self.rows, 1)
                    if g >= 2:
                        pe.wait_ge(self.scaled, (g - 1) * self.chunks)
                    r = consts[0:self.groups, CONSTS["ident"][0] + g:CONSTS["ident"][0] + g + 1]
                    pe.matmul(bank[7 - g % 2][:, 0:T], bass.AP(r.tensor, r.offset, [r.ap[0], [0, P]]), self.row[:, :],
                              start=True, stop=True).then_inc(self.spread_, 1)
                return pe

            def scale(self, c):
                def dve(dve):
                    g, at = c // self.chunks, self.first + c
                    dve.wait_ge(self.spread_, g + 1)
                    dve.scalar_tensor_tensor(out=self.src[:, at, :], in0=self.src[:, at, :], scalar=self.gain(at),
                                             in1=bank[7 - g % 2][:, 0:T], op0=ALU.mult, op1=ALU.mult).then_inc(self.scaled, 1)
                    if c >= 2:
                        self.rest(c - 2)(dve)
                return dve

            def cut(self, c):
                def act(act):
                    act.wait_ge(self.scaled, c + 1)
                    act.activation(self.dst.hi[:, self.first + c, :], self.src[:, self.first + c, :], ACT.Copy).then_inc(self.hi, 1)
                return act

            def rest(self, c):
                def dve(dve):
                    at = self.first + c
                    dve.wait_ge(self.hi, c + 1)
                    dve.tensor_tensor(self.dst.lo[:, at, :], self.src[:, at, :], self.dst.hi[:, at, :].bitcast(F32),
                                      ALU.subtract).then_inc(self.lo, 1)
                return dve

            def need(self, pe, c):
                pe.wait_ge(self.lo, c + 1)

            def into(self, between, sums_at, spread_at, per=2):
                pe_at, act_at, dve_at = between
                for c, i in enumerate(sums_at):
                    pe_at.setdefault(i, []).append(self.sums(c))
                last = sums_at[-1]
                act_at.setdefault(last - 1, []).append(self.root)
                dve_at.setdefault(last - 1, []).append(self.invert)
                pe_at.setdefault(last + 1, []).append(self.turn)
                act_at.setdefault(last, []).append(self.copy)
                for c in range(self.n):
                    i = spread_at + c // per
                    if c % self.chunks == 0:
                        pe_at.setdefault(i + 1, []).append(self.spread(c // self.chunks))
                    dve_at.setdefault(i, []).append(self.scale(c))
                    act_at.setdefault(i, []).append(self.cut(c))
                dve_at[i].extend([self.rest(self.n - 2), self.rest(self.n - 1)])

        def attention(jobs, oT, scale=1.0, causal=True, plain=False):
            (s_ready, s_max, exp_done, p_ready, t_ready, pt_ready, v_done, o_ready, o_hi, o_done, d_step) = semaphores(
                "s_ready", "s_max", "exp_done", "p_ready", "t_ready", "pt_ready", "v_done", "o_ready", "o_hi", "o_done",
                "attn_step")
            n = len(jobs)
            w0 = P if causal else T
            width = T + w0
            NP, NT = 4, 3
            rows = ((1, 0, T), (0, T, w0))
            cuts = [(T, 0), (0, P)] + ([(P, 2 * P)] if causal else [(T + P, 2 * P), (P, 3 * P)])
            chunks_of = lambda j: sorted({o[0] for o in jobs[j]["outs"]}) if jobs[j]["evict"] else []
            with scope() as s:
                sc = s("scores", [P, 2, width])
                pr = s("probs", [P, NP, width])
                pt = s("probsT", [P, NT, width])
                nm = s("neg_max", [P, 2, 2])
                sm = s("sums", [P, NP, 2])
                cf = s("coef", [P, 2, 2])
                zero = s("no_mask", [P, T])
                with block() as b:
                    @b.gpsimd
                    def _(pool):
                        pool.memset(zero[:, :], 0.0).then_inc(d_step, 1)

                    @b.tensor
                    def _(pe):
                        def score(j):
                            if j >= 2:
                                pe.wait_ge(s_max, 2 * (j - 1))
                            for q, at, keys in rows:
                                parts = jobs[j]["scores"]
                                for i, (qf, kf) in enumerate(parts):
                                    last = pe.matmul(bank[j % 2][:, at:at + keys], qf[:, q * P:(q + 1) * P],
                                                     kf[:, 0:keys], start=i == 0, stop=i == len(parts) - 1)
                            last.then_inc(s_ready, 1)

                        def turn(j):
                            pe.wait_ge(p_ready, j + 1)
                            if j >= 2:
                                pe.wait_ge(pt_ready, j - 1)
                            for a, c in cuts:
                                last = pe.transpose(bank[2 + j % 2][:, c:c + P], pr[:, j % NP, a:a + P], ident)
                            last.then_inc(t_ready, 1)

                        def values(j):
                            job = jobs[j]
                            pe.wait_ge(pt_ready, j + 1)
                            for i, (chunk, r0, rn, v) in enumerate(job["outs"]):
                                o = bank[4 + chunk % 4]
                                if job["first"] and chunk >= 4:
                                    pe.wait_ge(o_done, chunk - 3)
                                x = job.get("extra") if job["first"] else None
                                if x:
                                    pe.matmul(o[r0:r0 + rn, 0:T], x[0], x[1], start=True, stop=False)
                                pe.matmul(o[r0:r0 + rn, 0:T], v(0), pt[:, j % NT, 0:T],
                                          start=job["first"] and not x, stop=False)
                                a, c = (P, T) if causal else (0, T)
                                last = pe.matmul(o[r0:r0 + rn, a:T], v(1), pt[:, j % NT, c:width], start=False,
                                                 stop=job["last"])
                                if i < len(job["outs"]) - 1:
                                    last.then_inc(o_ready, 1)
                            last.then_inc(v_done, 1)
                            if job["evict"]:
                                pe.wait_ge(v_done, j + 1)
                                pe.sem_inc(o_ready, 1)

                        for j in range(n + 3):
                            if j < n:
                                score(j)
                            if 0 <= j - 2 < n:
                                turn(j - 2)
                            if 0 <= j - 3 < n:
                                values(j - 3)

                    @b.vector
                    def _(dve):
                        ring.flush_lo(dve)
                        steps = Steps(d_step)
                        steps.n = 1
                        dve.wait_ge(d_step, 1)

                        def peak(j):
                            dve.wait_ge(s_ready, j + 1)
                            if j >= 2:
                                dve.wait_ge(exp_done, 2 * (j - 1))
                            for i, (q, at, keys) in enumerate(rows):
                                add = jobs[j]["add"]
                                m = zero[:, 0:keys] if add is None else add[:, T - keys:T]
                                dve.tensor_tensor_reduce(
                                    out=sc[:, j % 2, at:at + keys], in0=bank[j % 2][:, at:at + keys], in1=m,
                                    scale=-scale, scalar=3e38, op0=ALU.add, op1=ALU.min,
                                    accum_out=nm[:, j % 2, i:i + 1]).then_inc(s_max, 1)

                        def weigh(j):
                            dve.wait_ge(exp_done, 2 * (j + 1))
                            steps.step(dve, dve.reciprocal(cf[:, j % 2, :], sm[:, j % NP, :]))
                            if jobs[j].get("coef") is not None:
                                steps.step(dve, dve.tensor_tensor(cf[:, j % 2, :], cf[:, j % 2, :], jobs[j]["coef"], ALU.mult))
                            for i, (q, at, keys) in enumerate(rows):
                                last = dve.tensor_scalar(pr[:, j % NP, at:at + keys], pr[:, j % NP, at:at + keys],
                                                         cf[:, j % 2, i:i + 1], None, ALU.mult)
                            last.then_inc(p_ready, 1)

                        def leave(j):
                            for chunk in chunks_of(j) if not plain else ():
                                dve.wait_ge(o_hi, chunk + 1)
                                dve.tensor_tensor(oT.lo[:, chunk, :], bank[4 + chunk % 4][:, 0:T],
                                                  oT.hi[:, chunk, :].bitcast(F32), ALU.subtract).then_inc(o_done, 1)

                        for j in range(n + 4):
                            if j < n:
                                peak(j)
                            if 0 <= j - 1 < n:
                                weigh(j - 1)
                            if 0 <= j - 4 < n:
                                leave(j - 4)

                    @b.scalar
                    def _(act):
                        ring.flush_hi(act)

                        def exps(j):
                            if j >= NP:
                                act.wait_ge(t_ready, j - NP + 1)
                            for i, (q, at, keys) in enumerate(rows):
                                act.wait_ge(s_max, 2 * j + i + 1)
                                act.activation(pr[:, j % NP, at:at + keys], sc[:, j % 2, at:at + keys], ACT.Exp,
                                               bias=nm[:, j % 2, i:i + 1], scale=-1.0,
                                               accum_out=sm[:, j % NP, i:i + 1]).then_inc(exp_done, 1)

                        def copies(j):
                            act.wait_ge(t_ready, j + 1)
                            if j >= NT:
                                act.wait_ge(v_done, j - NT + 1)
                            act.activation(pt[:, j % NT, :], bank[2 + j % 2][:, 0:width], ACT.Copy).then_inc(pt_ready, 1)

                        def leave(j):
                            for chunk in chunks_of(j):
                                act.wait_ge(o_ready, chunk + 1)
                                act.activation(oT[:, chunk, :] if plain else oT.hi[:, chunk, :], bank[4 + chunk % 4][:, 0:T],
                                               ACT.Copy).then_inc(o_done if plain else o_hi, 1)

                        for j in range(n + 3):
                            if j < n:
                                exps(j)
                            if 0 <= j - 2 < n:
                                copies(j - 2)
                            if 0 <= j - 3 < n:
                                leave(j - 3)


        def times(dve, dst, o, r=inv, factor=1.0):
            if factor == 1.0:
                return dve.tensor_tensor(dst, o, r[:, :], ALU.mult)
            return dve.scalar_tensor_tensor(out=dst, in0=o, scalar=factor, in1=r[:, :], op0=ALU.mult, op1=ALU.mult)

        def times_tok(dve, dst, o, r=inv_tok):
            for t in range(2):
                last = dve.tensor_scalar(dst[:, t, :], o[:, t, :], r[:, t:t + 1], None, ALU.mult)
            return last

        def add_to_h(dve, steps, i, o, posted):
            return dve.tensor_tensor(h[:, i, :], o, h[:, i, :], ALU.add)

        def to_residual(name, src, k, next_gain):
            project([Part(name, "f", src.at, k, DC)], add_to_h, tail=Tail(next_gain, xn), tail_src=lambda i: h[:, i, :])

        gain = lambda name: (lambda c: vec(name, c))


        class FirstTail:

            def __init__(self):
                self.tail = Tail(gain("ffn_a0"), xn)
                self.semaphores = [*self.tail.semaphores, *semaphores("x_in_0", "x_in_1")]
                self.x_in = self.semaphores[-2:]

            def pe(self, pe):
                pass

            def act(self, act):
                act.wait_ge(self.x_in[0], 32)
                for m in range(DC):
                    if m == DC // 2:
                        ring.cut_hi(act, 0)
                        act.wait_ge(self.x_in[1], 16)
                    self.tail.act(act, m, h[:, m, :])
                ring.cut_hi(act, 1)
                ring.left_hi = 2

            def dve(self, dve):
                dve.wait_ge(self.x_in[0], 32)
                dve.wait_ge(self.x_in[1], 16)
                dve.sem_inc(self.tail.given, DC)
                for m in range(DC):
                    if m == DC // 2:
                        ring.cut_lo(dve, 0)
                    self.tail.dve(dve, m, h[:, m, :])
                ring.left_lo = 1

        def start():
            first = FirstTail()
            half = slice(0, DC // 2), slice(DC // 2, DC)
            with block() as b:
                @b.sync
                def _(sp):
                    sp.dma_start(vecs[:, :], w["vecs"]).then_inc(first.x_in[0], 16)
                    sp.dma_start(h[:, half[0], :], w["xT"][:, half[0], :]).then_inc(first.x_in[0], 16)
                    sp.dma_start(h[:, half[1], :], w["xT"][:, half[1], :]).then_inc(first.x_in[1], 16)
                    for n in range(2):
                        ring.load(sp, n)
                    sp.dma_start(consts[:, :], w["consts"]).then_inc(consts_in, 16)
                    ring.load(sp, 2)

                @b.vector
                def _(dve):
                    dve.memset(ones, 1.0)
                    for i, e in enumerate((1e-6, 1e-5)):
                        dve.memset(eps_t[:, i:i + 1], e)
            opening.append(first)


        def mla(next_gain):
            with scope() as s:
                q = s("q", [P, HEADS, T])
                k = s("k", [P, HEADS, T])
                v = s("v", [P, 2, D])
                with scope() as s2:
                    c_in = s2("latents", [P, 5, T])
                    cn = pair(s2, "latents", 5)
                    k_rope = s2("k_rope", [P, T])
                    tmp = s2("tmp", [P, 2, T])
                    kv_sum = s2("kv_sum", [P, T])
                    inv_kv = s2("inv_kv", [P, T])
                    q_sum = s2("q_sum", [P, T])
                    kv_squares = s2("kv_squares", [P, 2, T])
                    tail_q = Tail(lambda c: vec("cq", c), cn, total=q_sum)
                    tail_kv = Tail(lambda c: vec("ckv", c), cn, total=kv_sum, offset=3, squares=kv_squares)

                    def leave(dve, steps, i, o, posted):
                        if i < 5:
                            return times(dve, c_in[:, i, :], o)
                        turned = i - 5
                        if not turned:
                            dve.wait_ge(steps.left, i)
                        last = dve.tensor_tensor(tmp[:, turned, :], o, const(("cos", "sin")[turned]), ALU.mult)
                        if turned:
                            steps.step(dve, last)
                            steps.step(dve, dve.tensor_tensor(tmp[:, 0, :], tmp[:, 0, :], tmp[:, 1, :], ALU.add))
                            last = times(dve, k_rope[:, :], tmp[:, 0, :])
                        return last

                    project([Part("mla_in", "f", xn.at, DC, 7)], leave, inverses=[Inverse(D)],
                            tail={0: (tail_q, 0), 1: (tail_q, 1), 2: (tail_q, 2), 3: (tail_kv, 0), 4: (tail_kv, 1)},
                            tail_src=lambda i: c_in[:, i, :])
                    rotate = s2("rotate", [P, T])

                    def leave(dve, steps, i, o, posted):
                        if i < HEADS:
                            if i == 0:
                                steps.step(dve, dve.tensor_tensor(rotate[:, :], inv[:, :], const("rotate"), ALU.mult))
                            return times(dve, q[:, i, :], o, rotate)
                        if i < HEADS + 8:
                            m = i - HEADS
                            for half in range(2):
                                rows = slice(64 * half, 64 * half + 64)
                                last = dve.tensor_tensor(k[0:MLA_NOPE, 2 * m + half, :], o[rows, :], inv_kv[rows, :], ALU.mult)
                            return last
                        m = i - HEADS - 8
                        return times_tok(dve, v[:, :, m * 256:(m + 1) * 256], o)

                    def post(act, i, left, posted):
                        if i < HEADS:
                            act.activation(k[MLA_NOPE:P, i, :], k_rope[MLA_NOPE:P, :], ACT.Copy)

                    kv_at = lambda c: cn.at(3 + c)
                    project([Part("mla_uq", "f", cn.at, 3, 16), Part("mla_uk", "f", kv_at, 2, 8),
                             Part("mla_uv", "t", kv_at, 2, 4, 256)], leave, post=post,
                            inverses=[Inverse(MLA_Q, total=q_sum),
                                      Inverse(MLA_KV, total=kv_sum, out=inv_kv, tok=inv_tok, b=6)])
                oT = pair(s, "heads_out", DC)
                jobs = []
                for hd in range(HEADS):
                    c, r = hd // 2, 64 * (hd % 2)
                    jobs.append(dict(
                        scores=[(q[:, hd, :], k[:, hd, :])],
                        add=const("mask"), first=True, last=True, evict=hd % 2 == 1,
                        outs=[(c, r, 64, lambda kb, hd=hd: v[:, kb, hd * 64:hd * 64 + 64])]))
                attention(jobs, oT, scale=(MLA_NOPE + MLA_ROPE) ** -0.5)
                to_residual("mla_o", oT, DC, next_gain)

        def nsa(next_gain):
            with scope() as s:
                qT = s("q", [P, DC, T])
                k_s = s("k_sel", [P, NSA_GROUPS, T])
                k_w = s("k_win", [P, NSA_GROUPS, T])
                v_s = s("v_sel", [P, 2, 256])
                v_w = s("v_win", [P, 2, 256])
                gates = s("gates", [P, 2, 48])
                bias = s("bias", [P, HEADS, T])
                vcm = s("v_cmp", [N_CMP, NSA_GROUPS, 64])
                pTc = s("probsT_cmp", [N_CMP, HEADS, T])
                with scope() as s2:
                    kc2, vc2 = y8[:, 0:NSA_GROUPS, :], y8[:, NSA_GROUPS:2 * NSA_GROUPS, :]
                    rel = s2("rel_bias", [REL_BUCKETS + 1, HEADS])
                    ext = s2("bias_by_distance", [HEADS, TOEP])
                    tmp = s2("tmp", [P, 2, T])
                    w1 = s2("w1", [P, 2, 16, P])
                    w2 = s2("w2", [P, 4, 64])
                    rel_in, rel_mm, rel_out, rel_stored, bias_in, w_in = semaphores(
                        "rel_in", "rel_mm", "rel_out", "rel_stored", "bias_in", "cmp_weights")

                    def sp_first(sp):
                        sp.dma_start(rel[0:REL_BUCKETS, :], w["rel_bias"]).then_inc(rel_in, 16)
                        sp.dma_start(rel[REL_BUCKETS:REL_BUCKETS + 1, :],
                                     w["consts"][0:1, CONSTS["ones"][0]:CONSTS["ones"][0] + HEADS]).then_inc(rel_in, 16)
                        sp.dma_start(w1[:, :, :, :], w["nsa_w1"].rearrange("a p (c m) -> p a c m", m=P)).then_inc(w_in, 16)
                        sp.dma_start(w2[:, :, :], w["nsa_w2"].rearrange("p (a m) -> p a m", m=64)).then_inc(w_in, 16)

                    def pool(eng):
                        eng.memset(kcm[:, :, :, :], 0.0).then_inc(zeroed, 1)
                        eng.wait_ge(rel_out, 1)
                        line = ext[:, :]
                        rows = bass.AP(line.tensor, T - 1 - P, [line.ap[0], [-1, P], [1, T]])
                        eng.dma_start(w["scratch"].rearrange("q h k -> h q k"), rows).then_inc(rel_stored, 16)
                        eng.wait_ge(rel_stored, 16)
                        eng.dma_start(bias[:, :, :], w["scratch"]).then_inc(bias_in, 16)
                        eng.wait_ge(bias_in, 16)

                    def pe_first(pe):
                        pe.wait_ge(rel_in, 32)
                        pe.matmul(bank[4][0:HEADS, 0:TOEP], rel[:, :], const("bucket")[0:REL_BUCKETS + 1, :],
                                  start=True, stop=True).then_inc(rel_mm, 1)

                    def act_first(act):
                        act.wait_ge(rel_mm, 1)
                        act.activation(ext[:, :], bank[4][0:HEADS, 0:TOEP], ACT.Copy).then_inc(rel_out, 1)

                    Q0, K0, V0 = 5, 13, 17

                    def place(i):
                        kind, half = divmod(i - 1, 2) if i < Q0 else divmod(i - K0 + 4, 2)
                        return ((kc2, 1), (vc2, 1), (k_s, 0), (k_w, 0))[kind] + (half,)

                    doubled = [*range(1, Q0), *range(K0, V0)]

                    def leave(dve, steps, i, o, posted):
                        if i == 0:
                            return dve.tensor_tensor(gatesT[:, :], o[0:3 * HEADS, :], inv[0:3 * HEADS, :], ALU.mult)
                        if Q0 <= i < K0:
                            return times(dve, qT[:, i - Q0, :], o, factor=NSA_QK ** -0.5)
                        if i >= V0:
                            return times_tok(dve, (v_s, v_w)[i - V0], o)
                        n = doubled.index(i)
                        if n >= 2:
                            dve.wait_ge(posted, n - 1)
                            dve.wait_ge(steps.left, i)
                        steps.step(dve, times(dve, tmp[:, n % 2, :], o))
                        dst, shift, half = place(i)
                        dve.tensor_copy(dst[64:128, 2 * half, 0:T - shift], tmp[0:64, n % 2, shift:T])
                        return dve.tensor_copy(dst[64:128, 2 * half + 1, 0:T - shift], tmp[64:128, n % 2, shift:T])

                    def post(act, i, left, posted):
                        if i in doubled:
                            n = doubled.index(i)
                            act.wait_ge(left, i + 1)
                            dst, _, half = place(i)
                            act.activation(dst[0:64, 2 * half, :], tmp[0:64, n % 2, :], ACT.Copy)
                            act.activation(dst[0:64, 2 * half + 1, :], tmp[64:128, n % 2, :], ACT.Copy).then_inc(posted, 1)
                        if i == 0:
                            act.wait_ge(left, 1)
                            act.activation(gatesT[:, :], gatesT[:, :], ACT.Sigmoid).then_inc(gated, 1)

                    gatesT = s2("gatesT", [3 * HEADS, T])
                    flat = s2("flat", [P, 2, 16, NSA_GROUPS * N_CMP])
                    hid = s2("cmp_hidden", [P, 2, NSA_GROUPS * N_CMP])
                    kcm = s2("k_cmp", [P, NSA_GROUPS, 2, N_CMP])
                    pc = s2("probs_cmp", [P, HEADS * 2, N_CMP])
                    bc = s2("bias_cmp", [P, HEADS, 2, N_CMP])
                    mx = s2("max_cmp", [P, HEADS * 2])
                    sm = s2("sum_cmp", [P, HEADS * 2])
                    (zeroed, gated, flattened, multiplied, hidden, compressed, scored, shifted, exponents, weighted, turned, copied,
                     d_step) = semaphores("zeroed", "gated", "flat", "cmp_mm", "hidden", "cmp", "cmp_scores", "cmp_shifted", "cmp_exp",
                                          "cmp_weighted", "cmp_turned", "cmp_copied", "cmp_step")
                    csteps = Steps(d_step)

                    def turn_gates(pe):
                        pe.wait_ge(gated, 1)
                        for t in range(2):
                            last = pe.transpose(bank[7][:, t * 3 * HEADS:(t + 1) * 3 * HEADS], gatesT[:, t * P:(t + 1) * P],
                                                ident[0:3 * HEADS, 0:3 * HEADS])
                        last.then_inc(gated, 1)

                    def take_gates(act):
                        act.wait_ge(gated, 2)
                        act.activation(gates[:, :, :], bank[7][:, 0:6 * HEADS].rearrange("p (t c) -> p t c", t=2), ACT.Copy
                                       ).then_inc(gated, 1)

                    def flatten(dve):
                        dve.wait_ge(project.posted, 4)
                        dve.wait_ge(project.left, Q0)
                        for i, (src, pos) in enumerate(((kc2, "pos_k"), (vc2, "pos_v"))):
                            a = src[:, :, :]
                            v0 = vec(pos)
                            view = bass.AP(a.tensor, a.offset, [a.ap[0], [2, 16], [T, NSA_GROUPS], [CMP_STRIDE, N_CMP]])
                            pos_view = bass.AP(v0.tensor, v0.offset, [v0.ap[0], [1, 16], [0, NSA_GROUPS], [0, N_CMP]])
                            dve.tensor_tensor(flat[:, i, :, :].rearrange("p c (g n) -> p c g n", g=NSA_GROUPS), view, pos_view,
                                              ALU.add).then_inc(flattened, 1)

                    def hidden_products(i, half):
                        def pe(pe):
                            if (i, half) == (0, 0):
                                pe.wait_ge(w_in, 32)
                                pe.wait_ge(flattened, 2)
                            for c in range(8 * half, 8 * half + 8):
                                last = pe.matmul(bank[5 + i][:, 0:60], w1[:, i, c, :], flat[:, i, c, :], start=c == 0, stop=c == 15)
                            if half:
                                last.then_inc(multiplied, 1)
                        return pe

                    def hidden_layers(act):
                        act.wait_ge(multiplied, 2)
                        for i in range(2):
                            act.activation(hid[:, i, :], bank[5 + i][:, 0:60], ACT.Gelu_apprx_tanh).then_inc(hidden, 1)

                    def compress(pe):
                        pe.wait_ge(hidden, 2)
                        pe.matmul(bank[7][:, 0:60], w2[:, 0:2, :].rearrange("p a m -> p (a m)"), hid[:, 0, :], start=True, stop=True)
                        for g in range(NSA_GROUPS):
                            last = pe.matmul(bank[4][0:N_CMP, g * 64:g * 64 + 64], hid[:, 1, g * N_CMP:(g + 1) * N_CMP],
                                             w2[:, 2, :], start=True, stop=True)
                        last.then_inc(multiplied, 1)

                    def take_compressed(act):
                        act.wait_ge(multiplied, 3)
                        act.wait_ge(zeroed, 1)
                        for o in range(2):
                            half = slice(64 * o, 64 * o + 64)
                            act.activation(kcm[half, :, o, :], bank[7][half, 0:60].rearrange("p (g n) -> p g n", g=NSA_GROUPS), ACT.Copy)
                        act.activation(vcm[:, :, :], bank[4][0:N_CMP, 0:256].rearrange("p (g c) -> p g c", g=4), ACT.Copy
                                       ).then_inc(compressed, 1)

                    def scores(half):
                        def pe(pe):
                            pe.wait_ge(compressed, 1)
                            pe.wait_ge(project.left, Q0 + 4 * (half + 1))
                            for two in range(4 * half, 4 * half + 4):
                                for q in range(2):
                                    at = (two * 2 + q) * 2 * N_CMP
                                    last = pe.matmul(bank[5][:, at:at + 2 * N_CMP], qT[:, two, q * P:(q + 1) * P],
                                                     kcm[:, two // 2, :, :].rearrange("p o n -> p (o n)"), start=True, stop=True)
                            last.then_inc(scored, 1)
                        return pe

                    rows = lambda t: t[:, :].rearrange("p (a b) -> p a b", b=1).to_broadcast([P, HEADS * 2, N_CMP])

                    def take_bias(dve):
                        dve.wait_ge(bias_in, 16)
                        late, early = CMP_BLOCK - 1, P + CMP_BLOCK - 1
                        csteps.step(dve, dve.memset(bc[:, :, 0, :], NEG))
                        csteps.step(dve, dve.tensor_copy(bc[:, :, 0, 0:N_CMP0], bias[:, :, early:early + CMP_STRIDE * (N_CMP0 - 1) + 1:CMP_STRIDE]))
                        csteps.step(dve, dve.tensor_copy(bc[:, :, 1, :], bias[:, :, late:late + CMP_STRIDE * (N_CMP - 1) + 1:CMP_STRIDE]))

                    def shift(dve):
                        dve.wait_ge(scored, 2)
                        for par in range(2):
                            odd = lambda t: t.rearrange("p (a o b) n -> p a o b n", o=2, b=2)[:, :, par, :, :]
                            csteps.step(dve, dve.tensor_tensor(
                                odd(pc[:, :, :]), bank[5][:, 0:2 * HEADS * N_CMP].rearrange("p (a b o n) -> p a o b n", a=8, b=2, o=2)[:, :, par, :, :],
                                odd(bc[:, :, :, :].rearrange("p h q n -> p (h q) n")), ALU.add))
                        csteps.step(dve, dve.tensor_reduce(mx[:, :], pc[:, :, :], AX.X, ALU.max))
                        dve.tensor_tensor(pc[:, :, :], pc[:, :, :], rows(mx), ALU.subtract).then_inc(shifted, 1)

                    def exponentiate(act):
                        act.wait_ge(shifted, 1)
                        act.activation(pc[:, :, :], pc[:, :, :], ACT.Exp).then_inc(exponents, 1)

                    def weigh(dve):
                        dve.wait_ge(exponents, 1)
                        dve.wait_ge(gated, 3)
                        csteps.step(dve, dve.tensor_reduce(sm[:, :], pc[:, :, :], AX.X, ALU.add))
                        csteps.step(dve, dve.reciprocal(sm[:, :], sm[:, :]))
                        by_q = lambda t: t[:, :].rearrange("p (h q) -> p h q", q=2)
                        csteps.step(dve, dve.tensor_tensor(by_q(sm), by_q(sm), gates[:, :, 0:48:3].rearrange("p q h -> p h q"), ALU.mult))
                        vv = const("valid")
                        ok = bass.AP(vv.tensor, vv.offset, [vv.ap[0], [0, HEADS], [N_CMP, 2], [1, N_CMP]])
                        pc4 = pc[:, :, :].rearrange("p (h q) n -> p h q n", q=2)
                        csteps.step(dve, dve.tensor_tensor(pc4, pc4, ok, ALU.mult))
                        dve.tensor_tensor(pc[:, :, :], pc[:, :, :], rows(sm), ALU.mult).then_inc(weighted, 1)

                    def turn(k):
                        def pe(pe):
                            pe.wait_ge(weighted, 1)
                            if k >= 4:
                                pe.wait_ge(copied, k - 3)
                            for i in range(4):
                                last = pe.transpose(bank[4 + k % 4][0:N_CMP, i * P:(i + 1) * P], pc[:, 4 * k + i, :], ident)
                            last.then_inc(turned, 1)
                        return pe

                    def copy(k):
                        def act(act):
                            act.wait_ge(turned, k + 1)
                            act.activation(pTc[:, 2 * k:2 * k + 2, :], bank[4 + k % 4][0:N_CMP, :].rearrange("p (h t) -> p h t", h=2),
                                           ACT.Copy).then_inc(copied, 1)
                        return act

                    between = ({3: [turn_gates], 7: [hidden_products(0, 0), hidden_products(0, 1)],
                                8: [hidden_products(1, 0)], 9: [hidden_products(1, 1)], 11: [compress],
                                13: [scores(0)], 14: [scores(1)],
                                18: [turn(k) for k in range(4)], 19: [turn(k) for k in range(4, 8)]},
                               {3: [take_gates], 9: [hidden_layers], 11: [take_compressed], 14: [exponentiate],
                                17: [copy(k) for k in range(4)], 18: [copy(k) for k in range(4, 8)]},
                               {4: [flatten], 13: [take_bias], 14: [shift], 15: [weigh]})
                    project([Part("nsa_g", "f", xn.at, DC, 1), Part("nsa_in", "f", xn.at, DC, 16),
                             Part("nsa_v", "t", xn.at, DC, 2, 256)], leave, inverses=[Inverse(D, tok=inv_tok)],
                            post=post, sp_first=sp_first, pe_first=pe_first, act_first=act_first, pool=pool, between=between)
                oT = pair(s, "heads_out", DC)
                jobs = []
                for hd in range(HEADS):
                    c, r, g = hd // 2, 64 * (hd % 2), hd // 4
                    for i, (kk, vv) in enumerate(((k_s, v_s), (k_w, v_w))):
                        jobs.append(dict(
                            scores=[(qT[r:r + 64, c, :], kk[r:r + 64, g, :])], add=bias[:, hd, :],
                            coef=gates[:, ::-1, 3 * hd + 1 + i], first=i == 0, last=i == 1, evict=i == 1 and hd % 2 == 1,
                            extra=(vcm[:, g, :], pTc[:, hd, :]),
                            outs=[(c, r, 64, lambda kb, vv=vv, g=g: vv[:, kb, g * 64:g * 64 + 64])]))
                attention(jobs, oT)
                to_residual("nsa_o", oT, DC, next_gain)

        def activated(name, dst, func, bias=None):
            def leave(dve, steps, i, o, posted):
                return times(dve, dst[:, i, :], o)

            def post(act, i, left, posted):
                act.wait_ge(left, i + 1)
                act.activation(dst[:, i, :], dst[:, i, :], func, bias=bias(i)).then_inc(posted, 1)
            return leave, post

        def two_branches(next_gain):
            with scope() as s:
                mixed = y8
                with scope() as s2:
                    gate = s2("gate", [P, DC, T])
                    qk = s2("qk", [P, 16, T])
                    v = s2("v", [P, 2, D])
                    neg_lam = s2("neg_lambda", [P, 2])
                    prod = s2("lambda_products", [64, 2])
                    ex = s2("lambda_exps", [P, 2])

                    def leave(dve, steps, i, o, posted):
                        if i < 16:
                            return times(dve, qk[:, i, :], o, factor=DA_QK ** -0.5 if i < 8 else 1.0)
                        return times_tok(dve, v[:, :, (i - 16) * 256:(i - 15) * 256], o)

                    project([Part("da_qk", "f", xn.at, DC, 16), Part("da_v", "t", xn.at, DC, 4, 256)], leave,
                            inverses=[Inverse(D, tok=inv_tok)])
                    lam, d_step = semaphores("lambda", "lam_step")
                    g_sub = s2("subln_gain", [P, 1])
                    with block() as b:
                        @b.vector
                        def _(dve):
                            steps = Steps(d_step)
                            at, _ = VECS["lam"]
                            dve.tensor_tensor(prod[:, :], vecs[0:64, at:at + 4:2], vecs[0:64, at + 1:at + 4:2], ALU.mult).then_inc(lam, 1)
                            dve.tensor_scalar(g_sub[:, :], vec("subln"), 1.0 - LAM_INIT, None, ALU.mult)
                            dve.wait_ge(lam, 3)
                            for i in range(2):
                                steps.step(dve, dve.tensor_tensor(neg_lam[:, i:i + 1], ex[:, 1:2], ex[:, 0:1], ALU.subtract))
                            dve.tensor_scalar(neg_lam[:, :], neg_lam[:, :], LAM_INIT, None, ALU.subtract)

                        @b.tensor
                        def _(pe):
                            pe.wait_ge(lam, 1)
                            pe.matmul(bank[0][:, 0:2], ones[0:64, :], prod[:, :], start=True, stop=True).then_inc(lam, 1)

                        @b.scalar
                        def _(act):
                            act.wait_ge(lam, 2)
                            act.activation(ex[:, :], bank[0][:, 0:2], ACT.Exp).then_inc(lam, 1)
                    oT = s2("heads_out", [P, DC, T])
                    on = pair(s2, "subln", DC)
                    jobs = []
                    for hd in range(DA_HEADS):
                        for i in range(2):
                            r = 64 * i
                            jobs.append(dict(
                                scores=[(qk[r:r + 64, hd, :], qk[r:r + 64, 8 + hd, :])], add=const("mask"),
                                coef=neg_lam[:, :] if i else None, first=i == 0, last=i == 1, evict=i == 1,
                                outs=[(hd, 0, P, lambda kb, hd=hd: v[:, kb, hd * P:(hd + 1) * P])]))
                    attention(jobs, oT, plain=True)
                    norm = GroupNorm(s2, oT, on, lambda c: g_sub[:, :], 1, DA_HEADS, 1e-5)
                    between = ({}, {}, {})
                    norm.into(between, [1] * DC, 2)

                    def leave(dve, steps, i, o, posted):
                        if i < DC:
                            return times(dve, gate[:, i, :], o)
                        if i == DC:
                            dve.wait_ge(posted, DC)
                        return dve.tensor_tensor(mixed[:, i - DC, :], o, gate[:, i - DC, :], ALU.mult)

                    def post(act, i, left, posted):
                        if i < DC:
                            act.wait_ge(left, i + 1)
                            act.activation(gate[:, i, :], gate[:, i, :], ACT.Sigmoid, bias=vec("b_gate", i)).then_inc(posted, 1)

                    project([Part("gate_a", "f", xn.at, DC, DC), Part("br_attn", "f", on.at, DC, DC, need=norm.need)], leave, post=post,
                            act_first=lambda act: [norm.square(c)(act) for c in range(DC)], between=between)
                y = s("y", [P, SC, T])
                ssd(y)
                yn = pair(s, "y", SC)
                with scope() as s2:
                    gate = s2("gate", [P, DC, T])
                    tmp = s2("tmp", [P, 2, T])
                    zt = s2("z", [P, 2, T])
                    mp = pair(s2, "mixed", DC)
                    multiplied, mixed_hi = semaphores("multiplied", "mixed_hi")
                    G2 = SSD_GROUPS // 2
                    norms = []
                    for k in range(2):
                        norms.append(GroupNorm(s2, y, yn, lambda c: vec("ssd_g", c), SC // SSD_GROUPS, G2, 1e-5,
                                               first=SC // 2 * k, buffers=2, before=norms[0] if k else None))
                    first_out = SC + DC
                    between = ({}, {}, {})
                    for k, v in enumerate(norms):
                        v.into(between, [c + SC // 2 * k + 4 for c in range(SC // 2)], SC // 2 * k + 12)

                    def leave(dve, steps, i, o, posted):
                        if i < first_out:
                            if i >= 2:
                                dve.wait_ge(posted, i - 1)
                            return times(dve, gate[:, i - SC, :] if i >= SC else tmp[:, i % 2, :], o)
                        if i == first_out:
                            dve.wait_ge(posted, first_out)
                        if i >= first_out + 2:
                            dve.wait_ge(steps.left, i - 1)
                        m = i - first_out
                        steps.step(dve, dve.tensor_tensor(tmp[:, i % 2, :], o, gate[:, m, :], ALU.mult))
                        return dve.tensor_tensor(mixed[:, m, :], mixed[:, m, :], tmp[:, i % 2, :], ALU.add)

                    def post(act, i, left, posted):
                        act.wait_ge(left, i + 1)
                        if i >= first_out:
                            m = i - first_out
                            act.activation(mp.hi[:, m, :], mixed[:, m, :], ACT.Copy).then_inc(mixed_hi, 1)
                            return
                        if i >= SC:
                            act.activation(gate[:, i - SC, :], gate[:, i - SC, :], ACT.Sigmoid,
                                           bias=vec("b_gate", DC + i - SC)).then_inc(posted, 1)
                        else:
                            if i >= 2:
                                act.wait_ge(multiplied, i - 1)
                            act.activation(zt[:, i % 2, :], tmp[:, i % 2, :], ACT.Silu).then_inc(posted, 1)
                        c = i - 2
                        if 0 <= c < SC:
                            act.wait_ge(multiplied, c + 1)
                            norms[c // (SC // 2)].square(c % (SC // 2))(act)

                    def later(dve, steps, i, left):
                        if i < SC:
                            dve.wait_ge(steps.posted, i + 1)
                            dve.tensor_tensor(y[:, i, :], y[:, i, :], zt[:, i % 2, :], ALU.mult).then_inc(multiplied, 1)
                        if i >= first_out:
                            m = i - first_out
                            dve.wait_ge(mixed_hi, m + 1)
                            dve.tensor_tensor(mp.lo[:, m, :], mixed[:, m, :], mp.hi[:, m, :].bitcast(F32), ALU.subtract)

                    project([Part("z", "f", xn.at, DC, SC), Part("gate_s", "f", xn.at, DC, DC),
                             Part("br_ssd", "f", yn.at, SC, DC,
                                  need=lambda pe, c: norms[c // (SC // 2)].need(pe, c % (SC // 2)))], leave, post=post, later=later, between=between)
                    project([Part("mix_out", "f", mp.at, DC, DC)], lambda dve, steps, i, o, posted: dve.tensor_copy(y8[:, i, :], o),
                            tail=Tail(), tail_src=lambda i: y8[:, i, :])
                opening.append(AddNormed(opening[-1].tail, gain("mix_post"), 1.0, next_gain))

        def ssd(y):
            xs = y
            with scope() as s:
                bcT = s("b_and_c", [P, 2 * SSD_GROUPS, T])
                dt_raw = s("dt_raw", [P, 2, SSD_HEADS])
                with scope() as s2:
                    padded = s2("padded", [P, 2, CONV - 1 + T])
                    acc = s2("conv", [P, 2, 2, T])
                    pad, tapped, summed, conv, fin = semaphores("pad", "tapped", "taps_summed", "conv", "conv_out")

                    def pool(eng):
                        eng.memset(padded[:, :, :], 0.0).then_inc(pad, 1)
                        for i in range(XBC):
                            a = acc[:, i % 2]
                            eng.wait_ge(summed, i + 1)
                            eng.tensor_tensor(a[:, 0, :], a[:, 0, :], a[:, 1, :], ALU.add).then_inc(conv, 1)

                    def leave(dve, steps, i, o, posted):
                        if i == XBC:
                            return times_tok(dve, dt_raw, o)
                        if i == 0:
                            dve.wait_ge(pad, 1)
                        if i >= 2:
                            dve.wait_ge(summed, i - 1)
                        return times(dve, padded[:, i % 2, CONV - 1:], o)

                    def post(act, i, left, posted):
                        if i < XBC:
                            act.wait_ge(left, i + 1)
                            if i >= 2:
                                act.wait_ge(fin, i - 1)
                            act.activation(acc[:, i % 2, 0, :], padded[:, i % 2, 0:T], ACT.Identity,
                                           scale=vec("conv_w", i * CONV), bias=vec("conv_b", i))
                            act.activation(acc[:, i % 2, 1, :], padded[:, i % 2, 1:1 + T], ACT.Copy,
                                           scale=vec("conv_w", i * CONV + 1)).then_inc(tapped, 1)
                        if 1 <= i:
                            k = i - 1
                            act.wait_ge(conv, k + 1)
                            act.activation(xs[:, k, :] if k < SC else bcT[:, k - SC, :], acc[:, k % 2, 0, :], ACT.Silu).then_inc(fin, 1)

                    def later(dve, steps, i, left):
                        if i >= XBC:
                            return
                        dve.wait_ge(tapped, i + 1)
                        dve.wait_ge(left, i + 1)
                        for t in range(2):
                            tap, a = t + 2, acc[:, i % 2, t, :]
                            last = dve.scalar_tensor_tensor(out=a, in0=padded[:, i % 2, tap:tap + T],
                                                            scalar=vec("conv_w", i * CONV + tap), in1=a, op0=ALU.mult, op1=ALU.add)
                        last.then_inc(summed, 1)

                    project([Part("xbc", "f", xn.at, DC, XBC), Part("dt", "t", xn.at, DC, 1, SSD_HEADS)], leave,
                            post=post, later=later, pool=pool)
                scan(s, xs, y, bcT, dt_raw)

        def scan(s, xs, y, bcT, dt_raw):
            H = SSD_HEADS
            xt = s("x_tokens", [P, 2, SSD_INNER])
            bt = s("b_tokens", [P, SSD_GROUPS, P])
            dt = s("dt", [P, 2, H])
            adt = s("a_dt", [P, 2, H])
            neg_cs = s("neg_cumsum", [P, 2, H])
            decay = s("decay", [P, H])
            cbm = s("masked_cb", [P, 2, SSD_GROUPS, P])
            st = s("states", [P, SSD_INNER])
            u = s("tmp", [P, 2, 2, H])
            a_neg = s("a", [P, H])
            step_a, step_d, dt_ok, cs_ok, tr, cp, cb_ok, stt = semaphores(
                "ssd_a", "ssd_d", "dt_ok", "cs_ok", "x_turned", "x_copied", "cb_ok", "state")
            spread = lambda t: bass.AP(t.tensor, t.offset, [t.ap[0], [0, 2], [1, H]])
            with block() as b:
                @b.scalar
                def _(act):
                    steps = Steps(step_a)
                    steps.step(act, act.activation(a_neg[:, :], vec("A_log", 0, H), ACT.Exp))
                    act.wait_ge(dt_ok, 1)
                    steps.step(act, act.activation(u[:, 1], u[:, 1], ACT.Exp))
                    act.activation(u[:, 1], u[:, 1], ACT.Ln, bias=1.0).then_inc(dt_ok, 1)
                    act.wait_ge(cs_ok, 2)
                    act.activation(decay[:, :], decay[:, :], ACT.Exp).then_inc(cs_ok, 1)

                @b.vector
                def _(dve):
                    steps = Steps(step_d)
                    steps.step(dve, dve.tensor_tensor(dt_raw[:, :, :], dt_raw[:, :, :], spread(vec("dt_bias", 0, H)), ALU.add))
                    steps.step(dve, dve.tensor_scalar(u[:, 0], dt_raw[:, :, :], -1.0, None, ALU.mult))
                    dve.tensor_tensor(u[:, 1], u[:, 0], dt_raw[:, :, :], ALU.min).then_inc(dt_ok, 1)
                    dve.wait_ge(dt_ok, 2)
                    steps.step(dve, dve.scalar_tensor_tensor(out=dt[:, :, :], in0=dt_raw[:, :, :], scalar=0.0, in1=u[:, 1],
                                                             op0=ALU.max, op1=ALU.add))
                    dve.wait_ge(step_a, 1)
                    dve.scalar_tensor_tensor(out=adt[:, :, :], in0=dt[:, :, :], scalar=-1.0, in1=spread(a_neg[:, :]),
                                             op0=ALU.mult, op1=ALU.mult).then_inc(dt_ok, 1)
                    dve.wait_ge(cs_ok, 1)
                    steps.step(dve, dve.tensor_scalar(neg_cs[:, :, :], bank[7][:, 0:2 * H].rearrange("p (t c) -> p t c", t=2), -1.0, None, ALU.mult))
                    dve.tensor_tensor(decay[:, :], bank[7][:, 2 * H:3 * H], neg_cs[:, 0, :], ALU.add).then_inc(cs_ok, 1)
                    dt_wide = dt[:, :, :].rearrange("p t (h o) -> p t h o", o=1)
                    heads = lambda t: t.rearrange("p (h d) -> p h d", d=SSD_P)
                    for j in range(8):
                        t, c4 = divmod(j, 4)
                        dve.wait_ge(tr, j + 1)
                        dve.tensor_tensor(heads(xt[:, t, c4 * 512:(c4 + 1) * 512]), heads(bank[j % 4][:, :]),
                                          dt_wide[:, t, c4 * 8:(c4 + 1) * 8, :].to_broadcast([P, 8, SSD_P]), ALU.mult).then_inc(cp, 1)
                    dve.wait_ge(tr, 9)
                    dve.tensor_copy(bt[:, :, :], bank[4][:, :].rearrange("p (g c) -> p g c", g=4)).then_inc(cp, 1)
                    for t in range(2):
                        dve.wait_ge(cb_ok, t + 1)
                        tri_w = bass.AP(tri.tensor, tri.offset, [tri.ap[0], [0, SSD_GROUPS], [1, P]])
                        dve.tensor_tensor(cbm[:, t, :, :], bank[5 + t][:, :].rearrange("p (g c) -> p g c", g=4), tri_w, ALU.mult)
                    dve.wait_ge(cs_ok, 3)
                    dve.wait_ge(cp, 9)
                    dec = decay[:, :].rearrange("p (h o) -> p h o", o=1)
                    dve.tensor_tensor(heads(st[:, :]), heads(xt[:, 0, :]), dec.to_broadcast([P, H, SSD_P]), ALU.mult).then_inc(stt, 1)
                    dve.wait_ge(stt, 5)
                    for g in range(SSD_GROUPS):
                        dve.tensor_copy(st[:, g * 512:(g + 1) * 512], bank[g][:, :])

                @b.tensor
                def _(pe):
                    for j in range(8):
                        t, c4 = divmod(j, 4)
                        if j >= 4:
                            pe.wait_ge(cp, j - 3)
                        for i in range(4):
                            last = pe.transpose(bank[j % 4][:, i * P:(i + 1) * P], xs[:, 4 * c4 + i, t * P:(t + 1) * P], ident)
                        last.then_inc(tr, 1)
                        if j == 3:
                            pe.wait_ge(dt_ok, 3)
                            for t2 in range(2):
                                pe.matmul(bank[7][:, t2 * H:(t2 + 1) * H], tri, adt[:, t2, :], start=True, stop=True)
                            pe.matmul(bank[7][:, 2 * H:3 * H], ones, adt[:, 0, :], start=True, stop=True).then_inc(cs_ok, 1)
                    for g in range(SSD_GROUPS):
                        last = pe.transpose(bank[4][:, g * P:(g + 1) * P], bcT[:, g, 0:P], ident)
                    last.then_inc(tr, 1)
                    for t in range(2):
                        for g in range(SSD_GROUPS):
                            last = pe.matmul(bank[5 + t][:, g * P:(g + 1) * P], bcT[:, g, t * P:(t + 1) * P],
                                             bcT[:, SSD_GROUPS + g, t * P:(t + 1) * P], start=True, stop=True)
                        last.then_inc(cb_ok, 1)
                    pe.wait_ge(cp, 9)
                    pe.wait_ge(stt, 1)
                    for g in range(SSD_GROUPS):
                        pe.matmul(bank[g][:, :], bt[:, g, :], st[:, g * 512:(g + 1) * 512], start=True, stop=True).then_inc(stt, 1)
            Q, NB = 4, 3
            seg_ok, seg_min, l_ok, m_ok, c_ok, y_ok, y_out, carry = semaphores(
                "seg_ok", "seg_min", "l_ok", "m_ok", "c_ok", "y_ok", "y_out", "carry")
            seg = s("segments", [P, NB, 2, Q, P])
            cs1 = s("carried_c", [P, NB, Q, P])
            quads = H // Q
            with block() as b:
                def decayed_scores(engine, k, t):
                    cb = cbm[:, t, k // 2, :]
                    wide = bass.AP(cb.tensor, cb.offset, [cb.ap[0], [0, Q], [1, P]])
                    return engine.tensor_tensor(seg[:, k % NB, t, :, :], seg[:, k % NB, t, :, :], wide, ALU.mult)

                @b.gpsimd
                def _(pool):
                    for k in range(quads):
                        c = bcT[:, SSD_GROUPS + k // 2, P:T]
                        wide = bass.AP(c.tensor, c.offset, [c.ap[0], [0, Q], [1, P]])
                        pool.wait_ge(carry, k + 1)
                        pool.tensor_tensor(cs1[:, k % NB, :, :], cs1[:, k % NB, :, :], wide, ALU.mult)
                        pool.wait_ge(l_ok, k + 1)
                        decayed_scores(pool, k, 1).then_inc(c_ok, 1)

                @b.tensor
                def _(pe):
                    def sums(k):
                        if k >= 2:
                            pe.wait_ge(seg_min, 8 * (k - 1))
                            pe.wait_ge(carry, k - 1)
                        for t in range(2):
                            for i in range(Q):
                                a = adt[:, t, Q * k + i:Q * k + i + 1]
                                col = bass.AP(a.tensor, a.offset, [a.ap[0], [0, P]])
                                last = pe.matmul(bank[2 * (k % 2) + t][:, i * P:(i + 1) * P], col, tri, start=True, stop=True)
                        last.then_inc(seg_ok, 1)

                    def outputs(k):
                        pe.wait_ge(m_ok, k + 1)
                        pe.wait_ge(c_ok, k + 1)
                        if k >= 2:
                            pe.wait_ge(y_out, 2 * (k - 1))
                        for i in range(Q):
                            hd = Q * k + i
                            r = 64 * (i % 2)
                            o = bank[4 + 2 * (k % 2) + i // 2]
                            cols = slice(hd * SSD_P, (hd + 1) * SSD_P)
                            pe.matmul(o[r:r + 64, 0:P], xt[:, 0, cols], seg[:, k % NB, 0, i, :], start=True, stop=True)
                            pe.matmul(o[r:r + 64, P:T], xt[:, 1, cols], seg[:, k % NB, 1, i, :], start=True, stop=False)
                            last = pe.matmul(o[r:r + 64, P:T], st[:, cols], cs1[:, k % NB, i, :], start=False, stop=True)
                        last.then_inc(y_ok, 1)

                    for k in range(quads + 2):
                        if k < quads:
                            sums(k)
                        if k >= 2:
                            outputs(k - 2)

                @b.vector
                def _(dve):
                    def minus(k):
                        dve.wait_ge(seg_ok, k + 1)
                        if k >= NB:
                            dve.wait_ge(y_ok, k - NB + 1)
                        for t in range(2):
                            if t == 1:
                                dve.wait_ge(carry, k + 1)
                            for i in range(Q):
                                hd = Q * k + i
                                dve.tensor_scalar(seg[:, k % NB, t, i, :], bank[2 * (k % 2) + t][:, i * P:(i + 1) * P],
                                                  neg_cs[:, t, hd:hd + 1], 0.0, ALU.add, ALU.min).then_inc(seg_min, 1)

                    def masked(k):
                        dve.wait_ge(l_ok, k + 1)
                        decayed_scores(dve, k, 0).then_inc(m_ok, 1)

                    def leave(k):
                        dve.wait_ge(y_ok, k + 1)
                        for i in range(2):
                            c = 2 * k + i
                            dve.scalar_tensor_tensor(out=y[:, c, :], in0=xs[:, c, :], scalar=vec("ssd_D", c),
                                                     in1=bank[4 + 2 * (k % 2) + i][:, 0:T], op0=ALU.mult,
                                                     op1=ALU.add).then_inc(y_out, 1)

                    for k in range(quads + 3):
                        if k < quads:
                            minus(k)
                        if 0 <= k - 1 < quads:
                            masked(k - 1)
                        if 0 <= k - 3 < quads:
                            leave(k - 3)

                @b.scalar
                def _(act):
                    for k in range(quads):
                        act.wait_ge(seg_ok, k + 1)
                        if k >= NB:
                            act.wait_ge(y_ok, k - NB + 1)
                        act.activation(cs1[:, k % NB, :, :], bank[2 * (k % 2) + 1][:, :].rearrange("p (i c) -> p i c", i=Q),
                                       ACT.Exp).then_inc(carry, 1)
                        act.wait_ge(seg_min, 8 * (k + 1))
                        act.activation(seg[:, k % NB, :, :, :], seg[:, k % NB, :, :, :], ACT.Exp).then_inc(l_ok, 1)

        def cross_attention(next_gain):
            with scope() as s:
                q = s("q", [P, DC, T])
                k = s("k", [P, DC, T])
                v = s("v", [P, 2, D])
                with scope() as s2:
                    mem = s2("memory", [P, DC, T])
                    mn = pair(s2, "memory", DC)
                    m_in, = semaphores("memory_in")

                    def sp_first(sp):
                        sp.dma_start(mem[:, :, :], w["memT"]).then_inc(m_in, 16)

                    norm = GroupNorm(s2, mem, mn, lambda c: vec("mem", c), DC, 1, 1e-6)
                    between = ({}, {}, {})
                    norm.into(between, [6] * DC, 6, per=4)

                    def leave(dve, steps, i, o, posted):
                        if i < DC:
                            return times(dve, q[:, i, :], o, factor=XA_HEAD_DIM ** -0.5)
                        if i < 2 * DC:
                            return dve.tensor_copy(k[:, i - DC, :], o)
                        return dve.tensor_copy(v[:, :, (i - 2 * DC) * 256:(i - 2 * DC + 1) * 256], o)

                    def act_first(act):
                        act.wait_ge(m_in, 16)
                        for c in range(DC):
                            norm.square(c)(act)

                    project([Part("xa_q", "f", xn.at, DC, DC), Part("xa_k", "f", mn.at, DC, DC, need=norm.need),
                             Part("xa_v", "t", mn.at, DC, 4, 256)], leave,
                            inverses=[Inverse(D)], sp_first=sp_first, act_first=act_first, between=between)
                oT = pair(s, "heads_out", DC)
                jobs = []
                for hd in range(XA_HEADS):
                    jobs.append(dict(
                        scores=[(q[:, 2 * hd + i, :], k[:, 2 * hd + i, :]) for i in range(2)], add=None,
                        first=True, last=True, evict=True,
                        outs=[(2 * hd + i, 0, P, lambda kb, c=2 * hd + i: v[:, kb, c * P:(c + 1) * P]) for i in range(2)]))
                attention(jobs, oT, causal=False)
                project([Part("xa_o", "f", oT.at, DC, DC)], lambda dve, steps, i, o, posted: dve.tensor_copy(y8[:, i, :], o),
                        tail=Tail(), tail_src=lambda i: y8[:, i, :])
                opening.append(AddNormed(opening[-1].tail, gain("xa_post"), 1.0, next_gain))

        def ffn_post(name, post, next_gain):
            ffn(name, y8)
            if next_gain:
                opening.append(AddNormed(opening[-1].tail, gain(post), 0.5, next_gain))
            else:
                add_and_store(y8, gain(post), 0.5)

        def ffn_final(name, next_gain):
            ffn(name)
            opening.append(FinalNorm(opening[-1].tail, gain("final"), 1.0, next_gain))

        stages = [
            ("start", start),
            ("ffn_a0", lambda: ffn("ffn_a0", None, gain("mix0"))),
            ("mla", lambda: mla(gain("ffn_b0"))),
            ("ffn_b0", lambda: ffn("ffn_b0", None, gain("ffn_a1"))),
            ("ffn_a1", lambda: ffn("ffn_a1", None, gain("mix1"))),
            ("nsa", lambda: nsa(gain("ffn_b1"))),
            ("final", lambda: ffn_final("ffn_b1", gain("ffn1_pre"))),
            ("ffn1", lambda: ffn_post("ffn1", "ffn1_post", gain("mix_pre"))),
            ("mix", lambda: two_branches(gain("xa_pre"))),
            ("xa", lambda: cross_attention(gain("ffn2_pre"))),
            ("ffn2", lambda: ffn_post("ffn2", "ffn2_post", None)),
        ]
        for name, stage in stages:
            stage()
            if stop == name and name != "ffn2":
                finish_opening()
                stored, = semaphores("stored")
                with block() as b:
                    @b.sync
                    def _(sp):
                        sp.dma_start(out, h[:, :, :]).then_inc(stored, 16)
                        sp.wait_ge(stored, 16)
                break
            if name != "ffn2":
                recycle()




def kernel(**inputs):
    import concourse.bacc as bacc
    from concourse.bass_utils import run_bass_kernel_spmd

    nc = bacc.Bacc("TRN2", target_bir_lowering=False, num_devices=1)
    arrays = lay_out({k: np.asarray(v) for k, v in inputs.items()})
    w = {n: nc.dram_tensor(f"in_{n}", a.shape, mybir.dt.from_np(a.dtype), kind="ExternalInput").ap() for n, a in arrays.items()}
    w["scratch"] = nc.dram_tensor("bias_rows", [P, HEADS, T], F32, kind="Internal").ap()
    out = nc.dram_tensor("out_dram", (P, DC, T), F32, kind="ExternalOutput").ap()
    emit(nc, w, out)
    r = run_bass_kernel_spmd(nc, [{f"in_{n}": a for n, a in arrays.items()}], core_ids=[0])
    got = r.results[0]["out_dram"]
    return np.ascontiguousarray(got.transpose(2, 1, 0)).reshape(1, T, D)
```
